# Optimizing a Trainium2 kernel written in Bass

```python
import math
import jax, jax.numpy as jnp
from jax import lax
import numpy as np

D_MODEL = 1024
BATCH = 1
SEQ = 256
DEPTH = 2

GROUP_WIDTH = D_MODEL // 4
HEAD_DIM = 64
N_FOX_HEADS = GROUP_WIDTH // HEAD_DIM
N_DIL_HEADS = GROUP_WIDTH // HEAD_DIM
N_DIFF_HEADS = GROUP_WIDTH // HEAD_DIM
DIFF_HALF = HEAD_DIM // 2
S5_CH = 16
S5_GROUPS = GROUP_WIDTH // S5_CH
S5_STATE = 64
BLOCK = 128
DIL_PAIRS = ((128, 1), (512, 4), (2048, 16))
REL_BUCKETS = 32
REL_MAX_EXACT = REL_BUCKETS // 2
REL_MAX_DIST = 2048
N_KEYS = 128
N_EXPERTS = N_KEYS * N_KEYS
PEER_HEADS = 8
PEER_TOPK = 16
PEER_QDIM = 256
PEER_CHUNK = 128
RMS_EPS = 1e-6
SPLIT_SIZES = [GROUP_WIDTH, GROUP_WIDTH, GROUP_WIDTH, N_FOX_HEADS,
               GROUP_WIDTH, GROUP_WIDTH, GROUP_WIDTH,
               GROUP_WIDTH, GROUP_WIDTH, GROUP_WIDTH,
               GROUP_WIDTH]
SPLIT_POINTS = [int(v) for v in np.cumsum(SPLIT_SIZES)[:-1]]
IN_WIDTH = int(sum(SPLIT_SIZES))

kernel_name = "hybrid_fox_dilated_diff_s5_peer"

def rms_norm(x, g):
    xf = x.astype(jnp.float32)
    y = xf * lax.rsqrt(jnp.mean(xf * xf, axis=-1, keepdims=True) + RMS_EPS)
    return (y * g.astype(jnp.float32)).astype(x.dtype)

def heads(t, n):
    b, s, _ = t.shape
    return t.reshape(b, s, n, -1).transpose(0, 2, 1, 3)

def to_blocks(t):
    b, h, s = t.shape[:3]
    t = t.reshape(b, h, s // BLOCK, BLOCK, *t.shape[3:])
    return jnp.moveaxis(t, 2, 0)

def unblock(o):
    nb, b, h, w, d = o.shape
    return o.transpose(1, 0, 3, 2, 4).reshape(b, nb * w, h * d)

def t5_bucket(dist):
    n = jnp.maximum(dist, 0)
    nf = jnp.maximum(n, REL_MAX_EXACT).astype(jnp.float32)
    large = REL_MAX_EXACT + (jnp.log(nf / REL_MAX_EXACT) / math.log(REL_MAX_DIST / REL_MAX_EXACT)
                             * (REL_BUCKETS - REL_MAX_EXACT)).astype(jnp.int32)
    large = jnp.minimum(large, REL_BUCKETS - 1)
    return jnp.where(n < REL_MAX_EXACT, n, large)

def forgetting_attention(q, k, v, f_logit):
    b, h, s, d = q.shape
    cum = jnp.cumsum(jax.nn.log_sigmoid(f_logit.astype(jnp.float32)), axis=1).transpose(0, 2, 1)
    scale = d ** -0.5
    kpos = jnp.arange(s)

    def block(args):
        qb, cq, q0 = args
        logits = jnp.einsum('bhqd,bhkd->bhqk', qb, k, preferred_element_type=jnp.float32) * scale
        logits = logits + (cq[..., :, None] - cum[..., None, :])
        qpos = q0 + jnp.arange(BLOCK)
        logits = jnp.where(kpos[None, :] <= qpos[:, None], logits, -jnp.inf)
        p = jax.nn.softmax(logits, axis=-1)
        return jnp.einsum('bhqk,bhkd->bhqd', p.astype(v.dtype), v)

    nb = s // BLOCK
    o = lax.map(block, (to_blocks(q), to_blocks(cum), jnp.arange(nb) * BLOCK))
    return unblock(o)

def dilated_branch(q, k, v, bias_tab, window, dil):
    b, h, s, d = q.shape
    ws = window // dil
    L = s // dil
    nb = -(-L // BLOCK)
    Lp = nb * BLOCK

    def strided(t):
        t = t.reshape(b, h, L, dil, d).transpose(0, 1, 3, 2, 4)
        t = jnp.pad(t, ((0, 0), (0, 0), (0, 0), (0, Lp - L), (0, 0)))
        return t.reshape(b, h, dil, nb, BLOCK, d)

    def with_prev(t):
        prev = jnp.pad(t, ((0, 0), (0, 0), (0, 0), (1, 0), (0, 0), (0, 0)))[:, :, :, :nb]
        return jnp.concatenate([prev, t], axis=-2)

    qs = strided(q)
    kk = with_prev(strided(k))
    vv = with_prev(strided(v))
    j = jnp.arange(BLOCK)[:, None]
    m = jnp.arange(2 * BLOCK)[None, :]
    sub_dist = BLOCK + j - m
    band = (sub_dist >= 0) & (sub_dist <= ws)
    blk = jnp.arange(nb)[:, None, None]
    valid = band[None] & (blk * BLOCK + m[None] - BLOCK >= 0)
    bias = bias_tab[t5_bucket(dil * jnp.clip(sub_dist, 0, ws))].transpose(2, 0, 1)
    logits = jnp.einsum('bhrnqd,bhrnkd->bhrnqk', qs, kk, preferred_element_type=jnp.float32) * (d ** -0.5)
    logits = logits + bias[:, None, None].astype(jnp.float32)
    logits = jnp.where(valid, logits, -jnp.inf)
    mx = jnp.max(logits, axis=-1, keepdims=True)
    e = jnp.exp(logits - mx)
    den = jnp.sum(e, axis=-1, keepdims=True)
    o = jnp.einsum('bhrnqk,bhrnkd->bhrnqd', (e / den).astype(v.dtype), vv)
    lse = (mx + jnp.log(den))[..., 0]

    def unstrided(t):
        rest = t.shape[5:]
        t = t.reshape(b, h, dil, Lp, *rest)[:, :, :, :L]
        t = jnp.moveaxis(t, 2, 3)
        return t.reshape(b, h, s, *rest)

    return unstrided(o), unstrided(lse)

def dilated_attention(q, k, v, bias_tab):
    b, h, s, d = q.shape
    branches = [dilated_branch(q, k, v, bias_tab, w, r) for (w, r) in DIL_PAIRS]
    outs = jnp.stack([o for o, _ in branches])
    wts = jax.nn.softmax(jnp.stack([l for _, l in branches]), axis=0)
    o = jnp.einsum('nbhs,nbhsd->bhsd', wts.astype(v.dtype), outs)
    return o.transpose(0, 2, 1, 3).reshape(b, s, h * d)

def diff_attention(q, k, v, bias_tab, lam, out_gain, lam_init):
    b, h, s = q.shape[:3]
    scale = DIFF_HALF ** -0.5
    kpos = jnp.arange(s)

    def block(args):
        qb, q0 = args
        qpos = q0 + jnp.arange(BLOCK)
        rel = qpos[:, None] - kpos[None, :]
        bias = bias_tab[t5_bucket(rel)].transpose(2, 0, 1).astype(jnp.float32)
        logits = jnp.einsum('bhqcd,bhkcd->cbhqk', qb, k, preferred_element_type=jnp.float32) * scale + bias
        logits = jnp.where(rel >= 0, logits, -jnp.inf)
        p = jax.nn.softmax(logits, axis=-1)
        attn = p[0] - lam * p[1]
        o = jnp.einsum('bhqk,bhkd->bhqd', attn.astype(v.dtype), v)
        return rms_norm(o, out_gain) * (1.0 - lam_init)

    nb = s // BLOCK
    o = lax.map(block, (to_blocks(q), jnp.arange(nb) * BLOCK))
    return unblock(o)

def s5_mixer(u, a_re, a_im, log_dt, b_re, b_im, c_re, c_im, d_skip, glu_w, glu_b):
    bsz, s, _ = u.shape
    uf = u.astype(jnp.float32).reshape(bsz, s, S5_GROUPS, S5_CH)
    dt = jnp.exp(log_dt.astype(jnp.float32))[:, None]
    ar, ai = a_re.astype(jnp.float32), a_im.astype(jnp.float32)
    mag = jnp.exp(dt * ar)
    abar_re, abar_im = mag * jnp.cos(dt * ai), mag * jnp.sin(dt * ai)
    den = ar * ar + ai * ai
    nr, ni = abar_re - 1.0, abar_im
    coef_re = (nr * ar + ni * ai) / den
    coef_im = (ni * ar - nr * ai) / den
    br, bi = b_re.astype(jnp.float32), b_im.astype(jnp.float32)
    bbar_re = coef_re[..., None] * br - coef_im[..., None] * bi
    bbar_im = coef_re[..., None] * bi + coef_im[..., None] * br
    bu_re = jnp.einsum('gnc,bsgc->bsgn', bbar_re, uf)
    bu_im = jnp.einsum('gnc,bsgc->bsgn', bbar_im, uf)
    a_full_re = jnp.broadcast_to(abar_re, bu_re.shape)
    a_full_im = jnp.broadcast_to(abar_im, bu_re.shape)

    def combine(e1, e2):
        a1r, a1i, b1r, b1i = e1
        a2r, a2i, b2r, b2i = e2
        return (a2r * a1r - a2i * a1i, a2r * a1i + a2i * a1r,
                a2r * b1r - a2i * b1i + b2r, a2r * b1i + a2i * b1r + b2i)

    _, _, xr, xi = lax.associative_scan(combine, (a_full_re, a_full_im, bu_re, bu_im), axis=1)
    y = (jnp.einsum('gcn,bsgn->bsgc', c_re.astype(jnp.float32), xr)
         - jnp.einsum('gcn,bsgn->bsgc', c_im.astype(jnp.float32), xi)
         + d_skip.astype(jnp.float32) * uf)
    g = jax.nn.gelu(y.reshape(bsz, s, -1))
    out = g * jax.nn.sigmoid(g @ glu_w.astype(jnp.float32) + glu_b.astype(jnp.float32))
    return out.astype(u.dtype)

def peer(h, wq, keys, u_tab, v_tab):
    b, s, dm = h.shape
    chunks = h.reshape(-1, PEER_CHUNK, dm)

    def chunk(xc):
        c = xc.shape[0]
        q = (xc @ wq).reshape(c, PEER_HEADS, 2, PEER_QDIM // 2)
        sc = jnp.einsum('thpd,hpkd->thpk', q, keys, preferred_element_type=jnp.float32)
        top_v, top_i = lax.top_k(sc, PEER_TOPK)
        cand = (top_v[:, :, 0, :, None] + top_v[:, :, 1, None, :]).reshape(c, PEER_HEADS, -1)
        cand_id = (top_i[:, :, 0, :, None] * N_KEYS + top_i[:, :, 1, None, :]).reshape(c, PEER_HEADS, -1)
        best_v, best_pos = lax.top_k(cand, PEER_TOPK)
        ids = jnp.take_along_axis(cand_id, best_pos, axis=-1)
        gate = jax.nn.softmax(best_v, axis=-1)
        ug = u_tab[ids]
        act = jax.nn.gelu(jnp.einsum('td,thkd->thk', xc, ug, preferred_element_type=jnp.float32)) * gate
        vg = v_tab[ids]
        return jnp.einsum('thk,thkd->td', act.astype(vg.dtype), vg)

    return lax.map(chunk, chunks).reshape(b, s, dm)

def setup_inputs(seed: int = 0) -> dict:
    key = jax.random.key(seed)
    ks = jax.random.split(key, 32)
    f32 = jnp.float32
    L, D, G, N, C = DEPTH, D_MODEL, S5_GROUPS, S5_STATE, S5_CH

    def nrm(k, shape, scale):
        return jax.random.normal(k, shape, f32) * scale

    def gain(k, shape):
        return 1.0 + 0.02 * jax.random.normal(k, shape, f32)

    return {
        "x": jax.random.normal(ks[0], (BATCH, SEQ, D), f32),
        "w_in": nrm(ks[1], (L, D, IN_WIDTH), D ** -0.5),
        "b_forget": jax.random.uniform(ks[2], (L, N_FOX_HEADS), f32, 1.0, 6.0),
        "w_out": nrm(ks[3], (L, D, D), D ** -0.5),
        "norm_mix": gain(ks[4], (L, D)),
        "norm_ffn": gain(ks[5], (L, D)),
        "fox_q_norm": gain(ks[6], (L, HEAD_DIM)),
        "fox_k_norm": gain(ks[7], (L, HEAD_DIM)),
        "dil_q_norm": gain(ks[8], (L, HEAD_DIM)),
        "dil_k_norm": gain(ks[9], (L, HEAD_DIM)),
        "diff_q_norm": gain(ks[10], (L, DIFF_HALF)),
        "diff_k_norm": gain(ks[11], (L, DIFF_HALF)),
        "diff_lambda": nrm(ks[12], (L, 4, DIFF_HALF), 0.1),
        "diff_out_norm": gain(ks[13], (L, HEAD_DIM)),
        "rel_bias": nrm(ks[14], (REL_BUCKETS, N_DIL_HEADS + N_DIFF_HEADS), 0.2),
        "s5_a_re": -0.5 + 0.01 * jax.random.normal(ks[15], (L, G, N), f32),
        "s5_a_im": math.pi * jnp.arange(N, dtype=f32)[None, None, :] + 0.01 * jax.random.normal(ks[16], (L, G, N), f32),
        "s5_log_dt": jax.random.uniform(ks[17], (L, G), f32, math.log(1e-3), math.log(1e-1)),
        "s5_b_re": nrm(ks[18], (L, G, N, C), (2 * C) ** -0.5),
        "s5_b_im": nrm(ks[19], (L, G, N, C), (2 * C) ** -0.5),
        "s5_c_re": nrm(ks[20], (L, G, C, N), N ** -0.5),
        "s5_c_im": nrm(ks[21], (L, G, C, N), N ** -0.5),
        "s5_d": nrm(ks[22], (L, G, C), 1.0),
        "s5_glu_w": nrm(ks[23], (L, GROUP_WIDTH, GROUP_WIDTH), GROUP_WIDTH ** -0.5),
        "s5_glu_b": nrm(ks[24], (L, GROUP_WIDTH), 0.01),
        "peer_wq": nrm(ks[25], (L, D, PEER_HEADS * PEER_QDIM), D ** -0.5),
        "peer_keys": nrm(ks[26], (L, PEER_HEADS, 2, N_KEYS, PEER_QDIM // 2), (PEER_QDIM // 2) ** -0.5),
        "peer_u": nrm(ks[27], (L, N_EXPERTS, D), D ** -0.5),
        "peer_v": nrm(ks[28], (L, N_EXPERTS, D), PEER_TOPK ** -0.5),
    }

def reference(x, w_in, b_forget, w_out, norm_mix, norm_ffn, fox_q_norm, fox_k_norm,
              dil_q_norm, dil_k_norm, diff_q_norm, diff_k_norm, diff_lambda, diff_out_norm,
              rel_bias, s5_a_re, s5_a_im, s5_log_dt, s5_b_re, s5_b_im, s5_c_re, s5_c_im,
              s5_d, s5_glu_w, s5_glu_b, peer_wq, peer_keys, peer_u, peer_v):
    b, s, _ = x.shape
    for layer in range(DEPTH):
        h = rms_norm(x, norm_mix[layer])
        z = h @ w_in[layer]
        fq, fk, fv, ff, dq, dk, dv, cq, ck, cv, su = jnp.split(z, SPLIT_POINTS, axis=-1)
        fox_o = forgetting_attention(rms_norm(heads(fq, N_FOX_HEADS), fox_q_norm[layer]),
                                     rms_norm(heads(fk, N_FOX_HEADS), fox_k_norm[layer]),
                                     heads(fv, N_FOX_HEADS), ff + b_forget[layer])
        dil_o = dilated_attention(rms_norm(heads(dq, N_DIL_HEADS), dil_q_norm[layer]),
                                  rms_norm(heads(dk, N_DIL_HEADS), dil_k_norm[layer]),
                                  heads(dv, N_DIL_HEADS), rel_bias[:, :N_DIL_HEADS])
        cqh = rms_norm(heads(cq, N_DIFF_HEADS).reshape(b, N_DIFF_HEADS, s, 2, DIFF_HALF), diff_q_norm[layer])
        ckh = rms_norm(heads(ck, N_DIFF_HEADS).reshape(b, N_DIFF_HEADS, s, 2, DIFF_HALF), diff_k_norm[layer])
        lam_init = 0.8 - 0.6 * math.exp(-0.3 * layer)
        lam_p = diff_lambda[layer].astype(jnp.float32)
        lam = jnp.exp(jnp.sum(lam_p[0] * lam_p[1])) - jnp.exp(jnp.sum(lam_p[2] * lam_p[3])) + lam_init
        diff_o = diff_attention(cqh, ckh, heads(cv, N_DIFF_HEADS), rel_bias[:, N_DIL_HEADS:],
                                lam, diff_out_norm[layer], lam_init)
        s5_o = s5_mixer(su, s5_a_re[layer], s5_a_im[layer], s5_log_dt[layer], s5_b_re[layer],
                        s5_b_im[layer], s5_c_re[layer], s5_c_im[layer], s5_d[layer],
                        s5_glu_w[layer], s5_glu_b[layer])
        mixed = jnp.concatenate([fox_o, dil_o, diff_o, s5_o], axis=-1)
        x = x + mixed @ w_out[layer]
        x = x + peer(rms_norm(x, norm_ffn[layer]), peer_wq[layer], peer_keys[layer],
                     peer_u[layer], peer_v[layer])
    return x


_drawn_inputs = setup_inputs


def setup_inputs(seed=0):
    import zlib

    import numpy as np

    out = dict(_drawn_inputs(seed))
    spreads = {}
    factors = {'fox_q_norm': 5.47,
     'fox_k_norm': 5.853,
     'dil_q_norm': 6.306,
     'dil_k_norm': 5.5,
     'diff_q_norm': 3.096,
     'diff_k_norm': 3.268,
     'diff_out_norm': 2.954,
     's5_a_re': 200.0,
     's5_glu_b': 8.0,
     's5_a_im': 21.656,
     's5_log_dt': 22.579,
     's5_b_re': 22.013,
     's5_b_im': 22.28,
     's5_c_re': 26.828,
     's5_c_im': 25.823}
    for name, (base, spread) in spreads.items():
        noise = np.random.default_rng([zlib.crc32(name.encode()), seed]).standard_normal(out[name].shape)
        drawn = base * np.exp(spread * noise) if base else spread * noise
        out[name] = __import__('jax').numpy.asarray(drawn.astype(out[name].dtype))
    for name, factor in factors.items():
        out[name] = (out[name] * factor).astype(out[name].dtype)
    return out
```

```python
import math
from contextlib import ExitStack

import numpy as np

import concourse.bass as bass
from concourse import mybir

ALU = mybir.AluOpType
ACT = mybir.ActivationFunctionType
AX = mybir.AxisListType.X
F32 = mybir.dt.float32
U32 = mybir.dt.uint32

P = 128
D = 1024
SEQ = 256
NB = SEQ // P
DEPTH = 2
KC = D // P
GW = D // 4
HD = 64
NH = GW // HD
DH = HD // 2
S5_G, S5_C, S5_N = 16, 16, 64
NJ = S5_G * S5_N // P
BUCKETS, MAX_EXACT, MAX_DIST = 32, 16, 2048
NK = 128
NE = NK * NK
PH, TOPK = 8, 16
HP = 2 * PH
SLOTS = PH * TOPK
EPS = 1e-6
NEG = -1.0e30
RING_G = 4
RING = 2 * RING_G
ITERS = SLOTS // RING

FQ, FK, FV, FF = 0, 256, 512, 768
DQ, DK, DV = 772, 1028, 1284
CQ, CK, CV = 1540, 1796, 2052
SU = 2308
IN_W = 2564
Z_CUTS = [0, 512, 772, 1284, 1796, 2308, 2564]

R_FQ, R_FK, R_DQ, R_DK = 0, 64, 128, 192
R_CQ, R_CK = 256, 288
R_CO = 320
R_BF = 384
R_LAM = 388
R_LC = 516
R_SD = 520
R_GB = 776
R_W = 1032

C_ID, C_TRI, C_ONE, C_MASK = 0, 128, 256, 384
C_TAU = 512
C_HM2, C_HM4 = 640, 642
C_IOTA = 646
C_W = 662

S_AR, S_AI, S_DT = 0, 8, 16
S_BR, S_BI = 24, 24 + NJ * S5_C
S_CR = S_BI + NJ * S5_C
S_CI = S_CR + GW
S_W = S_CI + GW

TWO_PI = 2.0 * math.pi
PI_A = 6.28125
PI_B = 0.0019340515136718750
PI_C = TWO_PI - PI_A - PI_B
ROUND = 12582912.0


def bc(ap, axis, n):
    dims = [list(d) for d in ap.ap]
    dims.insert(axis, [0, n])
    return bass.AP(ap.tensor, ap.offset, dims)


def rep(ap, n):
    return bass.AP(ap.tensor, ap.offset, [list(ap.ap[0]), [0, n]])


class Order:

    def __init__(self, eng, sem):
        self.eng, self.sem, self.n = eng, sem, 0

    def __call__(self, ins):
        ins.then_inc(self.sem, 1)
        self.n += 1
        self.eng.wait_ge(self.sem, self.n)


def trunk(nc, x_in, w_in, w_out, row_in, gain_mix, gain_ffn, s5_in, glu_w, peer_wq, keys_t, table_u, table_v,
          rel_bias, const_in, bucket_in, out):
    ctx = ExitStack()
    with ctx:
        def sb(name, shape, dt=F32):
            return ctx.enter_context(nc.sbuf_tensor(name, shape, dt))

        def sem(name):
            s = ctx.enter_context(nc.semaphore(name))
            return s

        W = sb("W", [P, KC * IN_W])
        x = sb("x", [P, NB, D])
        h = sb("h", [P, NB, D])
        hT = sb("hT", [P, KC, P])
        z = sb("z", [P, NB, IN_W])
        bias = sb("bias", [P, 2 * NH, SEQ])
        cst = sb("cst", [P, C_W])
        row = sb("row", [P, R_W])
        gain = sb("gain", [P, D])
        s5p = sb("s5p", [P, S_W])
        glu = sb("glu", [P, 2, GW])
        cosT = sb("cosT", [P, NJ, P])
        sinT = sb("sinT", [P, NJ, P])
        bT = sb("bT", [P, 4, 4, P])
        kT = sb("kT", [P, 3, 2, SEQ])
        T = sb("T", [P, 8192])
        small = sb("small", [P, 768])
        ids = sb("ids", [P, NB, SLOTS], U32)
        gates = sb("gates", [P, NB, SLOTS])
        ring_ids = sb("ring_ids", [P, RING], U32)
        dots = sb("dots", [P, RING])
        acts = sb("acts", [P, RING])

        win = W[:, :].rearrange("p (k n) -> p k n", k=KC)
        wq_v = [W[:, a * 8192:(a + 1) * 8192].rearrange("p (k n) -> p k n", k=KC) for a in range(2)]
        wout_v = wq_v[1]
        ring_u = W[:, 0:RING * D].rearrange("p (s n) -> p s n", s=RING)
        ring_v = W[:, RING * D:2 * RING * D].rearrange("p (s n) -> p s n", s=RING)
        ident, tri = cst[:, C_ID:C_ID + P], cst[:, C_TRI:C_TRI + P]
        triones = cst[:, C_TRI:C_TRI + 2 * P]
        ones, causal = cst[:, C_ONE:C_ONE + P], cst[:, C_MASK:C_MASK + P]
        mixed = h
        pbuf = T[:, 0:1024].rearrange("p (n k) -> p n k", k=SEQ)
        pT = T[:, 1024:2048].rearrange("p (n k) -> p n k", k=P)
        qm = T[:, 2048:3072]
        qm2 = T[:, 2048:4096]
        s5a, s5b, s5c, s5d = [T[:, 4096 + 1024 * i:5120 + 1024 * i].rearrange("p (j t) -> p j t", j=NJ)
                              for i in range(4)]
        sq = T[:, 0:1024]
        kts = T[:, 0:2048].rearrange("p (n k) -> p n k", k=NK)
        qts = T[:, 2048:4096].rearrange("p (n k) -> p n k", k=P)
        cand, cand2, sc2 = T[:, 4096:4352], T[:, 4352:4608], T[:, 4608:4736]
        v16 = T[:, 4736:4992].rearrange("p (n k) -> p n k", k=TOPK)
        i16f = T[:, 4992:5248].rearrange("p (n k) -> p n k", k=TOPK)
        best = T[:, 5248:5376].rearrange("p (n k) -> p n k", k=TOPK)
        hit = T[:, 5376:7424].rearrange("p (n k a) -> p n k a", k=TOPK, a=TOPK)
        posf = T[:, 7424:7552]
        idf = [T[:, 7552:7680], T[:, 7680:7808]]
        i16 = sb("i16", [P, HP, TOPK], U32)
        pos = sb("pos", [P, PH, TOPK], U32)
        posd = sb("posd", [P, SLOTS], U32)
        junk = T[:, 4096:5120]
        diag = T[:, 5120:6144].rearrange("p (s k) -> p s k", s=RING)
        zero = sb("zero", [P, P])

        ps = ctx.enter_context(nc.psum_tensor("ps", [P, 8, 512], F32))
        toep = nc.dram_tensor("toep", [2 * NH, P, 512], F32, kind="Internal").ap()

        once_in, bias_in, toep_out = sem("once_in"), sem("bias_in"), sem("toep_out")
        toep_ready, toep_ps, toep_copied, zero_set = sem("toep_ready"), sem("toep_ps"), sem("toep_copied"), sem("zero_set")
        out_stored = sem("out_stored")
        u_in = [sem(f"u_in{i}") for i in range(RING)]
        v_in = [sem(f"v_in{i}") for i in range(RING)]
        ring_staged, dots_done, gelu_done, diag_ready, v_used = (
            sem("ring_staged"), sem("dots_done"), sem("gelu_done"), sem("diag_ready"), sem("v_used"))
        layer_sems = []

        def lsem(name):
            s = sem(name)
            layer_sems.append(s)
            return s

        dve_step, act_step = lsem("dve_step"), lsem("act_step")
        win_in = [lsem(f"win_in{k}") for k in range(KC)]
        row_load, gain_load, s5_load, glu_load = lsem("row_load"), lsem("gain_load"), lsem("s5_load"), lsem("glu_load")
        ffn_load, wout_load, wqa_load, wqb_load, keys_load = (
            lsem("ffn_load"), lsem("wout_load"), lsem("wqa_load"), lsem("wqb_load"), lsem("keys_load"))
        sumsq, mean_inv, rstd = lsem("sumsq"), lsem("mean_inv"), lsem("rstd")
        h_ready, hT_ps, hT_ready = lsem("h_ready"), lsem("hT_ps"), lsem("hT_ready")
        z_ps, z_dve, z_act = lsem("z_ps"), lsem("z_dve"), lsem("z_act")
        s5_exp, s5_ang, s5_sin, s5_tab = lsem("s5_exp"), lsem("s5_ang"), lsem("s5_sin"), lsem("s5_tab")
        s5_bx, s5_bt_ps, s5_bt = lsem("s5_bx"), lsem("s5_bt_ps"), lsem("s5_bt")
        lam_sum, lam_exp = lsem("lam_sum"), lsem("lam_exp")
        qk_sq, qk_inv, qk_rstd, qk_ready = lsem("qk_sq"), lsem("qk_inv"), lsem("qk_rstd"), lsem("qk_ready")
        f_bias, f_ln, f_ready = lsem("f_bias"), lsem("f_ln"), lsem("f_ready")
        qkT_ps, kT_ready, qm_ready = lsem("qkT_ps"), lsem("kT_ready"), lsem("qm_ready")
        logit_ps, logit_max, p_exp, p_ready = lsem("logit_ps"), lsem("logit_max"), lsem("p_exp"), lsem("p_ready")
        pT_ps, pT_ready, o_ps, o_used = lsem("pT_ps"), lsem("pT_ready"), lsem("o_ps"), lsem("o_used")
        co_sq, co_inv, co_rstd = lsem("co_sq"), lsem("co_inv"), lsem("co_rstd")
        uT_ps, uT_ready, bu_ps, bu_used = lsem("uT_ps"), lsem("uT_ready"), lsem("bu_ps"), lsem("bu_used")
        s5_state, y_ps, y_ready, g_ready = lsem("s5_state"), lsem("y_ps"), lsem("y_ready"), lsem("g_ready")
        gT_ps, gT_ready, glu_ps, glu_sum, glu_sig = (
            lsem("gT_ps"), lsem("gT_ready"), lsem("glu_ps"), lsem("glu_sum"), lsem("glu_sig"))
        mixed_ready, mT_ps, mT_ready, wo_ps, x_ready = (
            lsem("mixed_ready"), lsem("mT_ps"), lsem("mT_ready"), lsem("wo_ps"), lsem("x_ready"))
        qT_ps, qT_ready, sc_ps, sc_used = lsem("qT_ps"), lsem("qT_ready"), lsem("sc_ps"), lsem("sc_used")
        best_sub, gate_exp, ids_ready = lsem("best_sub"), lsem("gate_exp"), lsem("ids_ready")
        acc_ps, x_done = lsem("acc_ps"), lsem("x_done")

        line = T[0:BUCKETS, 0:512]
        lines = T[0:1, 512:1536]
        tab = T[0:BUCKETS, 1536:1544]
        tabx = T[0:BUCKETS, 2048:2048 + 8 * P].rearrange("p (n k) -> p n k", n=2 * NH)
        line_sb = T[:, 4096:8192].rearrange("p (n k) -> p n k", n=2 * NH)
        with nc.Block() as block:
            @block.sync
            def _(sp):
                sp.dma_start(cst[:, :], const_in).then_inc(once_in, 16)
                sp.dma_start(line, bucket_in[0:BUCKETS, :]).then_inc(once_in, 16)
                sp.dma_start(lines, bucket_in[BUCKETS:BUCKETS + 2, :].rearrange("(a b) n -> a (b n)", a=1)).then_inc(once_in, 16)
                sp.dma_start(tab, rel_bias).then_inc(once_in, 16)
                sp.dma_start(x[:, :, :], x_in.rearrange("(b p) d -> p b d", p=P)).then_inc(once_in, 16)
                sp.wait_ge(toep_copied, 2 * NH)
                sp.dma_start(toep.rearrange("n p k -> p n k"), line_sb).then_inc(toep_out, 16)
                sp.wait_ge(toep_out, 16)
                for n in range(2 * NH):
                    skew = bass.AP(toep.tensor, n * P * 512 + P - 1, [[511, P], [1, SEQ]])
                    sp.dma_start(bias[:, n, :], skew).then_inc(bias_in, 16)
                sp.wait_ge(bias_in, 16 * 2 * NH)

            @block.vector
            def _(v):
                v.memset(zero[:, :], 0.0).then_inc(zero_set, 1)
                v.wait_ge(once_in, 80)
                v.tensor_copy(tabx, bc(tab, 2, P)).then_inc(toep_ready, 1)
                for n in range(2 * NH):
                    v.wait_ge(toep_ps, n + 1)
                    v.tensor_copy(line_sb[:, n, :], ps[:, n, :]).then_inc(toep_copied, 1)
                v.sem_inc(dots_done, RING)

            @block.tensor
            def _(pe):
                pe.wait_ge(once_in, 80)
                pe.wait_ge(toep_ready, 1)
                for n in range(2 * NH):
                    mask = lines[:, 0:512] if n < NH else lines[:, 512:1024]
                    pe.matmul(ps[:, n, :], tabx[:, n, :], line, start=True, stop=False)
                    pe.matmul(ps[:, n, :], ones[0:1, :], mask, start=False, stop=True).then_inc(toep_ps, 1)
                pe.sem_inc(v_used, RING)

        with nc.Fori(0, DEPTH) as layer:
          with nc.Block() as block:
            @block.sync
            def _(sp):
                sp.dma_start(gain[:, :], gain_mix[layer].partition_broadcast(P)).then_inc(gain_load, 16)
                for k in range(KC):
                    sp.dma_start(win[:, k, :], w_in[layer, k * P:(k + 1) * P, :]).then_inc(win_in[k], 16)
                sp.dma_start(row[:, :], row_in[layer].partition_broadcast(P)).then_inc(row_load, 16)
                sp.dma_start(s5p[:, :], s5_in[layer]).then_inc(s5_load, 16)
                sp.dma_start(glu[:, :, :], glu_w[layer].rearrange("(k p) n -> p k n", p=P)).then_inc(glu_load, 16)
                sp.wait_ge(h_ready, 2)
                sp.dma_start(gain[:, :], gain_ffn[layer].partition_broadcast(P)).then_inc(ffn_load, 16)
                sp.wait_ge(z_ps, 12)
                sp.dma_start(wout_v, w_out[layer].rearrange("(k p) n -> p k n", p=P)).then_inc(wout_load, 16)
                sp.dma_start(wq_v[0], peer_wq[layer, :, 0:D].rearrange("(k p) n -> p k n", p=P)).then_inc(wqa_load, 16)
                sp.wait_ge(wo_ps, 2)
                sp.dma_start(wq_v[1], peer_wq[layer, :, D:2 * D].rearrange("(k p) n -> p k n", p=P)).then_inc(wqb_load, 16)
                sp.wait_ge(mixed_ready, 2)
                sp.dma_start(kts, keys_t[layer]).then_inc(keys_load, 16)

            @block.scalar
            def _(a):
                step = Order(a, act_step)

                def rms_stats(n):
                    b = n % 2
                    if n >= 2:
                        a.wait_ge(x_ready, b + 1)
                    a.activation(T[:, 6144:7168] if n < 2 else T[:, 7168:8192], x[:, b, :], ACT.Square,
                                 accum_out=small[:, n:n + 1]).then_inc(sumsq, 1)
                    a.wait_ge(mean_inv, n + 1)
                    a.activation(small[:, 8 + n:9 + n], small[:, 4 + n:5 + n], ACT.Sqrt).then_inc(rstd, 1)

                def evac_hT(n, ps_count):
                    a.wait_ge(hT_ps, ps_count)
                    a.activation(hT[:, 4:8, :], ps[:, 7, :].rearrange("p (k t) -> p k t", t=P), ACT.Copy).then_inc(hT_ready, 1)
                    a.wait_ge(hT_ready, 2 * n + 1)

                for b in range(NB):
                    rms_stats(b)
                a.wait_ge(s5_load, 16)
                a.activation(small[:, 16:24], s5p[:, S_DT:S_DT + NJ], ACT.Exp).then_inc(s5_exp, 1)
                a.wait_ge(s5_ang, 1)
                a.activation(small[:, 32:40], small[:, 24:32], ACT.Exp).then_inc(s5_exp, 1)
                for b in range(NB):
                    for i in (1, 3, 5):
                        a.wait_ge(z_ps, 6 * b + i + 1)
                        a.activation(z[:, b, Z_CUTS[i]:Z_CUTS[i + 1]], ps[:, i, 0:Z_CUTS[i + 1] - Z_CUTS[i]],
                                     ACT.Copy).then_inc(z_act, 1)
                a.wait_ge(s5_ang, 2)
                a.activation(sinT[:, :, :], s5a, ACT.Sin).then_inc(s5_sin, 1)
                a.activation(cosT[:, :, :], s5a, ACT.Sin, scale=0.5).then_inc(s5_sin, 1)
                a.wait_ge(lam_sum, 1)
                a.activation(small[:, 42:44], small[:, 40:42], ACT.Exp).then_inc(lam_exp, 1)
                a.wait_ge(f_bias, 1)
                step(a.activation(small[:, 56:64], small[:, 48:56], ACT.Abs))
                step(a.activation(small[:, 56:64], small[:, 56:64], ACT.Exp, scale=-1.0))
                a.activation(small[:, 64:72], small[:, 56:64], ACT.Ln, bias=1.0).then_inc(f_ln, 1)
                for b in range(NB):
                    a.wait_ge(qk_inv, b + 1)
                    a.activation(small[:, 128 + 32 * b:160 + 32 * b], small[:, 96:128], ACT.Sqrt).then_inc(qk_rstd, 1)
                a.wait_ge(s5_bt_ps, 1)
                for i in range(4):
                    a.activation(bT[:, :, i, :], ps[:, 4, :].rearrange("p (r t) -> p r t", t=P), ACT.Copy,
                                 scale=cst[:, C_HM4 + i:C_HM4 + i + 1]).then_inc(s5_bt, 1)

                ex = pt = 0
                for b in range(NB):
                    nk = P * (b + 1)
                    a.wait_ge(uT_ps, b + 1)
                    a.activation(T[:, 7936:8192].rearrange("p (r t) -> p r t", t=P),
                                 ps[:, 5, 0:256].rearrange("p (r t) -> p r t", t=P), ACT.Copy).then_inc(uT_ready, 1)
                    for g in range(4):
                        a.wait_ge(logit_max, 4 * b + g + 1)
                        for i in range(4):
                            c = 72 + i
                            a.activation(pbuf[:, i, 0:nk], ps[:, 0:2, :].rearrange("p c n -> p (c n)")[:, i * nk:(i + 1) * nk],
                                         ACT.Exp, bias=small[:, c:c + 1],
                                         accum_out=small[:, 80 + i:81 + i]).then_inc(p_exp, 1)
                        nt = (4 if g < 2 else 2) * (b + 1)
                        for c in range((nt + 3) // 4):
                            m = min(4, nt - 4 * c)
                            pt += 1
                            a.wait_ge(pT_ps, pt)
                            a.activation(pT[:, 4 * c:4 * c + m, :], ps[:, 2 + c, 0:m * P].rearrange("p (n k) -> p n k", k=P),
                                         ACT.Copy).then_inc(pT_ready, 1)
                    a.wait_ge(co_inv, b + 1)
                    a.activation(small[:, 196:200], small[:, 192:196], ACT.Sqrt).then_inc(co_rstd, 1)
                    a.wait_ge(y_ready, b + 1)
                    a.activation(T[:, 4096:4352], T[:, 4096:4352], ACT.Gelu_apprx_tanh).then_inc(g_ready, 1)
                    a.wait_ge(glu_sum, b + 1)
                    a.activation(T[:, 4352:4608], T[:, 4352:4608], ACT.Sigmoid).then_inc(glu_sig, 1)

                for b in range(NB):
                    a.wait_ge(mT_ps, b + 1)
                    if b:
                        a.wait_ge(wo_ps, 1)
                    a.activation(hT[:, 4:8, :], ps[:, 3, :].rearrange("p (k t) -> p k t", t=P), ACT.Copy).then_inc(mT_ready, 1)
                for b in range(NB):
                    rms_stats(NB + b)
                for b in range(NB):
                    for i in (1, 3):
                        a.wait_ge(qT_ps, 4 * b + i + 1)
                        if b:
                            a.wait_ge(sc_ps, 4 * b)
                        a.activation(qts[:, 4 * i:4 * i + 4, :], ps[:, 4 + i, :].rearrange("p (n t) -> p n t", t=P),
                                     ACT.Copy).then_inc(qT_ready, 1)
                    a.wait_ge(best_sub, b + 1)
                    a.activation(gates[:, b, :], gates[:, b, :], ACT.Exp).then_inc(gate_exp, 1)
                for b in range(NB):
                    with a.Fori(0, ITERS) as it:
                        for g in range(2):
                            a.wait_ge(dots_done, ((layer * NB + b) * ITERS + it) * RING + RING + (g + 1) * RING_G)
                            a.wait_ge(keys_load, 16)
                            a.activation(acts[:, g * RING_G:(g + 1) * RING_G], dots[:, g * RING_G:(g + 1) * RING_G],
                                         ACT.Gelu_apprx_tanh).then_inc(gelu_done, 1)

            @block.vector
            def _(v):
                step = Order(v, dve_step)

                def rms_apply(n):
                    b = n % 2
                    v.wait_ge(sumsq, n + 1)
                    step(v.tensor_scalar(small[:, 4 + n:5 + n], small[:, n:n + 1], 1.0 / D, EPS, ALU.mult, ALU.add))
                    v.reciprocal(small[:, 4 + n:5 + n], small[:, 4 + n:5 + n]).then_inc(mean_inv, 1)
                    v.wait_ge(rstd, n + 1)
                    if n == 0:
                        v.wait_ge(gain_load, 16)
                    if n == 2:
                        v.wait_ge(ffn_load, 16)
                        v.wait_ge(mT_ps, 2)
                    v.scalar_tensor_tensor(out=h[:, b, :], in0=x[:, b, :], scalar=small[:, 8 + n:9 + n], in1=gain[:, :],
                                           op0=ALU.mult, op1=ALU.mult).then_inc(h_ready, 1)

                for b in range(NB):
                    rms_apply(b)
                for b in range(NB):
                    v.wait_ge(hT_ps, b + 1)
                    if b:
                        v.wait_ge(z_ps, 6)
                    v.tensor_copy(hT[:, 0:4, :], ps[:, 6, :].rearrange("p (k t) -> p k t", t=P)).then_inc(hT_ready, 1)
                    v.wait_ge(hT_ready, 2 * b + 1)
                    v.tensor_copy(hT[:, 4:8, :], ps[:, 7, :].rearrange("p (k t) -> p k t", t=P)).then_inc(hT_ready, 1)
                    if b == 0:
                        ar, ai = s5p[:, S_AR:S_AR + NJ], s5p[:, S_AI:S_AI + NJ]
                        v.wait_ge(s5_exp, 1)
                        v.tensor_tensor(small[:, 24:32], small[:, 16:24], ar, ALU.mult).then_inc(s5_ang, 1)
                        th, kk = small[:, 208:216], small[:, 216:224]
                        step(v.tensor_tensor(th, small[:, 16:24], ai, ALU.mult))

                        def reduce_angle(t, k):
                            step(v.tensor_scalar(k, t, 1.0 / TWO_PI, ROUND, ALU.mult, ALU.add))
                            step(v.tensor_scalar(k, k, ROUND, None, ALU.subtract))
                            for part in (PI_A, PI_B, PI_C):
                                step(v.scalar_tensor_tensor(out=t, in0=k, scalar=-part, in1=t, op0=ALU.mult, op1=ALU.add))

                        reduce_angle(th, kk)
                        step(v.tensor_tensor(s5a, bc(th, 2, P), bc(cst[:, C_TAU:C_TAU + P], 1, NJ), ALU.mult))
                        reduce_angle(s5a, s5b)
                        v.tensor_scalar(s5a, s5a, 3.1415925, -3.1415925, ALU.min, ALU.max).then_inc(s5_ang, 1)
                        v.wait_ge(row_load, 16)
                        lam = row[:, R_LAM:R_LAM + 128].rearrange("p (a b d) -> p a b d", a=2, b=2)
                        step(v.tensor_tensor(small[:, 224:288].rearrange("p (a d) -> p a d", a=2), lam[:, :, 0, :], lam[:, :, 1, :], ALU.mult))
                        v.reduce_sum(small[:, 40:42], small[:, 224:288].rearrange("p (a d) -> p a d", a=2), AX).then_inc(lam_sum, 1)
                        step(v.tensor_scalar(row[:, R_FQ:R_FQ + HD], row[:, R_FQ:R_FQ + HD], HD ** -0.5, None, ALU.mult))
                        step(v.tensor_scalar(row[:, R_DQ:R_DQ + HD], row[:, R_DQ:R_DQ + HD], HD ** -0.5, None, ALU.mult))
                        step(v.tensor_scalar(row[:, R_CQ:R_CQ + DH], row[:, R_CQ:R_CQ + DH], DH ** -0.5, None, ALU.mult))
                    for i in (0, 2, 4):
                        v.wait_ge(z_ps, 6 * b + i + 1)
                        v.tensor_copy(z[:, b, Z_CUTS[i]:Z_CUTS[i + 1]], ps[:, i, 0:Z_CUTS[i + 1] - Z_CUTS[i]]).then_inc(z_dve, 1)

                v.wait_ge(s5_sin, 2)
                step(v.tensor_tensor(cosT[:, :, :], cosT[:, :, :], cosT[:, :, :], ALU.mult))
                step(v.tensor_scalar(cosT[:, :, :], cosT[:, :, :], -2.0, 1.0, ALU.mult, ALU.add))
                v.wait_ge(s5_exp, 2)
                ar, ai, mag = s5p[:, S_AR:S_AR + NJ], s5p[:, S_AI:S_AI + NJ], small[:, 32:40]
                nr, ni, den, t0, t1, cr, ci = [small[:, 288 + 8 * i:296 + 8 * i] for i in range(7)]
                step(v.tensor_tensor(nr, mag, cosT[:, :, 0], ALU.mult))
                step(v.tensor_scalar(nr, nr, 1.0, None, ALU.subtract))
                step(v.tensor_tensor(ni, mag, sinT[:, :, 0], ALU.mult))
                step(v.tensor_tensor(t0, ar, ar, ALU.mult))
                step(v.tensor_tensor(t1, ai, ai, ALU.mult))
                step(v.tensor_tensor(den, t0, t1, ALU.add))
                step(v.reciprocal(den, den))
                step(v.tensor_tensor(t0, nr, ar, ALU.mult))
                step(v.tensor_tensor(t1, ni, ai, ALU.mult))
                step(v.tensor_tensor(cr, t0, t1, ALU.add))
                step(v.tensor_tensor(cr, cr, den, ALU.mult))
                step(v.tensor_tensor(t0, ni, ar, ALU.mult))
                step(v.tensor_tensor(t1, nr, ai, ALU.mult))
                step(v.tensor_tensor(ci, t0, t1, ALU.subtract))
                step(v.tensor_tensor(ci, ci, den, ALU.mult))
                br = s5p[:, S_BR:S_BR + P].rearrange("p (j c) -> p j c", c=S5_C)
                bi = s5p[:, S_BI:S_BI + P].rearrange("p (j c) -> p j c", c=S5_C)
                b0, b1, b2 = [T[:, 5120 + P * i:5120 + P * (i + 1)].rearrange("p (j c) -> p j c", c=S5_C) for i in range(3)]
                bx = T[:, 5632:6144].rearrange("p (r j g c) -> p r j g c", r=2, j=NJ, g=2)
                hm2 = cst[:, C_HM2:C_HM2 + 2]
                step(v.tensor_tensor(b0, br, bc(cr, 2, S5_C), ALU.mult))
                step(v.tensor_tensor(b1, bi, bc(ci, 2, S5_C), ALU.mult))
                step(v.tensor_tensor(b2, b0, b1, ALU.subtract))
                for g in range(2):
                    step(v.tensor_scalar(bx[:, 0, :, g, :], b2, hm2[:, g:g + 1], None, ALU.mult))
                step(v.tensor_tensor(b0, bi, bc(cr, 2, S5_C), ALU.mult))
                step(v.tensor_tensor(b1, br, bc(ci, 2, S5_C), ALU.mult))
                step(v.tensor_tensor(b2, b0, b1, ALU.add))
                step(v.tensor_scalar(bx[:, 1, :, 0, :], b2, hm2[:, 0:1], None, ALU.mult))
                v.tensor_scalar(bx[:, 1, :, 1, :], b2, hm2[:, 1:2], None, ALU.mult).then_inc(s5_bx, 1)
                step(v.tensor_scalar(s5p[:, S_CI:S_CI + GW], s5p[:, S_CI:S_CI + GW], -1.0, None, ALU.mult))

                v.wait_ge(lam_exp, 1)
                nlam = small[:, 44:45]
                step(v.tensor_tensor(nlam, small[:, 43:44], small[:, 42:43], ALU.subtract))
                step(v.tensor_tensor(nlam, nlam, row[:, R_LC:R_LC + 1], ALU.subtract))
                step(v.tensor_scalar(row[:, R_CO:R_CO + HD], row[:, R_CO:R_CO + HD], row[:, R_LC + 1:R_LC + 2], None, ALU.mult))

                v.wait_ge(z_act, 6)
                f = small[:, 48:56].rearrange("p (b n) -> p b n", b=NB)
                v.tensor_tensor(f, z[:, :, FF:FF + NH], bc(row[:, R_BF:R_BF + NH], 1, NB), ALU.add).then_inc(f_bias, 1)
                v.wait_ge(f_ln, 1)
                v.wait_ge(f_bias, 1)
                ls = small[:, 352:360]
                nls = small[:, 360:368]
                step(v.tensor_scalar(nls, small[:, 48:56], 0.0, None, ALU.min))
                step(v.tensor_tensor(ls, nls, small[:, 64:72], ALU.subtract))
                step(v.tensor_scalar(nls, ls, -1.0, None, ALU.mult))
                lsx = small[:, 512:768].rearrange("p (n k) -> p n k", n=1)
                v.nop().then_inc(f_ready, 1)

                for b in range(NB):
                    for i, (c0, w) in enumerate(((FQ, HD), (DQ, HD), (CQ, DH))):
                        n = 2 * GW // w
                        o = 96 + (0, 8, 16)[i]
                        s = T[:, 2048 + 512 * i:2560 + 512 * i]
                        step(v.tensor_tensor(s, z[:, b, c0:c0 + 512], z[:, b, c0:c0 + 512], ALU.mult))
                        step(v.reduce_sum(small[:, o:o + n], s.rearrange("p (n d) -> p n d", d=w), AX))
                        step(v.tensor_scalar(small[:, o:o + n], small[:, o:o + n], 1.0 / w, EPS, ALU.mult, ALU.add))
                    v.reciprocal(small[:, 96:128], small[:, 96:128]).then_inc(qk_inv, 1)
                    v.wait_ge(qk_rstd, b + 1)
                    for i, (c0, w, r0) in enumerate(((FQ, HD, R_FQ), (DQ, HD, R_DQ), (CQ, DH, R_CQ))):
                        n = 2 * GW // w
                        o = 128 + 32 * b + (0, 8, 16)[i]
                        zz = z[:, b, c0:c0 + 512].rearrange("p (n d) -> p n d", d=w)
                        step(v.tensor_tensor(zz, zz, bc(small[:, o:o + n], 2, w), ALU.mult))
                        zz = z[:, b, c0:c0 + 512].rearrange("p (a n d) -> p a n d", a=2, d=w)
                        gg = bc(row[:, r0:r0 + 2 * w].rearrange("p (a d) -> p a d", a=2), 2, n // 2)
                        v.tensor_tensor(zz, zz, gg, ALU.mult).then_inc(qk_ready, 1)
                        v.wait_ge(qk_ready, 3 * b + i + 1)

                ob = 0
                for b in range(NB):
                    nk = P * (b + 1)
                    cb, sbn = cosT, sinT
                    if b:
                        v.wait_ge(mixed_ready, b)
                    for hf in range(2):
                        v.wait_ge(bu_ps, 2 * b + hf + 1)
                        js = slice(4 * hf, 4 * hf + 4)
                        re = ps[:, 6, :].rearrange("p (j t) -> p j t", t=P)
                        im = ps[:, 7, :].rearrange("p (j t) -> p j t", t=P)
                        step(v.tensor_tensor(s5a[:, js, :], cb[:, js, :], re, ALU.mult))
                        step(v.tensor_tensor(s5c[:, js, :], sbn[:, js, :], im, ALU.mult))
                        step(v.tensor_tensor(s5b[:, js, :], cb[:, js, :], im, ALU.mult))
                        v.tensor_tensor(s5d[:, 0:4, :], sbn[:, js, :], re, ALU.mult).then_inc(bu_used, 1)
                        v.wait_ge(bu_used, 2 * b + hf + 1)
                        step(v.tensor_tensor(s5a[:, js, :], s5a[:, js, :], s5c[:, js, :], ALU.add))
                        step(v.tensor_tensor(s5b[:, js, :], s5b[:, js, :], s5d[:, 0:4, :], ALU.subtract))
                    carry = small[:, 384:400]
                    for j in range(NJ):
                        for s, buf in enumerate((s5a, s5b)):
                            init = 0.0 if b == 0 else carry[:, s * NJ + j:s * NJ + j + 1]
                            step(v.tensor_tensor_scan(buf[:, j, :], rep(mag[:, j:j + 1], P),
                                                      buf[:, j, :], init, ALU.mult, ALU.add))
                    step(v.tensor_tensor(s5c, cosT[:, :, :], s5a, ALU.mult))
                    step(v.tensor_tensor(s5d, sinT[:, :, :], s5b, ALU.mult))
                    step(v.tensor_tensor(s5c, s5c, s5d, ALU.subtract))
                    step(v.tensor_tensor(s5b, cosT[:, :, :], s5b, ALU.mult))
                    step(v.tensor_tensor(s5a, sinT[:, :, :], s5a, ALU.mult))
                    step(v.tensor_tensor(s5b, s5a, s5b, ALU.add))
                    if b == 0:
                        step(v.tensor_copy(carry[:, 0:NJ], s5c[:, :, P - 1]))
                        step(v.tensor_copy(carry[:, NJ:2 * NJ], s5b[:, :, P - 1]))
                    v.nop().then_inc(s5_state, 1)
                    for g in range(4):
                        if g < 3:
                            v.wait_ge(qkT_ps, 3 * b + g + 1)
                            tq = ps[:, 4, 0:256].rearrange("p (i t) -> p i t", t=P)
                            if g < 2:
                                step(v.tensor_tensor(qm[:, 0:512].rearrange("p (i c t) -> p i c t", i=2, c=2), bc(tq, 2, 2),
                                                     bc(bc(cst[:, C_HM2:C_HM2 + 2], 1, 2), 3, P), ALU.mult))
                            else:
                                step(v.tensor_tensor(qm2[:, 0:1024].rearrange("p (i c t) -> p i c t", i=2, c=4), bc(tq, 2, 4),
                                                     bc(bc(cst[:, C_HM4:C_HM4 + 4], 1, 2), 3, P), ALU.mult))
                            v.tensor_copy(kT[:, g, :, b * P:(b + 1) * P],
                                          ps[:, 4, 256:512].rearrange("p (i t) -> p i t", t=P)).then_inc(kT_ready, 1)
                        v.wait_ge(logit_ps, 4 * b + g + 1)
                        lg = ps[:, 0:2, :].rearrange("p c n -> p (c n)")[:, 0:4 * nk].rearrange("p (n k) -> p n k", k=nk)
                        step(v.reduce_max(small[:, 76:80], lg, AX))
                        v.tensor_scalar(small[:, 72:76], small[:, 76:80], -1.0, None, ALU.mult).then_inc(logit_max, 1)
                        v.wait_ge(p_exp, 16 * b + 4 * g + 4)
                        step(v.reciprocal(small[:, 84:88], small[:, 80:84]))
                        if g >= 2:
                            step(v.tensor_scalar(small[:, 88:92], small[:, 84:88], nlam, None, ALU.mult))
                            for i in range(2):
                                step(v.tensor_scalar(pbuf[:, 2 * i + 1, 0:nk], pbuf[:, 2 * i + 1, 0:nk],
                                                     small[:, 89 + 2 * i:90 + 2 * i], None, ALU.mult))
                                step(v.scalar_tensor_tensor(out=pbuf[:, 2 * i, 0:nk], in0=pbuf[:, 2 * i, 0:nk],
                                                            scalar=small[:, 84 + 2 * i:85 + 2 * i],
                                                            in1=pbuf[:, 2 * i + 1, 0:nk], op0=ALU.mult, op1=ALU.add))
                        v.nop().then_inc(p_ready, 1)
                        v.wait_ge(o_ps, 4 * b + g + 1)
                        if g < 2:
                            o = ps[:, 5, 256:512].rearrange("p (n d) -> p n d", d=HD)
                            v.tensor_tensor(mixed[:, b, g * GW:(g + 1) * GW].rearrange("p (n d) -> p n d", d=HD), o,
                                            bc(small[:, 84:88], 2, HD), ALU.mult).then_inc(o_used, 1)
                        else:
                            o = ps[:, 5, 256:384]
                            v.tensor_copy(mixed[:, b, 2 * GW + (g - 2) * 128:2 * GW + (g - 1) * 128], o).then_inc(o_used, 1)
                        v.wait_ge(o_used, 4 * b + g + 1)
                    co = mixed[:, b, 2 * GW:3 * GW]
                    step(v.tensor_tensor(T[:, 2048:2304], co, co, ALU.mult))
                    step(v.reduce_sum(small[:, 192:196], T[:, 2048:2304].rearrange("p (n d) -> p n d", d=HD), AX))
                    step(v.tensor_scalar(small[:, 192:196], small[:, 192:196], 1.0 / HD, EPS, ALU.mult, ALU.add))
                    v.reciprocal(small[:, 192:196], small[:, 192:196]).then_inc(co_inv, 1)
                    v.wait_ge(co_rstd, b + 1)
                    co = co.rearrange("p (n d) -> p n d", d=HD)
                    step(v.tensor_tensor(co, co, bc(small[:, 196:200], 2, HD), ALU.mult))
                    step(v.tensor_tensor(co, co, bc(row[:, R_CO:R_CO + HD], 1, NH), ALU.mult))
                    v.wait_ge(y_ps, b + 1)
                    step(v.tensor_tensor(T[:, 4608:4864], z[:, b, SU:SU + GW], row[:, R_SD:R_SD + GW], ALU.mult))
                    v.tensor_tensor(T[:, 4096:4352], T[:, 4608:4864], ps[:, 5, 0:256], ALU.add).then_inc(y_ready, 1)
                    v.wait_ge(gT_ps, b + 1)
                    v.tensor_copy(T[:, 4864:5120], ps[:, 5, 0:256]).then_inc(gT_ready, 1)
                    v.wait_ge(glu_ps, b + 1)
                    v.tensor_tensor(T[:, 4352:4608], ps[:, 5, 0:256], row[:, R_GB:R_GB + GW], ALU.add).then_inc(glu_sum, 1)
                    v.wait_ge(glu_sig, b + 1)
                    v.tensor_tensor(mixed[:, b, 3 * GW:4 * GW], T[:, 4096:4352], T[:, 4352:4608], ALU.mult).then_inc(mixed_ready, 1)

                for b in range(NB):
                    v.wait_ge(mT_ps, b + 1)
                    if b:
                        v.wait_ge(wo_ps, 1)
                    v.tensor_copy(hT[:, 0:4, :], ps[:, 2, :].rearrange("p (k t) -> p k t", t=P)).then_inc(mT_ready, 1)
                    v.wait_ge(wo_ps, b + 1)
                    v.tensor_tensor(x[:, b, :], x[:, b, :], ps[:, 0:2, :].rearrange("p c n -> p (c n)"), ALU.add).then_inc(x_ready, 1)
                for b in range(NB):
                    rms_apply(NB + b)

                for b in range(NB):
                    v.wait_ge(hT_ps, NB + b + 1)
                    if b:
                        v.wait_ge(qT_ps, 4)
                    step(v.tensor_copy(hT[:, 0:4, :], ps[:, 2, :].rearrange("p (k t) -> p k t", t=P)))
                    v.tensor_copy(hT[:, 4:8, :], ps[:, 3, :].rearrange("p (k t) -> p k t", t=P)).then_inc(hT_ready, 1)
                    for i in (0, 2):
                        v.wait_ge(qT_ps, 4 * b + i + 1)
                        v.tensor_copy(qts[:, 4 * i:4 * i + 4, :], ps[:, 4 + i, :].rearrange("p (n t) -> p n t", t=P)).then_inc(qT_ready, 1)
                    for n in range(HP):
                        if n % 4 == 0:
                            v.wait_ge(sc_ps, 4 * b + n // 4 + 1)
                        sc = ps[:, n // 4, (n % 4) * NK:(n % 4 + 1) * NK]
                        step(v.max(v16[:, n, 0:8], sc))
                        step(v.max_index(i16[:, n, 0:8], v16[:, n, 0:8], sc))
                        step(v.match_replace(sc2, v16[:, n, 0:8], sc, NEG))
                        step(v.max(v16[:, n, 8:16], sc2))
                        ins = v.max_index(i16[:, n, 8:16], v16[:, n, 8:16], sc2)
                        if n % 4 == 3:
                            ins.then_inc(sc_used, 1)
                            v.wait_ge(sc_used, 4 * b + n // 4 + 1)
                        else:
                            step(ins)
                    step(v.tensor_copy(i16f, i16[:, :, :]))
                    for n in range(PH):
                        c3 = cand.rearrange("p (a b) -> p a b", b=TOPK)
                        step(v.tensor_tensor(c3, bc(v16[:, 2 * n, :], 2, TOPK), bc(v16[:, 2 * n + 1, :], 1, TOPK), ALU.add))
                        step(v.max(best[:, n, 0:8], cand))
                        step(v.max_index(pos[:, n, 0:8], best[:, n, 0:8], cand))
                        step(v.match_replace(cand2, best[:, n, 0:8], cand, NEG))
                        step(v.max(best[:, n, 8:16], cand2))
                        step(v.max_index(pos[:, n, 8:16], best[:, n, 8:16], cand2))
                    v.tensor_tensor(gates[:, b, :].rearrange("p (n k) -> p n k", k=TOPK), best,
                                    bc(best[:, :, 0], 2, TOPK), ALU.subtract).then_inc(best_sub, 1)
                    pos_f = pos[:, :, :].rearrange("p n k -> p (n k)")
                    i4 = i16f.rearrange("p (n s) k -> p n s k", s=2)
                    for s in range(2):
                        if s == 0:
                            step(v.tensor_single_scalar(posd[:, :], pos_f, 4, op=ALU.logical_shift_right))
                        else:
                            step(v.tensor_single_scalar(posd[:, :], pos_f, TOPK - 1, op=ALU.bitwise_and))
                        step(v.tensor_copy(posf, posd[:, :]))
                        step(v.tensor_tensor(hit.rearrange("p n k a -> p (n k) a"), bc(posf, 2, TOPK),
                                             bc(cst[:, C_IOTA:C_IOTA + TOPK], 1, SLOTS), ALU.is_equal))
                        step(v.tensor_tensor(hit, hit, bc(i4[:, :, s, :], 2, TOPK), ALU.mult))
                        step(v.reduce_sum(idf[s], hit.rearrange("p n k a -> p (n k) a"), AX))
                    step(v.scalar_tensor_tensor(out=idf[0], in0=idf[0], scalar=float(NK), in1=idf[1], op0=ALU.mult, op1=ALU.add))
                    step(v.tensor_scalar(idf[0], idf[0], row[:, R_LC + 2:R_LC + 3], None, ALU.add))
                    v.tensor_copy(ids[:, b, :], idf[0]).then_inc(ids_ready, 1)
                    v.wait_ge(gate_exp, b + 1)
                    g3 = gates[:, b, :].rearrange("p (n k) -> p n k", k=TOPK)
                    step(v.reduce_sum(small[:, 400:408], g3, AX))
                    step(v.reciprocal(small[:, 400:408], small[:, 400:408]))
                    step(v.tensor_tensor(g3, g3, bc(small[:, 400:408], 2, TOPK), ALU.mult))
                for b in range(NB):
                    with v.Fori(0, ITERS) as it:
                        for g in range(2):
                            for s in range(g * RING_G, (g + 1) * RING_G):
                                turn = (layer * NB + b) * ITERS + it
                                v.wait_ge(u_in[s], turn * 16 + 16)
                                v.wait_ge(dots_done, turn * RING + RING + s)
                                v.wait_ge(keys_load, 16)
                                v.tensor_tensor_reduce(junk, ring_u[:, s, :], h[:, b, :], 1.0, 0.0, ALU.mult, ALU.add,
                                                       dots[:, s:s + 1]).then_inc(dots_done, 1)
                            v.wait_ge(gelu_done, turn * 2 + g + 1)
                            v.wait_ge(v_used, turn * RING + (g + 1) * RING_G)
                            v.wait_ge(keys_load, 16)
                            for s in range(g * RING_G, (g + 1) * RING_G):
                                v.tensor_scalar(diag[:, s, :], ident, acts[:, s:s + 1], gates[:, b, bass.ds(it * RING + s, 1)],
                                                ALU.mult, ALU.mult).then_inc(diag_ready, 1)
                    v.wait_ge(acc_ps, b + 1)
                    v.tensor_copy(x[:, b, :], ps[:, 0:2, :].rearrange("p c n -> p (c n)")).then_inc(x_done, 1)

            @block.tensor
            def _(pe):
                def turn_rows(src, banks, done):
                    for k in range(KC):
                        mm = pe.transpose(ps[:, banks[k // 4], (k % 4) * P:(k % 4 + 1) * P], src[:, k * P:(k + 1) * P], ident)
                    mm.then_inc(done, 1)

                for b in range(NB):
                    pe.wait_ge(h_ready, b + 1)
                    if b:
                        pe.wait_ge(hT_ready, 2)
                    turn_rows(h[:, b, :], (6, 7), hT_ps)
                    pe.wait_ge(hT_ready, 2 * b + 2)
                    for k in range(KC):
                        if b == 0:
                            pe.wait_ge(win_in[k], 16)
                        for i in range(6):
                            if b and k == 0:
                                if i % 2:
                                    pe.wait_ge(z_act, i // 2 + 1)
                                else:
                                    pe.wait_ge(z_dve, i // 2 + 1)
                            mm = pe.matmul(ps[:, i, 0:Z_CUTS[i + 1] - Z_CUTS[i]], hT[:, k, :], win[:, k, Z_CUTS[i]:Z_CUTS[i + 1]],
                                           start=(k == 0), stop=(k == KC - 1))
                            if k == KC - 1:
                                mm.then_inc(z_ps, 1)
                pe.wait_ge(s5_bx, 1)
                pe.wait_ge(z_dve, 6)
                bx = T[:, 5632:6144]
                for i in range(4):
                    mm = pe.transpose(ps[:, 4, i * P:(i + 1) * P], bx[:, i * P:(i + 1) * P], ident)
                mm.then_inc(s5_bt_ps, 1)
                pe.wait_ge(z_act, 6)
                pt = 0
                ls, nls = small[:, 352:360], small[:, 360:368]
                for b in range(NB):
                    nk = P * (b + 1)
                    if b:
                        pe.wait_ge(glu_sum, b)
                    for i in range(2):
                        mm = pe.transpose(ps[:, 5, i * P:(i + 1) * P], z[:, b, SU + i * P:SU + (i + 1) * P], ident)
                    mm.then_inc(uT_ps, 1)
                    pe.wait_ge(uT_ready, b + 1)
                    pe.wait_ge(s5_bt, 4)
                    uT = T[:, 7936:8192].rearrange("p (r t) -> p r t", t=P)
                    for hf in range(2):
                        pe.wait_ge(bu_used, 2 * b + hf) if b + hf else None
                        for r in range(2):
                            for j in range(4):
                                mm = pe.matmul(ps[:, 6 + r, j * P:(j + 1) * P], bT[:, 2 * r + hf, j, :], uT[:, hf, :],
                                               start=True, stop=True)
                        mm.then_inc(bu_ps, 1)
                    for g in range(4):
                        if g < 3:
                            c0 = (FQ, DQ, CQ)[g]
                            pe.wait_ge(qk_ready, 3 * b + g + 1)
                            if b + g:
                                pe.wait_ge(kT_ready, 3 * b + g)
                            for i in range(4):
                                mm = pe.transpose(ps[:, 4, i * P:(i + 1) * P], z[:, b, c0 + i * P:c0 + (i + 1) * P], ident)
                            mm.then_inc(qkT_ps, 1)
                            pe.wait_ge(kT_ready, 3 * b + g + 1)
                        if b + g:
                            pe.wait_ge(p_exp, 16 * b + 4 * g)
                        if g == 0:
                            pe.wait_ge(f_ready, 1)
                        lg = ps[:, 0:2, :].rearrange("p c n -> p (c n)")
                        for i in range(4):
                            dst = lg[:, i * nk:(i + 1) * nk]
                            own = lg[:, i * nk + b * P:(i + 1) * nk]
                            if g < 2:
                                q, k = qm[:, i * P:(i + 1) * P], kT[:, g, i // 2, 0:nk]
                            else:
                                q = qm[:, (g - 2) * 512 + i * P:(g - 2) * 512 + (i + 1) * P]
                                k = kT[:, 2, g - 2, 0:nk]
                            pe.matmul(dst, q, k, start=True, stop=False)
                            if g == 0:
                                for s in range(b + 1):
                                    at = lambda t: t[:, s * NH + i:s * NH + i + 1]
                                    pe.matmul(dst, tri if s == b else ones,
                                              rep(at(ls), nk), start=False, stop=False)
                                    pe.matmul(own if s == b else dst, rep(at(nls), P),
                                              tri if s == b else triones, start=False, stop=False)
                                mm = pe.matmul(own, ident, causal, start=False, stop=True)
                            else:
                                n = i if g == 1 else NH + 2 * (g - 2) + i // 2
                                mm = pe.matmul(dst, ident, bias[:, n, SEQ - nk:SEQ], start=False, stop=True)
                        mm.then_inc(logit_ps, 1)
                        pe.wait_ge(p_ready, 4 * b + g + 1)
                        heads = 4 if g < 2 else 2
                        nt = heads * (b + 1)
                        t = 0
                        base = pt
                        for i in range(heads):
                            for s in range(b + 1):
                                if t % 4 == 0 and base + t // 4 > 0:
                                    pe.wait_ge(pT_ready, base)
                                src = pbuf[:, i if g < 2 else 2 * i, s * P:(s + 1) * P]
                                mm = pe.transpose(ps[:, 2 + t // 4, (t % 4) * P:(t % 4 + 1) * P], src, ident)
                                t += 1
                                if t % 4 == 0 or t == nt:
                                    mm.then_inc(pT_ps, 1)
                                    pt += 1
                        pe.wait_ge(pT_ready, pt)
                        if b + g:
                            pe.wait_ge(o_used, 4 * b + g)
                        v0 = (FV, DV, CV, CV + 128)[g]
                        for i in range(heads):
                            for s in range(b + 1):
                                mm = pe.matmul(ps[:, 5, 256 + i * HD:256 + (i + 1) * HD], pT[:, i * (b + 1) + s, :],
                                               z[:, s, v0 + i * HD:v0 + (i + 1) * HD], start=(s == 0), stop=(s == b))
                        mm.then_inc(o_ps, 1)
                    pe.wait_ge(s5_state, b + 1)
                    pe.wait_ge(o_used, 4 * b + 4)
                    for j in range(NJ):
                        y = ps[:, 5, j * 32:(j + 1) * 32]
                        pe.matmul(y, s5c[:, j, :], s5p[:, S_CR + 32 * j:S_CR + 32 * (j + 1)], start=True, stop=False)
                        mm = pe.matmul(y, s5b[:, j, :], s5p[:, S_CI + 32 * j:S_CI + 32 * (j + 1)], start=False, stop=True)
                    mm.then_inc(y_ps, 1)
                    pe.wait_ge(g_ready, b + 1)
                    for i in range(2):
                        mm = pe.transpose(ps[:, 5, i * P:(i + 1) * P], T[:, 4096 + i * P:4096 + (i + 1) * P], ident)
                    mm.then_inc(gT_ps, 1)
                    pe.wait_ge(gT_ready, b + 1)
                    pe.wait_ge(glu_load, 16)
                    for i in range(2):
                        mm = pe.matmul(ps[:, 5, 0:256], T[:, 4864 + i * P:4864 + (i + 1) * P], glu[:, i, :], start=(i == 0), stop=(i == 1))
                    mm.then_inc(glu_ps, 1)

                pe.wait_ge(wout_load, 16)
                for b in range(NB):
                    pe.wait_ge(mixed_ready, b + 1)
                    if b:
                        pe.wait_ge(mT_ready, 2)
                    turn_rows(mixed[:, b, :], (2, 3), mT_ps)
                    pe.wait_ge(mT_ready, 2 * b + 2)
                    if b:
                        pe.wait_ge(x_ready, b)
                    for c in range(2):
                        for k in range(KC):
                            mm = pe.matmul(ps[:, c, :], hT[:, k, :], wout_v[:, k, c * 512:(c + 1) * 512], start=(k == 0), stop=(k == KC - 1))
                    mm.then_inc(wo_ps, 1)
                for b in range(NB):
                    pe.wait_ge(h_ready, NB + b + 1)
                    pe.wait_ge(mT_ready, 4)
                    if b:
                        pe.wait_ge(sc_used, 4)
                    turn_rows(h[:, b, :], (2, 3), hT_ps)
                    pe.wait_ge(hT_ready, 4 + b + 1)
                    for n in range(HP):
                        if n == 0 and b == 0:
                            pe.wait_ge(wqa_load, 16)
                        if n == PH and b == 0:
                            pe.wait_ge(wqb_load, 16)
                        if b and n % 4 == 0:
                            pe.wait_ge(qT_ready, 4)
                        for k in range(KC):
                            mm = pe.matmul(ps[:, 4 + n // 4, (n % 4) * P:(n % 4 + 1) * P],
                                           wq_v[n // PH][:, k, (n % PH) * P:(n % PH + 1) * P], hT[:, k, :],
                                           start=(k == 0), stop=(k == KC - 1))
                        if n % 4 == 3:
                            mm.then_inc(qT_ps, 1)
                    pe.wait_ge(keys_load, 16)
                    pe.wait_ge(x_ready, 2)
                    pe.wait_ge(qT_ready, 4 * b + 4)
                    for n in range(HP):
                        mm = pe.matmul(ps[:, n // 4, (n % 4) * NK:(n % 4 + 1) * NK], qts[:, n, :], kts[:, n, :], start=True, stop=True)
                        if n % 4 == 3:
                            mm.then_inc(sc_ps, 1)
                pe.wait_ge(sc_used, 8)
                for b in range(NB):
                    if b:
                        pe.wait_ge(x_done, b)
                    for c in range(2):
                        pe.matmul(ps[:, c, :], zero[:, :], x[:, b, c * 512:(c + 1) * 512], start=True, stop=False)
                    with pe.Fori(0, ITERS) as it:
                        for s in range(RING):
                            turn = (layer * NB + b) * ITERS + it
                            pe.wait_ge(v_in[s], turn * 16 + 16)
                            pe.wait_ge(diag_ready, turn * RING + s + 1)
                            pe.wait_ge(keys_load, 16)
                            for c in range(2):
                                mm = pe.matmul(ps[:, c, :], diag[:, s, :], ring_v[:, s, c * 512:(c + 1) * 512], start=False, stop=False)
                            mm.then_inc(v_used, 1)
                    for c in range(2):
                        mm = pe.matmul(ps[:, c, :], ident, x[:, b, c * 512:(c + 1) * 512], start=False, stop=True)
                    mm.then_inc(acc_ps, 1)

            @block.gpsimd
            def _(gp):
                gp.wait_ge(qT_ps, 8)
                for b in range(NB):
                    gp.wait_ge(ids_ready, b + 1)
                    with gp.Fori(0, ITERS) as it:
                        turn = (layer * NB + b) * ITERS + it
                        for g in range(2):
                            ss = range(g * RING_G, (g + 1) * RING_G)
                            gp.wait_ge(v_used, turn * RING + (g + 1) * RING_G)
                            gp.wait_ge(ids_ready, b + 1)
                            gp.tensor_copy(ring_ids[:, g * RING_G:(g + 1) * RING_G],
                                           ids[:, b, bass.ds(it * RING + g * RING_G, RING_G)]).then_inc(ring_staged, RING_G)
                            gp.wait_ge(ids_ready, b + 1)
                            gp.wait_ge(ring_staged, turn * RING + (g + 1) * RING_G)
                            gp.wait_ge(dots_done, turn * RING + (g + 1) * RING_G)
                            for s in ss:
                                gp.indirect_dma_start(ring_u[:, s, :], None, table_u,
                                                      bass.IndirectOffsetOnAxis(ap=ring_ids[:, s:s + 1], axis=0)).then_inc(u_in[s], 16)
                            for s in ss:
                                gp.indirect_dma_start(ring_v[:, s, :], None, table_v,
                                                      bass.IndirectOffsetOnAxis(ap=ring_ids[:, s:s + 1], axis=0)).then_inc(v_in[s], 16)

          nums = [s.num for s in layer_sems]
          assert max(nums) - min(nums) + 1 == len(nums)
          nc.sync.sem_clear(range(min(nums), max(nums) + 1))
          nc.all_engine_barrier()

        with nc.Block() as block:
            @block.sync
            def _(sp):
                sp.dma_start(out.rearrange("(b p) d -> p b d", p=P), x[:, :, :]).then_inc(out_stored, 16)
                sp.wait_ge(out_stored, 16)


def shape_constants():
    c = np.zeros((P, C_W), np.float32)
    p = np.arange(P)
    c[:, C_ID:C_ID + P] = np.eye(P)
    c[:, C_TRI:C_TRI + P] = p[:, None] <= p[None, :]
    c[:, C_ONE:C_ONE + P] = 1.0
    c[:, C_MASK:C_MASK + P] = np.where(p[None, :] <= p[:, None], 0.0, NEG)
    c[:, C_TAU:C_TAU + P] = p + 1
    for i in range(2):
        c[:, C_HM2 + i] = p // 64 == i
    for i in range(4):
        c[:, C_HM4 + i] = p // 32 == i
    c[:, C_IOTA:C_IOTA + TOPK] = np.arange(TOPK)
    return c


def bucket_constants():
    dist = 255 - np.arange(512)
    n = np.maximum(dist, 0)
    nf = np.maximum(n, MAX_EXACT).astype(np.float32)
    large = MAX_EXACT + (np.log(nf / np.float32(MAX_EXACT)) / math.log(MAX_DIST / MAX_EXACT)
                         * (BUCKETS - MAX_EXACT)).astype(np.int32)
    bucket = np.where(n < MAX_EXACT, n, np.minimum(large, BUCKETS - 1))
    c = np.zeros((BUCKETS + 2, 512), np.float32)
    c[bucket, np.arange(512)] = 1.0
    count = (dist <= 128).astype(int) + (dist % 4 == 0) + (dist % 16 == 0)
    seen = (dist >= 0) & (count > 0)
    c[BUCKETS] = np.where(seen, np.log(np.maximum(count, 1)), NEG)
    c[BUCKETS + 1] = np.where(dist >= 0, 0.0, NEG)
    return c


def layer_constants():
    c = np.zeros((DEPTH, 4), np.float32)
    for n in range(DEPTH):
        lam = 0.8 - 0.6 * math.exp(-0.3 * n)
        c[n] = lam, 1.0 - lam, n * NE, 0.0
    return c


def kernel(x, w_in, b_forget, w_out, norm_mix, norm_ffn, fox_q_norm, fox_k_norm, dil_q_norm, dil_k_norm,
           diff_q_norm, diff_k_norm, diff_lambda, diff_out_norm, rel_bias, s5_a_re, s5_a_im, s5_log_dt,
           s5_b_re, s5_b_im, s5_c_re, s5_c_im, s5_d, s5_glu_w, s5_glu_b, peer_wq, peer_keys, peer_u, peer_v):
    import concourse.bacc as bacc
    from concourse.bass_utils import run_bass_kernel_spmd

    L = DEPTH
    rows = np.concatenate([np.asarray(t).reshape(L, -1) for t in (
        fox_q_norm, fox_k_norm, dil_q_norm, dil_k_norm, diff_q_norm, diff_k_norm, diff_out_norm, b_forget,
        diff_lambda, layer_constants(), s5_d, s5_glu_b)], axis=1)

    def by_state(t):
        t = np.asarray(t)
        t = t.reshape((L, NJ, 2, S5_N) + t.shape[3:])
        t = np.moveaxis(t, 1, 3)
        return t.reshape((L, P, -1))

    def c_blocks(t):
        t = np.asarray(t)
        o = np.zeros((L, 2, S5_N, NJ, 2, S5_C), t.dtype)
        for g in range(2):
            o[:, g, :, :, g, :] = t.reshape(L, NJ, 2, S5_C, S5_N)[:, :, g].transpose(0, 3, 1, 2)
        return o.reshape(L, P, GW)

    dt = np.repeat(np.asarray(s5_log_dt)[:, :, None], S5_N, axis=2)
    s5 = np.concatenate([by_state(s5_a_re), by_state(s5_a_im), by_state(dt), by_state(s5_b_re), by_state(s5_b_im),
                         c_blocks(s5_c_re), c_blocks(s5_c_im)], axis=2)
    keys = np.asarray(peer_keys).reshape(L, HP, NK, P).transpose(0, 3, 1, 2)
    arrays = {
        "x_in": np.asarray(x).reshape(SEQ, D), "w_in": w_in, "w_out": w_out, "row_in": rows,
        "gain_mix": norm_mix, "gain_ffn": norm_ffn, "s5_in": s5, "glu_w": s5_glu_w, "peer_wq": peer_wq,
        "keys_t": keys, "table_u": np.asarray(peer_u).reshape(L * NE, D), "table_v": np.asarray(peer_v).reshape(L * NE, D),
        "rel_bias": rel_bias, "const_in": shape_constants(), "bucket_in": bucket_constants(),
    }
    arrays = {k: np.ascontiguousarray(v) for k, v in arrays.items()}
    nc = bacc.Bacc("TRN2", target_bir_lowering=False, num_devices=1)
    args = {k: nc.dram_tensor(k, v.shape, mybir.dt.from_np(v.dtype), kind="ExternalInput").ap() for k, v in arrays.items()}
    out = nc.dram_tensor("out", (SEQ, D), F32, kind="ExternalOutput").ap()
    trunk(nc, **args, out=out)
    r = run_bass_kernel_spmd(nc, [arrays], core_ids=[0])
    return r.results[0]["out"].reshape(1, SEQ, D)
```

```python
import math
from contextlib import ExitStack

import numpy as np

import concourse.bass as bass
from concourse import mybir

ALU = mybir.AluOpType
ACT = mybir.ActivationFunctionType
AX = mybir.AxisListType.X
F32 = mybir.dt.float32
U32 = mybir.dt.uint32

P = 128
D = 1024
SEQ = 256
NB = SEQ // P
DEPTH = 2
KC = D // P
GW = D // 4
HD = 64
NH = GW // HD
DH = HD // 2
S5_G, S5_C, S5_N = 16, 16, 64
NJ = S5_G * S5_N // P
BUCKETS, MAX_EXACT, MAX_DIST = 32, 16, 2048
NK = 128
NE = NK * NK
PH, TOPK = 8, 16
HP = 2 * PH
SLOTS = PH * TOPK
EPS = 1e-6
NEG = -1.0e30
RING_G = 4
RING = 2 * RING_G
ITERS = SLOTS // RING

PASSES = DEPTH * NB
HALVES = SLOTS // RING_G

IN_SPLIT = [GW, GW, GW, NH, GW, GW, GW, GW, GW, GW, GW]
IN_ORDER = [0, 4, 7, 10, 3, 1, 5, 8, 2, 6, 9]
IN_W = sum(IN_SPLIT)
SU, FF = 3 * GW, 4 * GW
ZQ_W = FF + NH
KV_W = IN_W - ZQ_W
KEYS, VALS = 0, 3 * GW
BANK_CUTS = [0, 512, 1024, 1412, 1796, 2180, IN_W]
WIN_SLOTS = 6

R_FQ, R_FK, R_DQ, R_DK = 0, 64, 128, 192
R_CQ, R_CK = 256, 288
R_CO = 320
R_BF = 384
R_LAM = 388
R_LC = 516
R_SD = 520
R_GB = 776
R_W = 1032

C_ID, C_TRI, C_ONE, C_MASK = 0, 128, 256, 384
C_TAU = 512
C_HM2, C_HM4 = 640, 642
C_IOTA = 646
C_W = 662

S_AR, S_AI, S_DT = 0, 8, 16
S_BR, S_BI = 24, 24 + NJ * S5_C
S_CR = S_BI + NJ * S5_C
S_CI = S_CR + GW
S_W = S_CI + GW

TWO_PI = 2.0 * math.pi
PI_A = 6.28125
PI_B = 0.0019340515136718750
PI_C = TWO_PI - PI_A - PI_B
ROUND = 12582912.0


def bc(ap, axis, n):
    dims = [list(d) for d in ap.ap]
    dims.insert(axis, [0, n])
    return bass.AP(ap.tensor, ap.offset, dims)


def rep(ap, n):
    return bass.AP(ap.tensor, ap.offset, [list(ap.ap[0]), [0, n]])


class Order:

    def __init__(self, eng, sem):
        self.eng, self.sem, self.n = eng, sem, 0

    def __call__(self, ins):
        ins.then_inc(self.sem, 1)
        self.n += 1
        self.eng.wait_ge(self.sem, self.n)


def plan_steps():
    attention = [["s5 turn back", "keys 0"], ["logits 0", "s5 scan"], ["weights 0", "keys 1", "s5 turn on"],
                 ["heads 0", "logits 1"], ["weights 1", "keys 2"], ["heads 1", "logits 2"],
                 ["weights 2"], ["heads 2", "logits 3"], ["weights 3", "s5 out"], ["heads 3", "s5 gate"], ["mixed"]]
    mix = [["norm 0", "rows 0"]] + [[f"project {k}"] for k in range(KC)] + [["s5 in", "qk norm", "bu"]] + attention
    mix += [["out 0"], ["out 1"], ["norm 1", "rows 1"], ["query 0"], ["query 1", "score 0"], ["query 2", "score 1"],
            ["query 3", "score 2"], ["score 3"], ["pairs 0"], ["pairs 1"], ["ids"]]
    assert len(mix) <= HALVES + 1
    plan = []

    def do(groups, n):
        for group in groups:
            for name in group:
                word = name.rsplit(" ", 1)
                if word[-1].isdigit():
                    plan.append((word[0], n, int(word[1])))
                else:
                    plan.append((name, n, 0))

    do(mix[:1] + [[f"tables {j}" for j in range(DEPTH)] + ["lines"]] + mix[1:], 0)
    for n in range(PASSES):
        left = list(mix) if n + 1 < PASSES else []
        for i in range(HALVES):
            plan.append(("dots", n, i))
            if i == 0 and n:
                plan.append(("gathered", n - 1, 0))
            take = 1 + (i == 1 and len(left) > HALVES - 1)
            do(left[:take], n + 1)
            left = left[take:]
            plan.append(("rows of v", n, i))
    plan.append(("gathered", PASSES - 1, 0))
    return plan


def trunk(nc, x_in, w_in, w_out, row_in, gain_mix, gain_ffn, s5_in, glu_w, peer_wq, keys_t, table_u, table_v,
          rel_bias, const_in, bucket_in, out):
    ctx = ExitStack()
    with ctx:
        def sb(name, shape, dt=F32):
            return ctx.enter_context(nc.sbuf_tensor(name, shape, dt))

        def sem(name):
            return ctx.enter_context(nc.semaphore(name))

        ring_u = sb("ring_u", [P, RING, D])
        ring_v = sb("ring_v", [P, RING, D])
        W = sb("W", [P, 16384])
        x = sb("x", [P, NB, D])
        h = sb("h", [P, NB, D])
        hT = sb("hT", [P, KC, P])
        zq = sb("zq", [P, ZQ_W])
        zkv = sb("zkv", [P, NB, KV_W])
        bias = sb("bias", [P, 2 * NH, SEQ])
        cst = sb("cst", [P, C_W])
        row = sb("row", [P, R_W])
        s5t = sb("s5t", [P, 3072])
        glu = sb("glu", [P, 2, GW])
        small = sb("small", [P, 768])
        mags = sb("mags", [P, DEPTH, NJ])
        zero = sb("zero", [P, P])
        ids = sb("ids", [P, NB, SLOTS], U32)
        gates = sb("gates", [P, NB, SLOTS])
        ring_ids = sb("ring_ids", [P, RING], U32)
        dots = sb("dots", [P, RING])
        acts = sb("acts", [P, RING])
        weights = sb("weights", [P, RING])
        diag = sb("diag", [P, RING, P])
        junk = sb("junk", [P, D], mybir.dt.bfloat16)

        win = W[:, 0:WIN_SLOTS * IN_W].rearrange("p (k n) -> p k n", n=IN_W)
        wout_v = W[:, 8192:16384].rearrange("p (k n) -> p k n", k=KC)
        wq_v = [W[:, 8192 + 4096 * i:12288 + 4096 * i].rearrange("p (k n) -> p k n", k=KC) for i in range(2)]
        T = W[:, 0:8192]
        ident, tri = cst[:, C_ID:C_ID + P], cst[:, C_TRI:C_TRI + P]
        triones = cst[:, C_TRI:C_TRI + 2 * P]
        ones, causal = cst[:, C_ONE:C_ONE + P], cst[:, C_MASK:C_MASK + P]
        hm2, hm4 = cst[:, C_HM2:C_HM2 + 2], cst[:, C_HM4:C_HM4 + 4]
        mixed = h

        def by(ap, n):
            return ap.rearrange("p (n k) -> p n k", k=n)

        cosT, sinT = by(s5t[:, 0:1024], P), by(s5t[:, 1024:2048], P)
        bT = by(s5t[:, 2048:2560], P)
        cR, cI = s5t[:, 2560:2816], s5t[:, 2816:3072]
        pbuf = by(T[:, 0:1024], SEQ)
        um = by(T[:, 0:1024], P)
        pT = by(T[:, 1024:2048], P)
        qm = T[:, 2048:3072]
        kT = T[:, 3072:3584].rearrange("p (i k) -> p i k", k=SEQ)
        ybuf, sbuf, gT = T[:, 3584:3840], T[:, 3840:4096], T[:, 1024:1280]
        s5a, s5b, s5c, s5d = [by(T[:, 4096 + 1024 * i:5120 + 1024 * i], P) for i in range(4)]
        sq = T[:, 4096:5632]
        gain_m = [zkv[:, b, 0:D] for b in range(NB)]
        gain_f = T[:, 4096:5120]
        kts, qts = by(T[:, 0:2048], NK), by(T[:, 2048:4096], P)
        hit = T[:, 0:2048].rearrange("p (n k a) -> p n k a", k=TOPK, a=TOPK)
        cand, cand2, sc2 = T[:, 4096:4352], T[:, 4352:4608], T[:, 4608:4736]
        v16, i16f, best = by(T[:, 4736:4992], TOPK), by(T[:, 4992:5248], TOPK), by(T[:, 5248:5376], TOPK)
        posf, idf = T[:, 5376:5504], [T[:, 5504:5632], T[:, 5632:5760]]
        i16, pos = by(T[:, 5760:6016].bitcast(U32), TOPK), by(T[:, 6016:6144].bitcast(U32), TOPK)
        posd = T[:, 6144:6272].bitcast(U32)

        ps = ctx.enter_context(nc.psum_tensor("ps", [P, 8, 512], F32))
        toep = nc.dram_tensor("toep", [2 * NH, P, 512], F32, kind="Internal").ap()
        s5_dram = nc.dram_tensor("s5_dram", [DEPTH, P, 3072], F32, kind="Internal").ap()

        once_in, bias_in, toep_out = sem("once_in"), sem("bias_in"), sem("toep_out")
        s5_in_done = [sem(f"s5_in_{n}") for n in range(DEPTH)]
        toep_ready, toep_ps, toep_copied, zero_set = sem("toep_ready"), sem("toep_ps"), sem("toep_copied"), sem("zero_set")
        s5_tabled, s5_out, out_stored = sem("s5_tabled"), sem("s5_out"), sem("out_stored")
        u_in = [sem(f"u_in{i}") for i in range(RING)]
        v_in = [sem(f"v_in{i}") for i in range(RING)]
        ring_staged, dots_done, gelu_done, weights_done, diag_ready, v_used = (
            sem("ring_staged"), sem("dots_done"), sem("gelu_done"), sem("weights_done"), sem("diag_ready"), sem("v_used"))
        acc_ps, x_done = sem("acc_ps"), sem("x_done")
        dve_step, act_step = sem("dve_step"), sem("act_step")
        win_in = [sem(f"win_in{k}") for k in range(WIN_SLOTS)]
        wq_in = [sem(f"wq_in{k}") for k in range(2)]
        row_load, gain_load, s5_load, glu_load, ffn_load, wout_load, keys_load = (
            sem("row_load"), sem("gain_load"), sem("s5_load"), sem("glu_load"), sem("ffn_load"), sem("wout_load"),
            sem("keys_load"))
        sumsq, mean_inv, rstd, h_ready = sem("sumsq"), sem("mean_inv"), sem("rstd"), sem("h_ready")
        rows_ps, rows_dve, rows_act = sem("rows_ps"), sem("rows_dve"), sem("rows_act")
        chunk_used, z_ps, z_dve, z_act = sem("chunk_used"), sem("z_ps"), sem("z_dve"), sem("z_act")
        s5_exp, s5_ang, s5_sin, s5_bx, s5_bt_ps = sem("s5_exp"), sem("s5_ang"), sem("s5_sin"), sem("s5_bx"), sem("s5_bt_ps")
        lam_sum, lam_exp = sem("lam_sum"), sem("lam_exp")
        qk_inv, qk_rstd, qk_ready = sem("qk_inv"), sem("qk_rstd"), sem("qk_ready")
        f_bias, f_ln, f_ready = sem("f_bias"), sem("f_ln"), sem("f_ready")
        keys_ps, keys_ready = sem("keys_ps"), sem("keys_ready")
        logit_ps, logit_max, p_exp, p_ready = sem("logit_ps"), sem("logit_max"), sem("p_exp"), sem("p_ready")
        pT_ps, pT_ready, o_ps, o_used = sem("pT_ps"), sem("pT_ready"), sem("o_ps"), sem("o_used")
        co_inv, co_rstd = sem("co_inv"), sem("co_rstd")
        uT_ps, um_ready, bu_ps, bu_used = sem("uT_ps"), sem("um_ready"), sem("bu_ps"), sem("bu_used")
        s5_state, y_ps, y_ready, g_ready = sem("s5_state"), sem("y_ps"), sem("y_ready"), sem("g_ready")
        gT_ps, gT_ready, glu_ps, glu_sum, glu_sig, mixed_ready = (
            sem("gT_ps"), sem("gT_ready"), sem("glu_ps"), sem("glu_sum"), sem("glu_sig"), sem("mixed_ready"))
        mT_ps, mT_dve, mT_act, wo_ps, x_ready = sem("mT_ps"), sem("mT_dve"), sem("mT_act"), sem("wo_ps"), sem("x_ready")
        qT_ps, qT_ready, sc_ps, sc_used = sem("qT_ps"), sem("qT_ready"), sem("sc_ps"), sem("sc_used")
        best_sub, gate_exp, ids_ready, gates_ready = sem("best_sub"), sem("gate_exp"), sem("ids_ready"), sem("gates_ready")

        plan = plan_steps()

        def walk(steps):
            for name, n, i in plan:
                if name in steps:
                    steps[name](n, i)

        line = ring_u[0:BUCKETS, 0, 0:512]
        lines = ring_u[0:1, 1, :]
        tab = ring_u[0:BUCKETS, 2, 0:8]
        tabx = ring_u[0:BUCKETS, 3, :].rearrange("p (n k) -> p n k", n=2 * NH)
        line_sb = ring_u[:, 4:8, :].rearrange("p a (n k) -> p (a n) k", k=512)
        s5p = ring_v[:, 0, 0:S_W]
        ang, turns = by(ring_v[:, 1, :], P), by(ring_v[:, 2, :], P)
        bsc = ring_v[:, 3, :]

        block = ctx.enter_context(nc.Block())

        @block.sync
        def _(sp):
            sp.dma_start(cst[:, :], const_in).then_inc(once_in, 16)
            sp.dma_start(x[:, :, :], x_in.rearrange("(b p) d -> p b d", p=P)).then_inc(once_in, 16)
            sp.dma_start(line, bucket_in[0:BUCKETS, :]).then_inc(once_in, 16)
            sp.dma_start(lines, bucket_in[BUCKETS:BUCKETS + 2, :].rearrange("(a b) n -> a (b n)", a=1)).then_inc(once_in, 16)
            sp.dma_start(tab, rel_bias).then_inc(once_in, 16)
            sp.dma_start(s5p, s5_in[0]).then_inc(s5_in_done[0], 16)

            def load_chunk(n, k):
                sp.dma_start(win[:, k % WIN_SLOTS, :], w_in[n // NB, k * P:(k + 1) * P, :]).then_inc(win_in[k % WIN_SLOTS], 16)

            for n in range(PASSES):
                layer, b = n // NB, n % NB
                if n:
                    sp.wait_ge(o_ps, 4 * n)
                sp.dma_start(gain_m[b], gain_mix[layer].partition_broadcast(P)).then_inc(gain_load, 16)
                if n:
                    sp.wait_ge(ids_ready, n)
                if b == 0:
                    sp.dma_start(row[:, :], row_in[layer].partition_broadcast(P)).then_inc(row_load, 16)
                for k in range(WIN_SLOTS):
                    load_chunk(n, k)
                if n == 0:
                    for i in range(DEPTH):
                        sp.wait_ge(s5_tabled, i + 1)
                        sp.dma_start(s5_dram[i], s5t[:, :]).then_inc(s5_out, 16)
                        if i + 1 < DEPTH:
                            sp.dma_start(s5p, s5_in[i + 1]).then_inc(s5_in_done[i + 1], 16)
                    sp.wait_ge(toep_copied, 2 * NH)
                    sp.dma_start(toep.rearrange("n p k -> p n k"), line_sb).then_inc(toep_out, 16)
                    sp.wait_ge(s5_out, 16 * DEPTH)
                if b == 0:
                    sp.dma_start(s5t[:, :], s5_dram[layer]).then_inc(s5_load, 16)
                    sp.dma_start(glu[:, :, :], glu_w[layer].rearrange("(k p) n -> p k n", p=P)).then_inc(glu_load, 16)
                for k in range(WIN_SLOTS, KC):
                    sp.wait_ge(chunk_used, KC * n + k - WIN_SLOTS + 1)
                    load_chunk(n, k)
                if n == 0:
                    sp.wait_ge(toep_out, 16)
                    for i in range(2 * NH):
                        skew = bass.AP(toep.tensor, i * P * 512 + P - 1, [[511, P], [1, SEQ]])
                        sp.dma_start(bias[:, i, :], skew).then_inc(bias_in, 16)
                sp.wait_ge(z_ps, 6 * n + 6)
                sp.dma_start(wout_v, w_out[layer].rearrange("(k p) n -> p k n", p=P)).then_inc(wout_load, 16)
                sp.wait_ge(y_ps, n + 1)
                sp.dma_start(gain_f, gain_ffn[layer].partition_broadcast(P)).then_inc(ffn_load, 16)
                sp.wait_ge(mixed_ready, n + 1)
                sp.dma_start(kts, keys_t[layer]).then_inc(keys_load, 16)
                sp.wait_ge(wo_ps, 2 * n + 2)
                for i in range(4):
                    if i >= 2:
                        sp.wait_ge(qT_ps, 4 * n + i - 1)
                    sp.dma_start(wq_v[i % 2], peer_wq[layer, :, i * 512:(i + 1) * 512].rearrange("(k p) n -> p k n", p=P))\
                        .then_inc(wq_in[i % 2], 16)
            for b in range(NB):
                sp.wait_ge(x_done, PASSES - NB + b + 1)
                sp.dma_start(out[b * P:(b + 1) * P, :], x[:, b, :]).then_inc(out_stored, 16)
            sp.wait_ge(out_stored, 16 * NB)

        @block.scalar
        def _(a):
            step = Order(a, act_step)

            def tables(_, n):
                a.wait_ge(s5_in_done[n], 16)
                if n:
                    a.wait_ge(s5_tabled, n)
                a.activation(small[:, 16:24], s5p[:, S_DT:S_DT + NJ], ACT.Exp).then_inc(s5_exp, 1)
                a.wait_ge(s5_ang, 2 * n + 1)
                a.activation(mags[:, n, :], small[:, 24:32], ACT.Exp).then_inc(s5_exp, 1)
                a.wait_ge(s5_ang, 2 * n + 2)
                if n:
                    a.wait_ge(s5_out, 16 * n)
                a.activation(sinT, ang, ACT.Sin).then_inc(s5_sin, 1)
                a.activation(cosT, ang, ACT.Sin, scale=0.5).then_inc(s5_sin, 1)

            def norm(n, i):
                m, b = 2 * n + i, n % NB
                if i == 0:
                    if n >= NB:
                        a.wait_ge(x_done, n - NB + 1)
                    elif n == 0:
                        a.wait_ge(once_in, 80)
                else:
                    a.wait_ge(x_ready, n + 1)
                a.wait_ge(rows_ps, m) if m else None
                a.activation(h[:, b, :], x[:, b, :], ACT.Square, accum_out=small[:, 0:1]).then_inc(sumsq, 1)
                a.wait_ge(mean_inv, m + 1)
                a.activation(small[:, 8:9], small[:, 4:5], ACT.Sqrt).then_inc(rstd, 1)

            def rows(n, i):
                m = 2 * n + i
                a.wait_ge(rows_ps, m + 1)
                a.activation(hT[:, 4:8, :], by(ps[:, 3 + 2 * i, :], P), ACT.Copy).then_inc(rows_act, 1)
                if i == 0 and n % NB == 0:
                    a.wait_ge(lam_sum, n // NB + 1)
                    a.activation(small[:, 42:44], small[:, 40:42], ACT.Exp).then_inc(lam_exp, 1)

            def project(n, k):
                if k < KC - 1:
                    return
                b = n % NB
                for bank, dst in ((1, zq[:, 512:1024]), (3, zkv[:, b, 384:768]), (5, zkv[:, b, 1152:1536])):
                    a.wait_ge(z_ps, 6 * n + bank + 1)
                    c0, c1 = BANK_CUTS[bank:bank + 2]
                    a.activation(dst, ps[:, 2 + bank, 0:c1 - c0], ACT.Copy).then_inc(z_act, 1)

            def qk_norm(n, i):
                a.wait_ge(f_bias, n + 1)
                step(a.activation(small[:, 56:60], small[:, 48:52], ACT.Abs))
                step(a.activation(small[:, 56:60], small[:, 56:60], ACT.Exp, scale=-1.0))
                a.activation(small[:, 64:68], small[:, 56:60], ACT.Ln, bias=1.0).then_inc(f_ln, 1)
                a.wait_ge(qk_inv, n + 1)
                a.activation(small[:, 128:160], small[:, 96:128], ACT.Sqrt).then_inc(qk_rstd, 1)

            def logits(n, g):
                nk = P * (n % NB + 1)
                lg = ps[:, 2:4, :].rearrange("p c n -> p (c n)")
                a.wait_ge(logit_max, 4 * n + g + 1)
                for i in range(4):
                    a.activation(pbuf[:, i, 0:nk], lg[:, i * nk:(i + 1) * nk], ACT.Exp, bias=small[:, 72 + i:73 + i],
                                 accum_out=small[:, 80 + i:81 + i]).then_inc(p_exp, 1)

            def head_weights(n, g):
                tiles = (4 if g < 2 else 2) * (n % NB + 1)
                a.wait_ge(pT_ps, 4 * n + g + 1)
                for c in range(0, tiles, 4):
                    m = min(4, tiles - c)
                    ins = a.activation(pT[:, c:c + m, :], by(ps[:, 4 + c // 4, 0:m * P], P), ACT.Copy)
                    if c + m == tiles:
                        ins.then_inc(pT_ready, 1)
                    else:
                        step(ins)

            def heads(n, g):
                if g == 3:
                    a.wait_ge(co_inv, n + 1)
                    a.activation(small[:, 196:200], small[:, 192:196], ACT.Sqrt).then_inc(co_rstd, 1)

            def s5_output(n, i):
                a.wait_ge(y_ready, n + 1)
                a.activation(ybuf, ybuf, ACT.Gelu_apprx_tanh).then_inc(g_ready, 1)

            def mix_end(n, i):
                a.wait_ge(glu_sum, n + 1)
                a.activation(sbuf, sbuf, ACT.Sigmoid).then_inc(glu_sig, 1)

            def out_rows(n, i):
                if i == 0:
                    a.wait_ge(mT_ps, n + 1)
                    a.activation(hT[:, 4:8, :], by(ps[:, 5, :], P), ACT.Copy).then_inc(mT_act, 1)

            def query(n, i):
                a.wait_ge(qT_ps, 4 * n + i + 1)
                a.activation(qts[:, 4 * i:4 * i + 4, :], by(ps[:, 6 + i % 2, :], P), ACT.Copy).then_inc(qT_ready, 1)

            def find_ids(n, i):
                a.wait_ge(best_sub, n + 1)
                a.activation(gates[:, n % NB, :], gates[:, n % NB, :], ACT.Exp).then_inc(gate_exp, 1)

            def take_dots(n, i):
                m, g = HALVES * n + i, i % 2
                a.wait_ge(dots_done, RING + RING_G * (m + 1))
                if m >= 2:
                    a.wait_ge(weights_done, m - 1)
                a.activation(acts[:, g * RING_G:(g + 1) * RING_G], dots[:, g * RING_G:(g + 1) * RING_G],
                             ACT.Gelu_apprx_tanh).then_inc(gelu_done, 1)

            def add_rows(n, i):
                m, g = HALVES * n + i, i % 2
                a.wait_ge(weights_done, m + 1)
                if m >= 2:
                    a.wait_ge(v_used, RING + RING_G * (m - 1))
                for s in range(g * RING_G, (g + 1) * RING_G):
                    a.activation(diag[:, s, :], ident, ACT.Copy, scale=weights[:, s:s + 1]).then_inc(diag_ready, 1)

            walk({"tables": tables, "norm": norm, "rows": rows, "project": project, "qk norm": qk_norm, "logits": logits,
                  "weights": head_weights, "heads": heads, "s5 out": s5_output, "mixed": mix_end, "out": out_rows,
                  "query": query, "ids": find_ids, "dots": take_dots, "rows of v": add_rows})

        @block.vector
        def _(v):
            step = Order(v, dve_step)

            v.memset(zero[:, :], 0.0).then_inc(zero_set, 1)
            v.sem_inc(dots_done, RING)
            v.wait_ge(once_in, 80)
            v.tensor_copy(tabx, bc(tab, 2, P)).then_inc(toep_ready, 1)

            def reduce_angle(t, k):
                step(v.tensor_scalar(k, t, 1.0 / TWO_PI, ROUND, ALU.mult, ALU.add))
                step(v.tensor_scalar(k, k, ROUND, None, ALU.subtract))
                for part in (PI_A, PI_B, PI_C):
                    step(v.scalar_tensor_tensor(out=t, in0=k, scalar=-part, in1=t, op0=ALU.mult, op1=ALU.add))

            def tables(_, n):
                ar, ai, mag = s5p[:, S_AR:S_AR + NJ], s5p[:, S_AI:S_AI + NJ], mags[:, n, :]
                th, kk = small[:, 208:216], small[:, 216:224]
                v.wait_ge(s5_in_done[n], 16)
                v.wait_ge(s5_exp, 2 * n + 1)
                v.tensor_tensor(small[:, 24:32], small[:, 16:24], ar, ALU.mult).then_inc(s5_ang, 1)
                step(v.tensor_tensor(th, small[:, 16:24], ai, ALU.mult))
                reduce_angle(th, kk)
                step(v.tensor_tensor(ang, bc(th, 2, P), bc(cst[:, C_TAU:C_TAU + P], 1, NJ), ALU.mult))
                reduce_angle(ang, turns)
                v.tensor_scalar(ang, ang, 3.1415925, -3.1415925, ALU.min, ALU.max).then_inc(s5_ang, 1)
                v.wait_ge(s5_sin, 2 * n + 2)
                step(v.tensor_tensor(cosT, cosT, cosT, ALU.mult))
                step(v.tensor_scalar(cosT, cosT, -2.0, 1.0, ALU.mult, ALU.add))
                v.wait_ge(s5_exp, 2 * n + 2)
                nr, ni, den, t0, t1, cr, ci = [small[:, 288 + 8 * i:296 + 8 * i] for i in range(7)]
                step(v.tensor_tensor(nr, mag, cosT[:, :, 0], ALU.mult))
                step(v.tensor_scalar(nr, nr, 1.0, None, ALU.subtract))
                step(v.tensor_tensor(ni, mag, sinT[:, :, 0], ALU.mult))
                step(v.tensor_tensor(t0, ar, ar, ALU.mult))
                step(v.tensor_tensor(t1, ai, ai, ALU.mult))
                step(v.tensor_tensor(den, t0, t1, ALU.add))
                step(v.reciprocal(den, den))
                step(v.tensor_tensor(t0, nr, ar, ALU.mult))
                step(v.tensor_tensor(t1, ni, ai, ALU.mult))
                step(v.tensor_tensor(cr, t0, t1, ALU.add))
                step(v.tensor_tensor(cr, cr, den, ALU.mult))
                step(v.tensor_tensor(t0, ni, ar, ALU.mult))
                step(v.tensor_tensor(t1, nr, ai, ALU.mult))
                step(v.tensor_tensor(ci, t0, t1, ALU.subtract))
                step(v.tensor_tensor(ci, ci, den, ALU.mult))
                br, bi = by(s5p[:, S_BR:S_BR + P], S5_C), by(s5p[:, S_BI:S_BI + P], S5_C)
                b0, b1, b2 = [by(bsc[:, P * i:P * (i + 1)], S5_C) for i in range(3)]
                bx = bsc[:, 512:1024].rearrange("p (r j g c) -> p r j g c", r=2, j=NJ, g=2)
                step(v.tensor_tensor(b0, br, bc(cr, 2, S5_C), ALU.mult))
                step(v.tensor_tensor(b1, bi, bc(ci, 2, S5_C), ALU.mult))
                step(v.tensor_tensor(b2, b0, b1, ALU.subtract))
                for g in range(2):
                    step(v.tensor_scalar(bx[:, 0, :, g, :], b2, hm2[:, g:g + 1], None, ALU.mult))
                step(v.tensor_tensor(b0, bi, bc(cr, 2, S5_C), ALU.mult))
                step(v.tensor_tensor(b1, br, bc(ci, 2, S5_C), ALU.mult))
                step(v.tensor_tensor(b2, b0, b1, ALU.add))
                step(v.tensor_scalar(bx[:, 1, :, 0, :], b2, hm2[:, 0:1], None, ALU.mult))
                v.tensor_scalar(bx[:, 1, :, 1, :], b2, hm2[:, 1:2], None, ALU.mult).then_inc(s5_bx, 1)
                step(v.tensor_copy(cR, s5p[:, S_CR:S_CR + GW]))
                step(v.tensor_scalar(cI, s5p[:, S_CI:S_CI + GW], -1.0, None, ALU.mult))
                v.wait_ge(s5_bt_ps, n + 1)
                v.tensor_copy(s5t[:, 2048:2560], ps[:, 1, :]).then_inc(s5_tabled, 1)

            def norm(n, i):
                m, b = 2 * n + i, n % NB
                v.wait_ge(sumsq, m + 1)
                step(v.tensor_scalar(small[:, 4:5], small[:, 0:1], 1.0 / D, EPS, ALU.mult, ALU.add))
                v.reciprocal(small[:, 4:5], small[:, 4:5]).then_inc(mean_inv, 1)
                v.wait_ge(rstd, m + 1)
                v.wait_ge((gain_load, ffn_load)[i], 16 * (n + 1))
                v.scalar_tensor_tensor(out=h[:, b, :], in0=x[:, b, :], scalar=small[:, 8:9], in1=(gain_m[b], gain_f)[i],
                                       op0=ALU.mult, op1=ALU.mult).then_inc(h_ready, 1)
                v.wait_ge(h_ready, m + 1)

            def rows(n, i):
                v.wait_ge(rows_ps, 2 * n + i + 1)
                v.tensor_copy(hT[:, 0:4, :], by(ps[:, 2 + 2 * i, :], P)).then_inc(rows_dve, 1)
                if i == 0 and n % NB == 0:
                    layer = n // NB
                    v.wait_ge(row_load, 16 * (layer + 1))
                    lam = row[:, R_LAM:R_LAM + 128].rearrange("p (a b d) -> p a b d", a=2, b=2)
                    prod = small[:, 224:288].rearrange("p (a d) -> p a d", a=2)
                    step(v.tensor_tensor(prod, lam[:, :, 0, :], lam[:, :, 1, :], ALU.mult))
                    v.reduce_sum(small[:, 40:42], prod, AX).then_inc(lam_sum, 1)
                    step(v.tensor_scalar(row[:, R_FQ:R_FQ + HD], row[:, R_FQ:R_FQ + HD], HD ** -0.5, None, ALU.mult))
                    step(v.tensor_scalar(row[:, R_DQ:R_DQ + HD], row[:, R_DQ:R_DQ + HD], HD ** -0.5, None, ALU.mult))
                    step(v.tensor_scalar(row[:, R_CQ:R_CQ + DH], row[:, R_CQ:R_CQ + DH], DH ** -0.5, None, ALU.mult))
                    step(v.tensor_scalar(row[:, R_CO:R_CO + HD], row[:, R_CO:R_CO + HD], row[:, R_LC + 1:R_LC + 2], None, ALU.mult))
                    v.wait_ge(lam_exp, layer + 1)
                    step(v.tensor_tensor(nlam, small[:, 43:44], small[:, 42:43], ALU.subtract))
                    step(v.tensor_tensor(nlam, nlam, row[:, R_LC:R_LC + 1], ALU.subtract))

            def lines_out(n, i):
                for j in range(2 * NH):
                    v.wait_ge(toep_ps, j + 1)
                    v.tensor_copy(line_sb[:, j, :], ps[:, j % 2, :]).then_inc(toep_copied, 1)

            nlam = small[:, 44:45]

            def project(n, k):
                if k < KC - 1:
                    return
                b = n % NB
                v.wait_ge(z_ps, 6 * n + 1)
                v.tensor_copy(zq[:, 0:512], ps[:, 2, :]).then_inc(z_dve, 1)
                v.wait_ge(z_ps, 6 * n + 3)
                v.tensor_copy(zq[:, FF:ZQ_W], ps[:, 4, 0:NH]).then_inc(z_dve, 1)
                v.tensor_copy(zkv[:, b, 0:384], ps[:, 4, NH:388]).then_inc(z_dve, 1)
                v.wait_ge(z_ps, 6 * n + 5)
                v.tensor_copy(zkv[:, b, 768:1152], ps[:, 6, 0:384]).then_inc(z_dve, 1)
                v.wait_ge(z_dve, 4 * n + 4)
                v.wait_ge(z_act, 3 * n + 3)

            def qk_norm(n, i):
                b, layer = n % NB, n // NB
                f = small[:, 48:52]
                v.tensor_tensor(f, zq[:, FF:FF + NH], row[:, R_BF:R_BF + NH], ALU.add).then_inc(f_bias, 1)
                groups = ((0, HD, R_FQ), (1, HD, R_DQ), (2, DH, R_CQ))
                step(v.tensor_tensor(sq[:, 0:768], zq[:, 0:768], zq[:, 0:768], ALU.mult))
                step(v.tensor_tensor(sq[:, 768:1536], zkv[:, b, KEYS:KEYS + 768], zkv[:, b, KEYS:KEYS + 768], ALU.mult))
                s2 = sq.rearrange("p (a n) -> p a n", a=2)
                st = small[:, 96:128].rearrange("p (a n) -> p a n", a=2)
                step(v.reduce_sum(st[:, :, 0:8], s2[:, :, 0:512].rearrange("p a (n d) -> p a n d", d=HD), AX))
                step(v.reduce_sum(st[:, :, 8:16], s2[:, :, 512:768].rearrange("p a (n d) -> p a n d", d=DH), AX))
                step(v.tensor_scalar(st[:, :, 0:8], st[:, :, 0:8], 1.0 / HD, EPS, ALU.mult, ALU.add))
                step(v.tensor_scalar(st[:, :, 8:16], st[:, :, 8:16], 1.0 / DH, EPS, ALU.mult, ALU.add))
                v.reciprocal(small[:, 96:128], small[:, 96:128]).then_inc(qk_inv, 1)
                v.wait_ge(f_ln, n + 1)
                ls, nls = small[:, 352 + NH * b:356 + NH * b], small[:, 360 + NH * b:364 + NH * b]
                step(v.tensor_scalar(nls, f, 0.0, None, ALU.min))
                step(v.tensor_tensor(ls, nls, small[:, 64:68], ALU.subtract))
                v.tensor_scalar(nls, ls, -1.0, None, ALU.mult).then_inc(f_ready, 1)
                v.wait_ge(qk_rstd, n + 1)
                rs = small[:, 128:160].rearrange("p (a n) -> p a n", a=2)
                for g, w, r0 in groups:
                    heads = GW // w
                    for a_, src in enumerate((zq[:, GW * g:GW * (g + 1)], zkv[:, b, KEYS + GW * g:KEYS + GW * (g + 1)])):
                        zz = by(src, w)
                        r = rs[:, a_, NH * g:NH * g + heads]
                        gg = row[:, r0 + a_ * w:r0 + (a_ + 1) * w]
                        step(v.tensor_tensor(zz, zz, bc(r, 2, w), ALU.mult))
                        ins = v.tensor_tensor(zz, zz, bc(gg, 1, heads), ALU.mult)
                        if a_:
                            ins.then_inc(qk_ready, 1)
                            v.wait_ge(qk_ready, 3 * n + g + 1)
                        else:
                            step(ins)

            def s5_inputs(n, i):
                v.wait_ge(uT_ps, n + 1)
                v.tensor_tensor(T[:, 0:1024].rearrange("p (h j t) -> p h j t", h=2, j=4), bc(by(ps[:, 2, 0:256], P), 2, 4),
                                bc(bc(hm4, 1, 2), 3, P), ALU.mult).then_inc(um_ready, 1)

            def keys(n, g):
                b = n % NB
                v.wait_ge(keys_ps, 3 * n + g + 1)
                tq = by(ps[:, 7, 0:256], P)
                if g < 2:
                    step(v.tensor_tensor(qm[:, 0:512].rearrange("p (i c t) -> p i c t", i=2, c=2), bc(tq, 2, 2),
                                         bc(bc(hm2, 1, 2), 3, P), ALU.mult))
                else:
                    step(v.tensor_tensor(qm.rearrange("p (i c t) -> p i c t", i=2, c=4), bc(tq, 2, 4),
                                         bc(bc(hm4, 1, 2), 3, P), ALU.mult))
                nk = P * (b + 1)
                v.tensor_copy(kT[:, :, 0:nk], ps[:, 6, 0:2 * nk].rearrange("p (i k) -> p i k", k=nk)).then_inc(keys_ready, 1)

            def s5_turn_back(n, i):
                v.wait_ge(bu_ps, n + 1)
                re, im = (ps[:, 4 + r:7 + r:2, :].rearrange("p h (j t) -> p h j t", t=P) for r in range(2))
                hv = lambda t: t.rearrange("p (h j) t -> p h j t", h=2)
                step(v.tensor_tensor(hv(s5a), hv(cosT), re, ALU.mult))
                step(v.tensor_tensor(hv(s5c), hv(sinT), im, ALU.mult))
                step(v.tensor_tensor(hv(s5b), hv(cosT), im, ALU.mult))
                v.tensor_tensor(hv(s5d), hv(sinT), re, ALU.mult).then_inc(bu_used, 1)
                v.wait_ge(bu_used, n + 1)
                step(v.tensor_tensor(s5a, s5a, s5c, ALU.add))
                step(v.tensor_tensor(s5b, s5b, s5d, ALU.subtract))

            carry = small[:, 384:400]

            def s5_scan(n, i):
                for j in range(NJ):
                    for c, buf in enumerate((s5a, s5b)):
                        init = 0.0 if n % NB == 0 else carry[:, c * NJ + j:c * NJ + j + 1]
                        step(v.tensor_tensor_scan(buf[:, j, :], rep(mags[:, n // NB, j:j + 1], P), buf[:, j, :], init,
                                                  ALU.mult, ALU.add))

            def s5_turn_on(n, i):
                step(v.tensor_tensor(s5c, cosT, s5a, ALU.mult))
                step(v.tensor_tensor(s5d, sinT, s5b, ALU.mult))
                step(v.tensor_tensor(s5c, s5c, s5d, ALU.subtract))
                step(v.tensor_tensor(s5b, cosT, s5b, ALU.mult))
                step(v.tensor_tensor(s5a, sinT, s5a, ALU.mult))
                v.tensor_tensor(s5b, s5a, s5b, ALU.add).then_inc(s5_state, 1)
                if n % NB == 0:
                    v.wait_ge(s5_state, n + 1)
                    step(v.tensor_copy(carry[:, 0:NJ], s5c[:, :, P - 1]))
                    step(v.tensor_copy(carry[:, NJ:2 * NJ], s5b[:, :, P - 1]))

            def logits(n, g):
                nk = P * (n % NB + 1)
                v.wait_ge(logit_ps, 4 * n + g + 1)
                lg = by(ps[:, 2:4, :].rearrange("p c n -> p (c n)")[:, 0:4 * nk], nk)
                step(v.reduce_max(small[:, 76:80], lg, AX))
                v.tensor_scalar(small[:, 72:76], small[:, 76:80], -1.0, None, ALU.mult).then_inc(logit_max, 1)

            def head_weights(n, g):
                nk = P * (n % NB + 1)
                inv = small[:, 84 + 4 * (g % 2):88 + 4 * (g % 2)]
                v.wait_ge(p_exp, 16 * n + 4 * g + 4)
                if g < 2:
                    v.reciprocal(inv, small[:, 80:84]).then_inc(p_ready, 1)
                    v.wait_ge(p_ready, 4 * n + g + 1)
                    return
                step(v.reciprocal(inv, small[:, 80:84]))
                step(v.tensor_scalar(small[:, 92:96], inv, nlam, None, ALU.mult))
                for i in range(2):
                    step(v.tensor_scalar(pbuf[:, 2 * i + 1, 0:nk], pbuf[:, 2 * i + 1, 0:nk],
                                         small[:, 93 + 2 * i:94 + 2 * i], None, ALU.mult))
                for i in range(2):
                    ins = v.scalar_tensor_tensor(out=pbuf[:, 2 * i, 0:nk], in0=pbuf[:, 2 * i, 0:nk], scalar=inv[:, 2 * i:2 * i + 1],
                                                 in1=pbuf[:, 2 * i + 1, 0:nk], op0=ALU.mult, op1=ALU.add)
                    if i:
                        ins.then_inc(p_ready, 1)
                    else:
                        step(ins)

            def heads(n, g):
                b = n % NB
                v.wait_ge(o_ps, 4 * n + g + 1)
                if g < 2:
                    v.tensor_tensor(by(mixed[:, b, g * GW:(g + 1) * GW], HD), by(ps[:, 7, 256:512], HD),
                                    bc(small[:, 84 + 4 * g:88 + 4 * g], 2, HD), ALU.mult).then_inc(o_used, 1)
                else:
                    v.tensor_copy(mixed[:, b, 2 * GW + (g - 2) * P:2 * GW + (g - 1) * P], ps[:, 7, 256:384]).then_inc(o_used, 1)
                v.wait_ge(o_used, 4 * n + g + 1)
                if g == 3:
                    co = mixed[:, b, 2 * GW:3 * GW]
                    step(v.tensor_tensor(T[:, 2048:2304], co, co, ALU.mult))
                    step(v.reduce_sum(small[:, 192:196], by(T[:, 2048:2304], HD), AX))
                    step(v.tensor_scalar(small[:, 192:196], small[:, 192:196], 1.0 / HD, EPS, ALU.mult, ALU.add))
                    v.reciprocal(small[:, 192:196], small[:, 192:196]).then_inc(co_inv, 1)
                    v.wait_ge(co_rstd, n + 1)
                    co = by(co, HD)
                    step(v.tensor_tensor(co, co, bc(small[:, 196:200], 2, HD), ALU.mult))
                    step(v.tensor_tensor(co, co, bc(row[:, R_CO:R_CO + HD], 1, NH), ALU.mult))

            def s5_output(n, i):
                step(v.tensor_tensor(T[:, 2048:2304], zq[:, SU:SU + GW], row[:, R_SD:R_SD + GW], ALU.mult))
                v.wait_ge(y_ps, n + 1)
                v.tensor_tensor(ybuf, T[:, 2048:2304], ps[:, 6, 0:256], ALU.add).then_inc(y_ready, 1)
                v.wait_ge(y_ready, n + 1)

            def s5_gate(n, i):
                v.wait_ge(gT_ps, n + 1)
                v.tensor_copy(gT, ps[:, 6, 0:256]).then_inc(gT_ready, 1)

            def mix_end(n, i):
                v.wait_ge(glu_ps, n + 1)
                v.tensor_tensor(sbuf, ps[:, 6, 0:256], row[:, R_GB:R_GB + GW], ALU.add).then_inc(glu_sum, 1)
                v.wait_ge(glu_sig, n + 1)
                v.tensor_tensor(mixed[:, n % NB, 3 * GW:4 * GW], ybuf, sbuf, ALU.mult).then_inc(mixed_ready, 1)

            def out_rows(n, i):
                if i == 0:
                    v.wait_ge(mT_ps, n + 1)
                    v.tensor_copy(hT[:, 0:4, :], by(ps[:, 4, :], P)).then_inc(mT_dve, 1)
                else:
                    b = n % NB
                    v.wait_ge(wo_ps, 2 * n + 2)
                    v.tensor_tensor(x[:, b, :], x[:, b, :], ps[:, 2:4, :].rearrange("p c n -> p (c n)"), ALU.add).then_inc(x_ready, 1)

            def score(n, q):
                v.wait_ge(sc_ps, 4 * n + q + 1)
                for i in range(4):
                    k = 4 * q + i
                    sc = ps[:, 2 + q, i * NK:(i + 1) * NK]
                    step(v.max(v16[:, k, 0:8], sc))
                    step(v.max_index(i16[:, k, 0:8], v16[:, k, 0:8], sc))
                    step(v.match_replace(sc2, v16[:, k, 0:8], sc, NEG))
                    step(v.max(v16[:, k, 8:16], sc2))
                    ins = v.max_index(i16[:, k, 8:16], v16[:, k, 8:16], sc2)
                    if i == 3:
                        ins.then_inc(sc_used, 1)
                        v.wait_ge(sc_used, 4 * n + q + 1)
                    else:
                        step(ins)

            def pairs(n, q):
                if q == 0:
                    step(v.tensor_copy(i16f, i16))
                for k in range(4 * q, 4 * q + 4):
                    step(v.tensor_tensor(by(cand, TOPK), bc(v16[:, 2 * k, :], 2, TOPK), bc(v16[:, 2 * k + 1, :], 1, TOPK), ALU.add))
                    step(v.max(best[:, k, 0:8], cand))
                    step(v.max_index(pos[:, k, 0:8], best[:, k, 0:8], cand))
                    step(v.match_replace(cand2, best[:, k, 0:8], cand, NEG))
                    step(v.max(best[:, k, 8:16], cand2))
                    step(v.max_index(pos[:, k, 8:16], best[:, k, 8:16], cand2))

            def find_ids(n, i):
                b = n % NB
                g3 = by(gates[:, b, :], TOPK)
                v.tensor_tensor(g3, best, bc(best[:, :, 0], 2, TOPK), ALU.subtract).then_inc(best_sub, 1)
                pos_f = pos.rearrange("p n k -> p (n k)")
                i4 = i16f.rearrange("p (n s) k -> p n s k", s=2)
                for s in range(2):
                    if s == 0:
                        step(v.tensor_single_scalar(posd, pos_f, 4, op=ALU.logical_shift_right))
                    else:
                        step(v.tensor_single_scalar(posd, pos_f, TOPK - 1, op=ALU.bitwise_and))
                    step(v.tensor_copy(posf, posd))
                    step(v.tensor_tensor(hit.rearrange("p n k a -> p (n k) a"), bc(posf, 2, TOPK),
                                         bc(cst[:, C_IOTA:C_IOTA + TOPK], 1, SLOTS), ALU.is_equal))
                    step(v.tensor_tensor(hit, hit, bc(i4[:, :, s, :], 2, TOPK), ALU.mult))
                    step(v.reduce_sum(idf[s], hit.rearrange("p n k a -> p (n k) a"), AX))
                step(v.scalar_tensor_tensor(out=idf[0], in0=idf[0], scalar=float(NK), in1=idf[1], op0=ALU.mult, op1=ALU.add))
                step(v.tensor_scalar(idf[0], idf[0], row[:, R_LC + 2:R_LC + 3], None, ALU.add))
                v.tensor_copy(ids[:, b, :], idf[0]).then_inc(ids_ready, 1)
                v.wait_ge(gate_exp, n + 1)
                step(v.reduce_sum(small[:, 400:408], g3, AX))
                step(v.reciprocal(small[:, 400:408], small[:, 400:408]))
                v.tensor_tensor(g3, g3, bc(small[:, 400:408], 2, TOPK), ALU.mult).then_inc(gates_ready, 1)
                v.wait_ge(gates_ready, n + 1)

            def take_dots(n, i):
                m, g, b = HALVES * n + i, i % 2, n % NB
                for j in range(RING_G):
                    s = g * RING_G + j
                    v.wait_ge(u_in[s], 16 * (m // 2 + 1))
                    v.wait_ge(dots_done, RING + RING_G * m + j)
                    if m >= 2 and j == 0:
                        v.wait_ge(gelu_done, m - 1)
                    v.tensor_tensor_reduce(junk[:, :], ring_u[:, s, :], h[:, b, :], 1.0, 0.0, ALU.mult, ALU.add,
                                           dots[:, s:s + 1]).then_inc(dots_done, 1)

            def add_rows(n, i):
                m, g, b = HALVES * n + i, i % 2, n % NB
                ss = slice(g * RING_G, (g + 1) * RING_G)
                v.wait_ge(gelu_done, m + 1)
                if m >= 2:
                    v.wait_ge(diag_ready, RING_G * (m - 1))
                v.tensor_tensor(weights[:, ss], acts[:, ss], gates[:, b, i * RING_G:(i + 1) * RING_G], ALU.mult)\
                    .then_inc(weights_done, 1)

            def gathered(n, i):
                v.wait_ge(acc_ps, n + 1)
                v.tensor_copy(x[:, n % NB, :], ps[:, 0:2, :].rearrange("p c n -> p (c n)")).then_inc(x_done, 1)

            walk({"tables": tables, "lines": lines_out, "norm": norm, "rows": rows, "project": project, "qk norm": qk_norm, "s5 in": s5_inputs, "keys": keys,
                  "s5 turn back": s5_turn_back, "s5 scan": s5_scan, "s5 turn on": s5_turn_on, "logits": logits,
                  "weights": head_weights, "heads": heads, "s5 out": s5_output, "s5 gate": s5_gate, "mixed": mix_end,
                  "out": out_rows, "score": score, "pairs": pairs, "ids": find_ids, "dots": take_dots,
                  "rows of v": add_rows, "gathered": gathered})

        @block.tensor
        def _(pe):
            def turn_rows(src, bank, done):
                for k in range(KC):
                    mm = pe.transpose(ps[:, bank + k // 4, (k % 4) * P:(k % 4 + 1) * P], src[:, k * P:(k + 1) * P], ident)
                mm.then_inc(done, 1)

            pe.wait_ge(once_in, 80)
            pe.sem_inc(v_used, RING)

            def rows(n, i):
                m, b = 2 * n + i, n % NB
                pe.wait_ge(h_ready, m + 1)
                if i == 0 and n:
                    pe.wait_ge(sc_used, 4 * n)
                if i == 1:
                    pe.wait_ge(mT_act, n + 1)
                turn_rows(h[:, b, :], 2 + 2 * i, rows_ps)

            def tables(_, n):
                pe.wait_ge(s5_bx, n + 1)
                for k in range(4):
                    mm = pe.transpose(ps[:, 1, k * P:(k + 1) * P], bsc[:, 512 + k * P:512 + (k + 1) * P], ident)
                mm.then_inc(s5_bt_ps, 1)

            def lines_out(n, i):
                pe.wait_ge(toep_ready, 1)
                pe.wait_ge(s5_tabled, DEPTH)
                for j in range(2 * NH):
                    if j >= 2:
                        pe.wait_ge(toep_copied, j - 1)
                    mask = lines[:, 0:512] if j < NH else lines[:, 512:1024]
                    pe.matmul(ps[:, j % 2, :], tabx[:, j, :], line, start=True, stop=False)
                    pe.matmul(ps[:, j % 2, :], ones[0:1, :], mask, start=False, stop=True).then_inc(toep_ps, 1)

            def project(n, k):
                if k == 0:
                    pe.wait_ge(rows_dve, 2 * n + 1)
                    pe.wait_ge(rows_act, 2 * n + 1)
                    if n:
                        pe.wait_ge(qT_ready, 4 * n)
                slot = k % WIN_SLOTS
                pe.wait_ge(win_in[slot], 16 * (n * (1 + (slot < KC - WIN_SLOTS)) + k // WIN_SLOTS + 1))
                for i in range(6):
                    c0, c1 = BANK_CUTS[i:i + 2]
                    mm = pe.matmul(ps[:, 2 + i, 0:c1 - c0], hT[:, k, :], win[:, slot, c0:c1], start=(k == 0), stop=(k == KC - 1))
                    if k == KC - 1:
                        mm.then_inc(z_ps, 1)
                if k < KC - 1:
                    mm.then_inc(chunk_used, 1)
                else:
                    pe.sem_inc(chunk_used, 1)

            def s5_inputs(n, i):
                pe.wait_ge(z_act, 3 * n + 3)
                pe.wait_ge(z_dve, 4 * n + 4)
                for j in range(2):
                    mm = pe.transpose(ps[:, 2, j * P:(j + 1) * P], zq[:, SU + j * P:SU + (j + 1) * P], ident)
                mm.then_inc(uT_ps, 1)

            def bu(n, i):
                pe.wait_ge(um_ready, n + 1)
                pe.wait_ge(s5_load, 16 * (n // NB + 1))
                for hf in range(2):
                    for r in range(2):
                        for j in range(4):
                            mm = pe.matmul(ps[:, 4 + 2 * hf + r, j * P:(j + 1) * P], bT[:, 2 * r + hf, :], um[:, 4 * hf + j, :],
                                           start=True, stop=True)
                mm.then_inc(bu_ps, 1)

            def keys(n, g):
                b = n % NB
                pe.wait_ge(qk_ready, 3 * n + g + 1)
                if g == 0:
                    pe.wait_ge(bu_used, n + 1)
                else:
                    pe.wait_ge(keys_ready, 3 * n + g)
                for i in range(2):
                    for s in range(b + 1):
                        c0 = KEYS + GW * g + i * P
                        t = i * (b + 1) + s
                        pe.transpose(ps[:, 6, t * P:(t + 1) * P], zkv[:, s, c0:c0 + P], ident)
                for i in range(2):
                    mm = pe.transpose(ps[:, 7, i * P:(i + 1) * P], zq[:, GW * g + i * P:GW * g + (i + 1) * P], ident)
                mm.then_inc(keys_ps, 1)

            def logits(n, g):
                b = n % NB
                nk = P * (b + 1)
                pe.wait_ge(keys_ready, 3 * n + min(g, 2) + 1)
                if g == 0:
                    pe.wait_ge(f_ready, n + 1)
                    pe.wait_ge(bias_in, 16 * 2 * NH)
                else:
                    pe.wait_ge(p_exp, 16 * n + 4 * g)
                lg = ps[:, 2:4, :].rearrange("p c n -> p (c n)")
                for i in range(4):
                    dst = lg[:, i * nk:(i + 1) * nk]
                    own = lg[:, i * nk + b * P:(i + 1) * nk]
                    if g < 2:
                        q, k = qm[:, i * P:(i + 1) * P], kT[:, i // 2, 0:nk]
                    else:
                        q, k = qm[:, (g - 2) * 512 + i * P:(g - 2) * 512 + (i + 1) * P], kT[:, g - 2, 0:nk]
                    pe.matmul(dst, q, k, start=True, stop=False)
                    if g == 0:
                        for s in range(b + 1):
                            ls = small[:, 352 + s * NH + i:353 + s * NH + i]
                            nls = small[:, 360 + s * NH + i:361 + s * NH + i]
                            pe.matmul(dst, tri if s == b else ones, rep(ls, nk), start=False, stop=False)
                            pe.matmul(own if s == b else dst, rep(nls, P), tri if s == b else triones, start=False, stop=False)
                        mm = pe.matmul(own, ident, causal, start=False, stop=True)
                    else:
                        j = i if g == 1 else NH + 2 * (g - 2) + i // 2
                        mm = pe.matmul(dst, ident, bias[:, j, SEQ - nk:SEQ], start=False, stop=True)
                mm.then_inc(logit_ps, 1)

            def head_weights(n, g):
                b = n % NB
                pe.wait_ge(p_ready, 4 * n + g + 1)
                if g == 0:
                    pe.wait_ge(bu_used, n + 1)
                else:
                    pe.wait_ge(pT_ready, 4 * n + g)
                t = 0
                for i in range(4 if g < 2 else 2):
                    for s in range(b + 1):
                        src = pbuf[:, i if g < 2 else 2 * i, s * P:(s + 1) * P]
                        mm = pe.transpose(ps[:, 4 + t // 4, (t % 4) * P:(t % 4 + 1) * P], src, ident)
                        t += 1
                mm.then_inc(pT_ps, 1)

            def heads(n, g):
                b = n % NB
                pe.wait_ge(pT_ready, 4 * n + g + 1)
                pe.wait_ge(keys_ready, 3 * n + min(g + 2, 3))
                if g:
                    pe.wait_ge(o_used, 4 * n + g)
                v0 = VALS + (0, GW, 2 * GW, 2 * GW + P)[g]
                for i in range(4 if g < 2 else 2):
                    for s in range(b + 1):
                        mm = pe.matmul(ps[:, 7, 256 + i * HD:256 + (i + 1) * HD], pT[:, i * (b + 1) + s, :],
                                       zkv[:, s, v0 + i * HD:v0 + (i + 1) * HD], start=(s == 0), stop=(s == b))
                mm.then_inc(o_ps, 1)

            def s5_output(n, i):
                pe.wait_ge(s5_state, n + 1)
                for j in range(NJ):
                    y = ps[:, 6, j * 32:(j + 1) * 32]
                    pe.matmul(y, s5c[:, j, :], cR[:, 32 * j:32 * (j + 1)], start=True, stop=False)
                    mm = pe.matmul(y, s5b[:, j, :], cI[:, 32 * j:32 * (j + 1)], start=False, stop=True)
                mm.then_inc(y_ps, 1)

            def s5_gate(n, i):
                pe.wait_ge(g_ready, n + 1)
                for j in range(2):
                    mm = pe.transpose(ps[:, 6, j * P:(j + 1) * P], ybuf[:, j * P:(j + 1) * P], ident)
                mm.then_inc(gT_ps, 1)

            def mix_end(n, i):
                pe.wait_ge(gT_ready, n + 1)
                pe.wait_ge(glu_load, 16 * (n // NB + 1))
                for j in range(2):
                    mm = pe.matmul(ps[:, 6, 0:256], gT[:, j * P:(j + 1) * P], glu[:, j, :], start=(j == 0), stop=(j == 1))
                mm.then_inc(glu_ps, 1)

            def out_rows(n, c):
                if c == 0:
                    pe.wait_ge(mixed_ready, n + 1)
                    turn_rows(mixed[:, n % NB, :], 4, mT_ps)
                    pe.wait_ge(mT_dve, n + 1)
                    pe.wait_ge(mT_act, n + 1)
                    pe.wait_ge(wout_load, 16 * (n + 1))
                for k in range(KC):
                    mm = pe.matmul(ps[:, 2 + c, :], hT[:, k, :], wout_v[:, k, c * 512:(c + 1) * 512], start=(k == 0), stop=(k == KC - 1))
                mm.then_inc(wo_ps, 1)

            def query(n, q):
                if q == 0:
                    pe.wait_ge(rows_dve, 2 * n + 2)
                    pe.wait_ge(rows_act, 2 * n + 2)
                elif q >= 2:
                    pe.wait_ge(qT_ready, 4 * n + q - 1)
                pe.wait_ge(wq_in[q % 2], 16 * (2 * n + q // 2 + 1))
                for i in range(4):
                    for k in range(KC):
                        mm = pe.matmul(ps[:, 6 + q % 2, i * P:(i + 1) * P], wq_v[q % 2][:, k, i * P:(i + 1) * P], hT[:, k, :],
                                       start=(k == 0), stop=(k == KC - 1))
                mm.then_inc(qT_ps, 1)

            def score(n, q):
                if q == 0:
                    pe.wait_ge(keys_load, 16 * (n + 1))
                    pe.wait_ge(x_ready, n + 1)
                pe.wait_ge(qT_ready, 4 * n + q + 1)
                for i in range(4):
                    mm = pe.matmul(ps[:, 2 + q, i * NK:(i + 1) * NK], qts[:, 4 * q + i, :], kts[:, 4 * q + i, :], start=True, stop=True)
                mm.then_inc(sc_ps, 1)

            def add_rows(n, i):
                m, g, b = HALVES * n + i, i % 2, n % NB
                if i == 0:
                    if n:
                        pe.wait_ge(x_done, n)
                    else:
                        pe.wait_ge(toep_copied, 2 * NH)
                        pe.wait_ge(zero_set, 1)
                    for c in range(2):
                        pe.matmul(ps[:, c, :], zero[:, :], x[:, b, c * 512:(c + 1) * 512], start=True, stop=False,
                                  skip_group_check=True)
                for j in range(RING_G):
                    s = g * RING_G + j
                    pe.wait_ge(v_in[s], 16 * (m // 2 + 1))
                    pe.wait_ge(diag_ready, RING_G * m + j + 1)
                    for c in range(2):
                        mm = pe.matmul(ps[:, c, :], diag[:, s, :], ring_v[:, s, c * 512:(c + 1) * 512], start=False, stop=False,
                                       skip_group_check=True)
                    mm.then_inc(v_used, 1)
                if i == HALVES - 1:
                    for c in range(2):
                        mm = pe.matmul(ps[:, c, :], ident, x[:, b, c * 512:(c + 1) * 512], start=False, stop=True,
                                       skip_group_check=True)
                    mm.then_inc(acc_ps, 1)

            walk({"tables": tables, "lines": lines_out, "rows": rows, "project": project, "s5 in": s5_inputs, "bu": bu, "keys": keys, "logits": logits,
                  "weights": head_weights, "heads": heads, "s5 out": s5_output, "s5 gate": s5_gate, "mixed": mix_end,
                  "out": out_rows, "query": query, "score": score, "rows of v": add_rows})

        @block.gpsimd
        def _(gp):
            gp.wait_ge(toep_out, 16)
            gp.wait_ge(s5_out, 16 * DEPTH)
            for n in range(PASSES):
                b = n % NB
                gp.wait_ge(ids_ready, n + 1)
                with gp.Fori(n * ITERS, (n + 1) * ITERS) as turn:
                    for g in range(2):
                        ss = range(g * RING_G, (g + 1) * RING_G)
                        gp.wait_ge(v_used, turn * RING + (g + 1) * RING_G)
                        gp.wait_ge(ids_ready, n + 1)
                        gp.tensor_copy(ring_ids[:, g * RING_G:(g + 1) * RING_G],
                                       ids[:, b, bass.ds(turn * RING + (g * RING_G - n * SLOTS), RING_G)]).then_inc(ring_staged, RING_G)
                        gp.wait_ge(ids_ready, n + 1)
                        gp.wait_ge(ring_staged, turn * RING + (g + 1) * RING_G)
                        gp.wait_ge(dots_done, turn * RING + (g + 1) * RING_G)
                        for s in ss:
                            gp.indirect_dma_start(ring_u[:, s, :], None, table_u,
                                                  bass.IndirectOffsetOnAxis(ap=ring_ids[:, s:s + 1], axis=0)).then_inc(u_in[s], 16)
                        for s in ss:
                            gp.indirect_dma_start(ring_v[:, s, :], None, table_v,
                                                  bass.IndirectOffsetOnAxis(ap=ring_ids[:, s:s + 1], axis=0)).then_inc(v_in[s], 16)


def shape_constants():
    c = np.zeros((P, C_W), np.float32)
    p = np.arange(P)
    c[:, C_ID:C_ID + P] = np.eye(P)
    c[:, C_TRI:C_TRI + P] = p[:, None] <= p[None, :]
    c[:, C_ONE:C_ONE + P] = 1.0
    c[:, C_MASK:C_MASK + P] = np.where(p[None, :] <= p[:, None], 0.0, NEG)
    c[:, C_TAU:C_TAU + P] = p + 1
    for i in range(2):
        c[:, C_HM2 + i] = p // 64 == i
    for i in range(4):
        c[:, C_HM4 + i] = p // 32 == i
    c[:, C_IOTA:C_IOTA + TOPK] = np.arange(TOPK)
    return c


def bucket_constants():
    dist = 255 - np.arange(512)
    n = np.maximum(dist, 0)
    nf = np.maximum(n, MAX_EXACT).astype(np.float32)
    large = MAX_EXACT + (np.log(nf / np.float32(MAX_EXACT)) / math.log(MAX_DIST / MAX_EXACT)
                         * (BUCKETS - MAX_EXACT)).astype(np.int32)
    bucket = np.where(n < MAX_EXACT, n, np.minimum(large, BUCKETS - 1))
    c = np.zeros((BUCKETS + 2, 512), np.float32)
    c[bucket, np.arange(512)] = 1.0
    count = (dist <= 128).astype(int) + (dist % 4 == 0) + (dist % 16 == 0)
    seen = (dist >= 0) & (count > 0)
    c[BUCKETS] = np.where(seen, np.log(np.maximum(count, 1)), NEG)
    c[BUCKETS + 1] = np.where(dist >= 0, 0.0, NEG)
    return c


def layer_constants():
    c = np.zeros((DEPTH, 4), np.float32)
    for n in range(DEPTH):
        lam = 0.8 - 0.6 * math.exp(-0.3 * n)
        c[n] = lam, 1.0 - lam, n * NE, 0.0
    return c


def kernel(x, w_in, b_forget, w_out, norm_mix, norm_ffn, fox_q_norm, fox_k_norm, dil_q_norm, dil_k_norm,
           diff_q_norm, diff_k_norm, diff_lambda, diff_out_norm, rel_bias, s5_a_re, s5_a_im, s5_log_dt,
           s5_b_re, s5_b_im, s5_c_re, s5_c_im, s5_d, s5_glu_w, s5_glu_b, peer_wq, peer_keys, peer_u, peer_v):
    import concourse.bacc as bacc
    from concourse.bass_utils import run_bass_kernel_spmd

    L = DEPTH
    rows = np.concatenate([np.asarray(t).reshape(L, -1) for t in (
        fox_q_norm, fox_k_norm, dil_q_norm, dil_k_norm, diff_q_norm, diff_k_norm, diff_out_norm, b_forget,
        diff_lambda, layer_constants(), s5_d, s5_glu_b)], axis=1)

    def by_state(t):
        t = np.asarray(t)
        t = t.reshape((L, NJ, 2, S5_N) + t.shape[3:])
        t = np.moveaxis(t, 1, 3)
        return t.reshape((L, P, -1))

    def c_blocks(t):
        t = np.asarray(t)
        o = np.zeros((L, 2, S5_N, NJ, 2, S5_C), t.dtype)
        for g in range(2):
            o[:, g, :, :, g, :] = t.reshape(L, NJ, 2, S5_C, S5_N)[:, :, g].transpose(0, 3, 1, 2)
        return o.reshape(L, P, GW)

    parts = np.split(np.asarray(w_in), np.cumsum(IN_SPLIT)[:-1], axis=2)
    w_in = np.concatenate([parts[i] for i in IN_ORDER], axis=2)
    dt = np.repeat(np.asarray(s5_log_dt)[:, :, None], S5_N, axis=2)
    s5 = np.concatenate([by_state(s5_a_re), by_state(s5_a_im), by_state(dt), by_state(s5_b_re), by_state(s5_b_im),
                         c_blocks(s5_c_re), c_blocks(s5_c_im)], axis=2)
    keys = np.asarray(peer_keys).reshape(L, HP, NK, P).transpose(0, 3, 1, 2)
    arrays = {
        "x_in": np.asarray(x).reshape(SEQ, D), "w_in": w_in, "w_out": w_out, "row_in": rows,
        "gain_mix": norm_mix, "gain_ffn": norm_ffn, "s5_in": s5, "glu_w": s5_glu_w, "peer_wq": peer_wq,
        "keys_t": keys, "table_u": np.asarray(peer_u).reshape(L * NE, D), "table_v": np.asarray(peer_v).reshape(L * NE, D),
        "rel_bias": rel_bias, "const_in": shape_constants(), "bucket_in": bucket_constants(),
    }
    arrays = {k: np.ascontiguousarray(v) for k, v in arrays.items()}
    nc = bacc.Bacc("TRN2", target_bir_lowering=False, num_devices=1)
    args = {k: nc.dram_tensor(k, v.shape, mybir.dt.from_np(v.dtype), kind="ExternalInput").ap() for k, v in arrays.items()}
    out = nc.dram_tensor("out", (SEQ, D), F32, kind="ExternalOutput").ap()
    trunk(nc, **args, out=out)
    r = run_bass_kernel_spmd(nc, [arrays], core_ids=[0])
    return r.results[0]["out"].reshape(1, SEQ, D)
```

```python
import math
from contextlib import ExitStack

import numpy as np

import concourse.bass as bass
from concourse import mybir

ALU = mybir.AluOpType
ACT = mybir.ActivationFunctionType
AX = mybir.AxisListType.X
F32 = mybir.dt.float32
U32 = mybir.dt.uint32

P = 128
D = 1024
SEQ = 256
NB = SEQ // P
DEPTH = 2
KC = D // P
GW = D // 4
HD = 64
NH = GW // HD
DH = HD // 2
S5_G, S5_C, S5_N = 16, 16, 64
NJ = S5_G * S5_N // P
BUCKETS, MAX_EXACT, MAX_DIST = 32, 16, 2048
NK = 128
NE = NK * NK
PH, TOPK = 8, 16
HP = 2 * PH
SLOTS = PH * TOPK
EPS = 1e-6
NEG = -1.0e30
RING_G = 4
RING = 2 * RING_G
ITERS = SLOTS // RING

PASSES = DEPTH * NB
HALVES = SLOTS // RING_G

IN_SPLIT = [GW, GW, GW, NH, GW, GW, GW, GW, GW, GW, GW]
IN_ORDER = [0, 4, 7, 10, 3, 1, 5, 8, 2, 6, 9]
IN_W = sum(IN_SPLIT)
SU, FF = 3 * GW, 4 * GW
ZQ_W = FF + NH
KV_W = IN_W - ZQ_W
KEYS, VALS = 0, 3 * GW
BANK_CUTS = [0, 512, 1024, 1412, 1796, 2180, IN_W]
WIN_SLOTS = 6

R_FQ, R_FK, R_DQ, R_DK = 0, 64, 128, 192
R_CQ, R_CK = 256, 288
R_CO = 320
R_BF = 384
R_LAM = 388
R_LC = 516
R_SD = 520
R_GB = 776
R_W = 1032

C_ID, C_TRI, C_ONE, C_MASK = 0, 128, 256, 384
C_TAU = 512
C_HM2, C_HM4 = 640, 642
C_IOTA = 646
C_W = 662

S_AR, S_AI, S_DT = 0, 8, 16
S_BR, S_BI = 24, 24 + NJ * S5_C
S_CR = S_BI + NJ * S5_C
S_CI = S_CR + GW
S_W = S_CI + GW

TWO_PI = 2.0 * math.pi
PI_A = 6.28125
PI_B = 0.0019340515136718750
PI_C = TWO_PI - PI_A - PI_B
ROUND = 12582912.0


def bc(ap, axis, n):
    dims = [list(d) for d in ap.ap]
    dims.insert(axis, [0, n])
    return bass.AP(ap.tensor, ap.offset, dims)


def rep(ap, n):
    return bass.AP(ap.tensor, ap.offset, [list(ap.ap[0]), [0, n]])


class Order:

    def __init__(self, eng, sem):
        self.eng, self.sem, self.n = eng, sem, 0

    def __call__(self, ins):
        ins.then_inc(self.sem, 1)
        self.n += 1
        self.eng.wait_ge(self.sem, self.n)

    def free(self, ins):
        ins.then_inc(self.sem, 1)
        self.n += 1

    def join(self):
        self.eng.wait_ge(self.sem, self.n)


def plan_steps():
    project = [[f"project {k}", f"project {k + 1}"] for k in range(0, KC, 2)]
    s5 = [["s5 in", "qk sums", "bu"], ["qk scale"], ["keys 0", "s5 turn back"]]
    attention = [["logits 0", "s5 scan"], ["keys 1"], ["weights 0", "logits 1"], ["s5 turn on 0", "heads 0", "keys 2"],
                 ["weights 1", "logits 2"], ["s5 turn on 1", "heads 1"], ["weights 2", "logits 3"], ["heads 2", "s5 out"],
                 ["weights 3"], ["heads 3", "s5 gate", "mixed"]]
    search = [["out 0"], ["out 1"], ["norm 1", "rows 1"], ["query 0"], ["score 0", "query 1"], ["score 1", "query 2"],
              ["pairs 0"], ["ids 0"], ["score 2", "query 3"], ["score 3"], ["pairs 1"], ["ids 1"]]
    mix = [["norm 0", "rows 0"]] + project + s5 + attention + search
    assert len(mix) <= HALVES
    plan = []

    def do(groups, n):
        for group in groups:
            for name in group:
                word = name.rsplit(" ", 1)
                if word[-1].isdigit():
                    plan.append((word[0], n, int(word[1])))
                else:
                    plan.append((name, n, 0))

    k = 1 + len(project)
    out = mix.index(["out 0"]) + 1
    do(mix[:1] + [["phases 0", "tables 0", "phases 1"]] + mix[1:k] + [["turned 0"]] + mix[k:k + 1] + [["lines"]]
       + mix[k + 1:out] + [["tables 1"]] + mix[out:out + 2] + [["turned 1"]] + mix[out + 2:], 0)
    for n in range(PASSES):
        left = list(mix) if n + 1 < PASSES else []
        for i in range(HALVES):
            plan.append(("dots", n, i))
            if i == 0 and n:
                plan.append(("gathered", n - 1, 0))
            plan.append(("weigh", n, i))
            late = not (left and left[0][0].startswith("norm"))
            if not late:
                plan.append(("rows of v", n, i))
            do(left[:1], n + 1)
            left = left[1:]
            if late:
                plan.append(("rows of v", n, i))
    plan.append(("gathered", PASSES - 1, 0))
    return plan


def trunk(nc, x_in, w_in, w_out, row_in, gain_mix, gain_ffn, s5_in, glu_w, peer_wq, keys_t, table_u, table_v,
          rel_bias, const_in, bucket_in, out):
    ctx = ExitStack()
    with ctx:
        def sb(name, shape, dt=F32):
            return ctx.enter_context(nc.sbuf_tensor(name, shape, dt))

        def sem(name):
            return ctx.enter_context(nc.semaphore(name))

        ring_u = sb("ring_u", [P, RING, D])
        ring_v = sb("ring_v", [P, RING, D])
        W = sb("W", [P, 16384])
        x = sb("x", [P, NB, D])
        h = sb("h", [P, NB, D])
        hT = sb("hT", [P, KC, P])
        zq = sb("zq", [P, ZQ_W])
        zkv = sb("zkv", [P, NB, KV_W])
        bias = sb("bias", [P, 2 * NH, SEQ])
        cst = sb("cst", [P, C_W])
        row = sb("row", [P, R_W])
        s5t = sb("s5t", [P, 3072])
        glu = sb("glu", [P, 2, GW])
        small = sb("small", [P, 768])
        mags = sb("mags", [P, DEPTH, NJ])
        zero = sb("zero", [P, P])
        ids = sb("ids", [P, NB, SLOTS], U32)
        gates = sb("gates", [P, NB, SLOTS])
        ring_ids = sb("ring_ids", [P, 2, RING], U32)
        dots = sb("dots", [P, RING])
        acts = sb("acts", [P, RING])
        weights = sb("weights", [P, RING])
        diag = sb("diag", [P, RING, P])
        junk = sb("junk", [P, D], mybir.dt.bfloat16)

        win = W[:, 0:WIN_SLOTS * IN_W].rearrange("p (k n) -> p k n", n=IN_W)
        wout_v = W[:, 8192:16384].rearrange("p (k n) -> p k n", k=KC)
        wq_v = [W[:, 8192 + 4096 * i:12288 + 4096 * i].rearrange("p (k n) -> p k n", k=KC) for i in range(2)]
        T = W[:, 0:8192]
        ident, tri = cst[:, C_ID:C_ID + P], cst[:, C_TRI:C_TRI + P]
        triones = cst[:, C_TRI:C_TRI + 2 * P]
        ones, causal = cst[:, C_ONE:C_ONE + P], cst[:, C_MASK:C_MASK + P]
        hm2, hm4 = cst[:, C_HM2:C_HM2 + 2], cst[:, C_HM4:C_HM4 + 4]
        mixed = h

        def by(ap, n):
            return ap.rearrange("p (n k) -> p n k", k=n)

        cosT, sinT = by(s5t[:, 0:1024], P), by(s5t[:, 1024:2048], P)
        bT = by(s5t[:, 2048:2560], P)
        cR, cI = s5t[:, 2560:2816], s5t[:, 2816:3072]
        pbuf = by(T[:, 0:1024], SEQ)
        um = by(T[:, 0:1024], P)
        pT = by(T[:, 1024:2048], P)
        qm = T[:, 2048:3072]
        kT = T[:, 3072:3584].rearrange("p (i k) -> p i k", k=SEQ)
        ybuf, sbuf, gT = T[:, 3584:3840], T[:, 3840:4096], T[:, 1024:1280]
        s5a, s5b, s5c, s5d = [by(T[:, 4096 + 1024 * i:5120 + 1024 * i], P) for i in range(4)]
        sq = T[:, 4096:5632]
        gain_m = [zkv[:, b, 0:D] for b in range(NB)]
        gain_f = T[:, 4096:5120]
        kts, qts = by(T[:, 0:2048], NK), by(T[:, 2048:4096], P)
        hit = T[:, 6272:7296].rearrange("p (n k a) -> p n k a", k=TOPK, a=TOPK)
        sc2, cand = by(T[:, 4096:4608], NK), by(T[:, 6272:7296], 2 * P)
        v16, i16f, best = by(T[:, 4736:4992], TOPK), by(T[:, 4992:5248], TOPK), by(T[:, 5248:5376], TOPK)
        posf, idf = T[:, 5376:5504], [T[:, 5504:5632], T[:, 5632:5760]]
        i16, pos = by(T[:, 5760:6016].bitcast(U32), TOPK), by(T[:, 6016:6144].bitcast(U32), TOPK)
        posd = T[:, 6144:6272].bitcast(U32)

        ps = ctx.enter_context(nc.psum_tensor("ps", [P, 8, 512], F32))
        toep = nc.dram_tensor("toep", [2 * NH, P, 512], F32, kind="Internal").ap()
        s5_dram = nc.dram_tensor("s5_dram", [DEPTH - 1, P, 3072], F32, kind="Internal").ap()

        once_in, bias_in, toep_out = sem("once_in"), sem("bias_in"), sem("toep_out")
        s5_in_done = [sem(f"s5_in_{n}") for n in range(DEPTH)]
        toep_ready, toep_ps, toep_copied, zero_set = sem("toep_ready"), sem("toep_ps"), sem("toep_copied"), sem("zero_set")
        s5_tabled, s5_out, out_stored = sem("s5_tabled"), sem("s5_out"), sem("out_stored")
        u_in = [sem(f"u_in{i}") for i in range(RING)]
        v_in = [sem(f"v_in{i}") for i in range(RING)]
        u_staged, v_staged, dots_done, gelu_done, weights_done, diag_ready, v_used = (
            sem("u_staged"), sem("v_staged"), sem("dots_done"), sem("gelu_done"), sem("weights_done"), sem("diag_ready"), sem("v_used"))
        acc_ps, x_done = sem("acc_ps"), sem("x_done")
        dve_step, act_step = sem("dve_step"), sem("act_step")
        win_in = [sem(f"win_in{k}") for k in range(WIN_SLOTS)]
        wq_in = [sem(f"wq_in{k}") for k in range(2)]
        row_load, gain_load, s5_load, glu_load, ffn_load, wout_load, keys_load = (
            sem("row_load"), sem("gain_load"), sem("s5_load"), sem("glu_load"), sem("ffn_load"), sem("wout_load"),
            sem("keys_load"))
        sumsq, mean_inv, rstd, h_ready = sem("sumsq"), sem("mean_inv"), sem("rstd"), sem("h_ready")
        rows_ps, rows_dve, rows_act = sem("rows_ps"), sem("rows_dve"), sem("rows_act")
        chunk_used, z_ps, z_dve, z_act = sem("chunk_used"), sem("z_ps"), sem("z_dve"), sem("z_act")
        s5_exp, s5_ang, s5_sin, s5_bx, s5_bt_ps = sem("s5_exp"), sem("s5_ang"), sem("s5_sin"), sem("s5_bx"), sem("s5_bt_ps")
        lam_sum, lam_exp = sem("lam_sum"), sem("lam_exp")
        qk_inv, qk_rstd, qk_ready = sem("qk_inv"), sem("qk_rstd"), sem("qk_ready")
        f_bias, f_ln, f_ready = sem("f_bias"), sem("f_ln"), sem("f_ready")
        keys_ps, keys_ready = sem("keys_ps"), sem("keys_ready")
        logit_ps, logit_max, p_exp, p_ready = sem("logit_ps"), sem("logit_max"), sem("p_exp"), sem("p_ready")
        pT_ps, pT_ready, o_ps, o_used = sem("pT_ps"), sem("pT_ready"), sem("o_ps"), sem("o_used")
        co_inv, co_rstd = sem("co_inv"), sem("co_rstd")
        uT_ps, um_ready, bu_ps, bu_used = sem("uT_ps"), sem("um_ready"), sem("bu_ps"), sem("bu_used")
        s5_state, y_ps, y_ready, g_ready = sem("s5_state"), sem("y_ps"), sem("y_ready"), sem("g_ready")
        gT_ps, gT_ready, glu_ps, glu_sum, glu_sig, mixed_ready = (
            sem("gT_ps"), sem("gT_ready"), sem("glu_ps"), sem("glu_sum"), sem("glu_sig"), sem("mixed_ready"))
        mT_ps, mT_dve, mT_act, wo_ps, x_ready = sem("mT_ps"), sem("mT_dve"), sem("mT_act"), sem("wo_ps"), sem("x_ready")
        qT_ps, qT_ready, sc_ps, sc_used = sem("qT_ps"), sem("qT_ready"), sem("sc_ps"), sem("sc_used")
        best_sub, gate_exp, ids_ready, gates_ready = sem("best_sub"), sem("gate_exp"), sem("ids_ready"), sem("gates_ready")

        def keys_bank(g):
            return 6 if g else 2

        plan = plan_steps()

        def walk(steps):
            for name, n, i in plan:
                if name in steps:
                    steps[name](n, i)

        line = ring_u[0:BUCKETS + 2, 0, 0:512]
        tab = ring_u[0:BUCKETS + 2, 2, 0:8]
        tabx = ring_u[0:BUCKETS + 2, 3, :].rearrange("p (n k) -> p n k", n=2 * NH)
        line_sb = ring_u[:, 4:8, :].rearrange("p a (n k) -> p (a n) k", k=512)
        s5p = [ring_v[:, 0, 0:S_W], ring_v[:, 7, 0:S_W]]
        ang, turns = by(ring_v[:, 1, :], P), by(ring_v[:, 2, :], P)
        bsc = [ring_v[:, 3, :], ring_u[:, 1, :]]
        tables_at = [s5t[:, :], ring_v[:, 4:7, :].rearrange("p a n -> p (a n)")]

        block = ctx.enter_context(nc.Block())

        @block.sync
        def _(sp):
            sp.dma_start(cst[:, :], const_in).then_inc(once_in, 16)
            sp.dma_start(x[:, :, :], x_in.rearrange("(b p) d -> p b d", p=P)).then_inc(once_in, 16)
            sp.dma_start(line, bucket_in).then_inc(once_in, 16)
            sp.dma_start(tab, rel_bias).then_inc(once_in, 16)
            for i in range(DEPTH):
                sp.dma_start(s5p[i], s5_in[i]).then_inc(s5_in_done[i], 16)

            def load_chunk(n, k):
                sp.dma_start(win[:, k % WIN_SLOTS, :], w_in[n // NB, k * P:(k + 1) * P, :]).then_inc(win_in[k % WIN_SLOTS], 16)

            for n in range(PASSES):
                layer, b = n // NB, n % NB
                if n:
                    sp.wait_ge(o_ps, 4 * n)
                sp.dma_start(gain_m[b], gain_mix[layer].partition_broadcast(P)).then_inc(gain_load, 16)
                if n:
                    sp.wait_ge(ids_ready, 2 * n)
                if b == 0:
                    sp.dma_start(row[:, :], row_in[layer].partition_broadcast(P)).then_inc(row_load, 16)
                for k in range(WIN_SLOTS):
                    load_chunk(n, k)
                if b == 0:
                    if layer:
                        sp.wait_ge(s5_out, 16 * layer)
                        sp.dma_start(s5t[:, :], s5_dram[layer - 1]).then_inc(s5_load, 16)
                    sp.dma_start(glu[:, :, :], glu_w[layer].rearrange("(k p) n -> p k n", p=P)).then_inc(glu_load, 16)
                for k in range(WIN_SLOTS, KC):
                    sp.wait_ge(chunk_used, KC * n + k - WIN_SLOTS + 1)
                    load_chunk(n, k)
                sp.wait_ge(z_ps, 6 * n + 6)
                sp.dma_start(wout_v, w_out[layer].rearrange("(k p) n -> p k n", p=P)).then_inc(wout_load, 16)
                if n == 0:
                    sp.wait_ge(toep_copied, 2 * NH)
                    sp.dma_start(toep.rearrange("n p k -> p n k"), line_sb).then_inc(toep_out, 16)
                    sp.wait_ge(toep_out, 16)
                    for i in range(2 * NH):
                        skew = bass.AP(toep.tensor, i * P * 512 + P - 1, [[511, P], [1, SEQ]])
                        sp.dma_start(bias[:, i, :], skew).then_inc(bias_in, 16)
                sp.wait_ge(y_ps, n + 1)
                sp.dma_start(gain_f, gain_ffn[layer].partition_broadcast(P)).then_inc(ffn_load, 16)
                sp.wait_ge(mixed_ready, n + 1)
                sp.dma_start(kts, keys_t[layer]).then_inc(keys_load, 16)
                sp.wait_ge(wo_ps, 2 * n + 2)
                for i in range(4):
                    if n == 0 and i == 2:
                        sp.wait_ge(s5_tabled, 2)
                        sp.dma_start(s5_dram[0], tables_at[1]).then_inc(s5_out, 16)
                    if i >= 2:
                        sp.wait_ge(qT_ps, 4 * n + i - 1)
                    sp.dma_start(wq_v[i % 2], peer_wq[layer, :, i * 512:(i + 1) * 512].rearrange("(k p) n -> p k n", p=P))\
                        .then_inc(wq_in[i % 2], 16)
            for b in range(NB):
                sp.wait_ge(x_done, PASSES - NB + b + 1)
                sp.dma_start(out[b * P:(b + 1) * P, :], x[:, b, :]).then_inc(out_stored, 16)
            sp.wait_ge(out_stored, 16 * NB)

        @block.scalar
        def _(a):
            step = Order(a, act_step)

            def phases(_, n):
                a.wait_ge(s5_in_done[n], 16)
                a.activation(small[:, 16:24], s5p[n][:, S_DT:S_DT + NJ], ACT.Exp).then_inc(s5_exp, 1)
                a.wait_ge(s5_ang, 2 * n + 1)
                a.activation(mags[:, n, :], small[:, 24:32], ACT.Exp).then_inc(s5_exp, 1)

            def lines_out(n, i):
                for j in range(2 * NH):
                    a.wait_ge(toep_ps, j + 1)
                    a.activation(line_sb[:, j, :], ps[:, j % 2, :], ACT.Copy).then_inc(toep_copied, 1)

            def tables(_, n):
                sinT, cosT = by(tables_at[n][:, 1024:2048], P), by(tables_at[n][:, 0:1024], P)
                a.wait_ge(s5_ang, 2 * n + 2)
                a.activation(sinT, ang, ACT.Sin).then_inc(s5_sin, 1)
                a.activation(cosT, ang, ACT.Sin, scale=0.5).then_inc(s5_sin, 1)

            def norm(n, i):
                m, b = 2 * n + i, n % NB
                if i == 0:
                    if n >= NB:
                        a.wait_ge(x_done, n - NB + 1)
                    elif n == 0:
                        a.wait_ge(once_in, 64)
                else:
                    a.wait_ge(x_ready, n + 1)
                a.wait_ge(rows_ps, m) if m else None
                a.activation(h[:, b, :], x[:, b, :], ACT.Square, accum_out=small[:, 0:1]).then_inc(sumsq, 1)
                a.wait_ge(mean_inv, m + 1)
                a.activation(small[:, 8:9], small[:, 4:5], ACT.Sqrt).then_inc(rstd, 1)

            def rows(n, i):
                m = 2 * n + i
                a.wait_ge(rows_ps, m + 1)
                a.activation(hT[:, 4:8, :], by(ps[:, 3 + 2 * i, :], P), ACT.Copy).then_inc(rows_act, 1)
                if i == 0 and n % NB == 0:
                    a.wait_ge(lam_sum, n // NB + 1)
                    a.activation(small[:, 42:44], small[:, 40:42], ACT.Exp).then_inc(lam_exp, 1)

            def project(n, k):
                if k < KC - 1:
                    return
                b = n % NB
                for bank, dst in ((1, zq[:, 512:1024]), (3, zkv[:, b, 384:768]), (5, zkv[:, b, 1152:1536])):
                    a.wait_ge(z_ps, 6 * n + bank + 1)
                    c0, c1 = BANK_CUTS[bank:bank + 2]
                    a.activation(dst, ps[:, 2 + bank, 0:c1 - c0], ACT.Copy).then_inc(z_act, 1)

            def qk_sums(n, i):
                a.wait_ge(f_bias, n + 1)
                step(a.activation(small[:, 56:60], small[:, 48:52], ACT.Abs))
                step(a.activation(small[:, 56:60], small[:, 56:60], ACT.Exp, scale=-1.0))
                a.activation(small[:, 64:68], small[:, 56:60], ACT.Ln, bias=1.0).then_inc(f_ln, 1)
                a.wait_ge(qk_inv, n + 1)
                a.activation(small[:, 128:160], small[:, 96:128], ACT.Sqrt).then_inc(qk_rstd, 1)

            def logits(n, g):
                nk = P * (n % NB + 1)
                lg = ps[:, 2:4, :].rearrange("p c n -> p (c n)")
                a.wait_ge(logit_max, 4 * n + g + 1)
                for i in range(4):
                    a.activation(pbuf[:, i, 0:nk], lg[:, i * nk:(i + 1) * nk], ACT.Exp, bias=small[:, 72 + i:73 + i],
                                 accum_out=small[:, 80 + i:81 + i]).then_inc(p_exp, 1)

            def head_weights(n, g):
                tiles = (4 if g < 2 else 2) * (n % NB + 1)
                a.wait_ge(pT_ps, 4 * n + g + 1)
                for c in range(0, tiles, 4):
                    m = min(4, tiles - c)
                    ins = a.activation(pT[:, c:c + m, :], by(ps[:, 4 + c // 4, 0:m * P], P), ACT.Copy)
                    if c + m == tiles:
                        ins.then_inc(pT_ready, 1)
                    else:
                        step(ins)

            def heads(n, g):
                if g == 3:
                    a.wait_ge(co_inv, n + 1)
                    a.activation(small[:, 196:200], small[:, 192:196], ACT.Sqrt).then_inc(co_rstd, 1)

            def s5_output(n, i):
                a.wait_ge(y_ready, n + 1)
                a.activation(ybuf, ybuf, ACT.Gelu_apprx_tanh).then_inc(g_ready, 1)

            def mix_end(n, i):
                a.wait_ge(glu_sum, n + 1)
                a.activation(sbuf, sbuf, ACT.Sigmoid).then_inc(glu_sig, 1)

            def out_rows(n, i):
                if i == 0:
                    a.wait_ge(mT_ps, n + 1)
                    a.activation(hT[:, 4:8, :], by(ps[:, 5, :], P), ACT.Copy).then_inc(mT_act, 1)

            def query(n, i):
                a.wait_ge(qT_ps, 4 * n + i + 1)
                a.activation(qts[:, 4 * i:4 * i + 4, :], by(ps[:, 6 + i % 2, :], P), ACT.Copy).then_inc(qT_ready, 1)

            def find_ids(n, q):
                half = gates[:, n % NB, q * SLOTS // 2:(q + 1) * SLOTS // 2]
                a.wait_ge(best_sub, 2 * n + q + 1)
                a.activation(half, half, ACT.Exp).then_inc(gate_exp, 1)

            def take_dots(n, i):
                m, g = HALVES * n + i, i % 2
                a.wait_ge(dots_done, RING + RING_G * (m + 1))
                if m >= 2:
                    a.wait_ge(weights_done, m - 1)
                a.activation(acts[:, g * RING_G:(g + 1) * RING_G], dots[:, g * RING_G:(g + 1) * RING_G],
                             ACT.Gelu_apprx_tanh).then_inc(gelu_done, 1)

            def weigh(n, i):
                m, g = HALVES * n + i, i % 2
                a.wait_ge(weights_done, m + 1)
                if m >= 2:
                    a.wait_ge(v_used, RING + RING_G * (m - 1))
                for s in range(g * RING_G, (g + 1) * RING_G):
                    a.activation(diag[:, s, :], ident, ACT.Copy, scale=weights[:, s:s + 1]).then_inc(diag_ready, 1)

            walk({"phases": phases, "lines": lines_out, "tables": tables, "norm": norm, "rows": rows, "project": project,
                  "qk sums": qk_sums, "logits": logits,
                  "weights": head_weights, "heads": heads, "s5 out": s5_output, "mixed": mix_end, "out": out_rows,
                  "query": query, "ids": find_ids, "dots": take_dots, "weigh": weigh})

        @block.vector
        def _(v):
            step = Order(v, dve_step)

            v.memset(zero[:, :], 0.0).then_inc(zero_set, 1)
            v.sem_inc(dots_done, RING)
            v.wait_ge(once_in, 64)
            v.tensor_copy(tabx, bc(tab, 2, P)).then_inc(toep_ready, 1)

            def reduce_angle(t, k):
                step(v.tensor_scalar(k, t, 1.0 / TWO_PI, ROUND, ALU.mult, ALU.add))
                step(v.tensor_scalar(k, k, ROUND, None, ALU.subtract))
                for part in (PI_A, PI_B, PI_C):
                    step(v.scalar_tensor_tensor(out=t, in0=k, scalar=-part, in1=t, op0=ALU.mult, op1=ALU.add))

            def phases(_, n):
                ar, ai = s5p[n][:, S_AR:S_AR + NJ], s5p[n][:, S_AI:S_AI + NJ]
                th, kk = small[:, 208:216], small[:, 216:224]
                v.wait_ge(s5_in_done[n], 16)
                v.wait_ge(s5_exp, 2 * n + 1)
                v.tensor_tensor(small[:, 24:32], small[:, 16:24], ar, ALU.mult).then_inc(s5_ang, 1)
                step(v.tensor_tensor(th, small[:, 16:24], ai, ALU.mult))
                reduce_angle(th, kk)
                step(v.tensor_tensor(ang, bc(th, 2, P), bc(cst[:, C_TAU:C_TAU + P], 1, NJ), ALU.mult))
                reduce_angle(ang, turns)
                v.tensor_scalar(ang, ang, 3.1415925, -3.1415925, ALU.min, ALU.max).then_inc(s5_ang, 1)

            def tables(_, n):
                ar, ai, mag = s5p[n][:, S_AR:S_AR + NJ], s5p[n][:, S_AI:S_AI + NJ], mags[:, n, :]
                at = tables_at[n]
                cosT, sinT, cR, cI = by(at[:, 0:1024], P), by(at[:, 1024:2048], P), at[:, 2560:2816], at[:, 2816:3072]
                v.wait_ge(s5_sin, 2 * n + 2)
                step(v.tensor_tensor(cosT, cosT, cosT, ALU.mult))
                step(v.tensor_scalar(cosT, cosT, -2.0, 1.0, ALU.mult, ALU.add))
                v.wait_ge(s5_exp, 2 * n + 2)
                nr, ni, den, t0, t1, cr, ci = [small[:, 288 + 8 * i:296 + 8 * i] for i in range(7)]
                step(v.tensor_tensor(nr, mag, cosT[:, :, 0], ALU.mult))
                step(v.tensor_scalar(nr, nr, 1.0, None, ALU.subtract))
                step(v.tensor_tensor(ni, mag, sinT[:, :, 0], ALU.mult))
                step(v.tensor_tensor(t0, ar, ar, ALU.mult))
                step(v.tensor_tensor(t1, ai, ai, ALU.mult))
                step(v.tensor_tensor(den, t0, t1, ALU.add))
                step(v.reciprocal(den, den))
                step(v.tensor_tensor(t0, nr, ar, ALU.mult))
                step(v.tensor_tensor(t1, ni, ai, ALU.mult))
                step(v.tensor_tensor(cr, t0, t1, ALU.add))
                step(v.tensor_tensor(cr, cr, den, ALU.mult))
                step(v.tensor_tensor(t0, ni, ar, ALU.mult))
                step(v.tensor_tensor(t1, nr, ai, ALU.mult))
                step(v.tensor_tensor(ci, t0, t1, ALU.subtract))
                step(v.tensor_tensor(ci, ci, den, ALU.mult))
                br, bi = by(s5p[n][:, S_BR:S_BR + P], S5_C), by(s5p[n][:, S_BI:S_BI + P], S5_C)
                b0, b1, b2 = [by(bsc[n][:, P * i:P * (i + 1)], S5_C) for i in range(3)]
                bx = bsc[n][:, 512:1024].rearrange("p (r j g c) -> p r j g c", r=2, j=NJ, g=2)
                step(v.tensor_tensor(b0, br, bc(cr, 2, S5_C), ALU.mult))
                step(v.tensor_tensor(b1, bi, bc(ci, 2, S5_C), ALU.mult))
                step(v.tensor_tensor(b2, b0, b1, ALU.subtract))
                for g in range(2):
                    step(v.tensor_scalar(bx[:, 0, :, g, :], b2, hm2[:, g:g + 1], None, ALU.mult))
                step(v.tensor_tensor(b0, bi, bc(cr, 2, S5_C), ALU.mult))
                step(v.tensor_tensor(b1, br, bc(ci, 2, S5_C), ALU.mult))
                step(v.tensor_tensor(b2, b0, b1, ALU.add))
                step(v.tensor_scalar(bx[:, 1, :, 0, :], b2, hm2[:, 0:1], None, ALU.mult))
                v.tensor_scalar(bx[:, 1, :, 1, :], b2, hm2[:, 1:2], None, ALU.mult).then_inc(s5_bx, 1)
                step(v.tensor_copy(cR, s5p[n][:, S_CR:S_CR + GW]))
                step(v.tensor_scalar(cI, s5p[n][:, S_CI:S_CI + GW], -1.0, None, ALU.mult))

            def turned(_, n):
                v.wait_ge(s5_bt_ps, n + 1)
                v.tensor_copy(tables_at[n][:, 2048:2560], ps[:, 1 - n, :]).then_inc(s5_tabled, 1)

            def norm(n, i):
                m, b = 2 * n + i, n % NB
                v.wait_ge(sumsq, m + 1)
                step(v.tensor_scalar(small[:, 4:5], small[:, 0:1], 1.0 / D, EPS, ALU.mult, ALU.add))
                v.reciprocal(small[:, 4:5], small[:, 4:5]).then_inc(mean_inv, 1)
                v.wait_ge(rstd, m + 1)
                v.wait_ge((gain_load, ffn_load)[i], 16 * (n + 1))
                v.scalar_tensor_tensor(out=h[:, b, :], in0=x[:, b, :], scalar=small[:, 8:9], in1=(gain_m[b], gain_f)[i],
                                       op0=ALU.mult, op1=ALU.mult).then_inc(h_ready, 1)
                v.wait_ge(h_ready, m + 1)

            def rows(n, i):
                v.wait_ge(rows_ps, 2 * n + i + 1)
                v.tensor_copy(hT[:, 0:4, :], by(ps[:, 2 + 2 * i, :], P)).then_inc(rows_dve, 1)
                if i == 0 and n % NB == 0:
                    layer = n // NB
                    v.wait_ge(row_load, 16 * (layer + 1))
                    lam = row[:, R_LAM:R_LAM + 128].rearrange("p (a b d) -> p a b d", a=2, b=2)
                    prod = small[:, 224:288].rearrange("p (a d) -> p a d", a=2)
                    step(v.tensor_tensor(prod, lam[:, :, 0, :], lam[:, :, 1, :], ALU.mult))
                    v.reduce_sum(small[:, 40:42], prod, AX).then_inc(lam_sum, 1)
                    step(v.tensor_scalar(row[:, R_FQ:R_FQ + HD], row[:, R_FQ:R_FQ + HD], HD ** -0.5, None, ALU.mult))
                    step(v.tensor_scalar(row[:, R_DQ:R_DQ + HD], row[:, R_DQ:R_DQ + HD], HD ** -0.5, None, ALU.mult))
                    step(v.tensor_scalar(row[:, R_CQ:R_CQ + DH], row[:, R_CQ:R_CQ + DH], DH ** -0.5, None, ALU.mult))
                    step(v.tensor_scalar(row[:, R_CO:R_CO + HD], row[:, R_CO:R_CO + HD], row[:, R_LC + 1:R_LC + 2], None, ALU.mult))
                    v.wait_ge(lam_exp, layer + 1)
                    step(v.tensor_tensor(nlam, small[:, 43:44], small[:, 42:43], ALU.subtract))
                    step(v.tensor_tensor(nlam, nlam, row[:, R_LC:R_LC + 1], ALU.subtract))

            nlam = small[:, 44:45]

            def project(n, k):
                if k < KC - 1:
                    return
                b = n % NB
                v.wait_ge(z_ps, 6 * n + 1)
                v.tensor_copy(zq[:, 0:512], ps[:, 2, :]).then_inc(z_dve, 1)
                v.wait_ge(z_ps, 6 * n + 3)
                v.tensor_copy(zq[:, FF:ZQ_W], ps[:, 4, 0:NH]).then_inc(z_dve, 1)
                v.tensor_copy(zkv[:, b, 0:384], ps[:, 4, NH:388]).then_inc(z_dve, 1)
                v.wait_ge(z_ps, 6 * n + 5)
                v.tensor_copy(zkv[:, b, 768:1152], ps[:, 6, 0:384]).then_inc(z_dve, 1)
                v.wait_ge(z_dve, 4 * n + 4)
                v.wait_ge(z_act, 3 * n + 3)

            def qk_sums(n, i):
                b = n % NB
                f = small[:, 48:52]
                v.tensor_tensor(f, zq[:, FF:FF + NH], row[:, R_BF:R_BF + NH], ALU.add).then_inc(f_bias, 1)
                step(v.tensor_tensor(sq[:, 0:768], zq[:, 0:768], zq[:, 0:768], ALU.mult))
                step(v.tensor_tensor(sq[:, 768:1536], zkv[:, b, KEYS:KEYS + 768], zkv[:, b, KEYS:KEYS + 768], ALU.mult))
                s2 = sq.rearrange("p (a n) -> p a n", a=2)
                st = small[:, 96:128].rearrange("p (a n) -> p a n", a=2)
                step(v.reduce_sum(st[:, :, 0:8], s2[:, :, 0:512].rearrange("p a (n d) -> p a n d", d=HD), AX))
                step(v.reduce_sum(st[:, :, 8:16], s2[:, :, 512:768].rearrange("p a (n d) -> p a n d", d=DH), AX))
                step(v.tensor_scalar(st[:, :, 0:8], st[:, :, 0:8], 1.0 / HD, EPS, ALU.mult, ALU.add))
                step(v.tensor_scalar(st[:, :, 8:16], st[:, :, 8:16], 1.0 / DH, EPS, ALU.mult, ALU.add))
                v.reciprocal(small[:, 96:128], small[:, 96:128]).then_inc(qk_inv, 1)

            def qk_scale(n, i):
                b, f = n % NB, small[:, 48:52]
                v.wait_ge(f_ln, n + 1)
                ls, nls = small[:, 352 + NH * b:356 + NH * b], small[:, 360 + NH * b:364 + NH * b]
                step(v.tensor_scalar(nls, f, 0.0, None, ALU.min))
                step(v.tensor_tensor(ls, nls, small[:, 64:68], ALU.subtract))
                v.tensor_scalar(nls, ls, -1.0, None, ALU.mult).then_inc(f_ready, 1)
                v.wait_ge(qk_rstd, n + 1)
                groups = ((0, HD, R_FQ), (1, HD, R_DQ), (2, DH, R_CQ))
                rs = small[:, 128:160].rearrange("p (a n) -> p a n", a=2)
                for g, w, r0 in groups:
                    heads = GW // w
                    for a_, src in enumerate((zq[:, GW * g:GW * (g + 1)], zkv[:, b, KEYS + GW * g:KEYS + GW * (g + 1)])):
                        zz = by(src, w)
                        r = rs[:, a_, NH * g:NH * g + heads]
                        gg = row[:, r0 + a_ * w:r0 + (a_ + 1) * w]
                        step(v.tensor_tensor(zz, zz, bc(r, 2, w), ALU.mult))
                        ins = v.tensor_tensor(zz, zz, bc(gg, 1, heads), ALU.mult)
                        if a_:
                            ins.then_inc(qk_ready, 1)
                            v.wait_ge(qk_ready, 3 * n + g + 1)
                        else:
                            step(ins)

            def s5_inputs(n, i):
                v.wait_ge(uT_ps, n + 1)
                v.tensor_tensor(T[:, 0:1024].rearrange("p (h j t) -> p h j t", h=2, j=4), bc(by(ps[:, 2, 0:256], P), 2, 4),
                                bc(bc(hm4, 1, 2), 3, P), ALU.mult).then_inc(um_ready, 1)

            def keys(n, g):
                b = n % NB
                v.wait_ge(keys_ps, 3 * n + g + 1)
                c = keys_bank(g)
                tq = by(ps[:, c + 1, 0:256], P)
                if g < 2:
                    step(v.tensor_tensor(qm[:, 0:512].rearrange("p (i c t) -> p i c t", i=2, c=2), bc(tq, 2, 2),
                                         bc(bc(hm2, 1, 2), 3, P), ALU.mult))
                else:
                    step(v.tensor_tensor(qm.rearrange("p (i c t) -> p i c t", i=2, c=4), bc(tq, 2, 4),
                                         bc(bc(hm4, 1, 2), 3, P), ALU.mult))
                nk = P * (b + 1)
                v.tensor_copy(kT[:, :, 0:nk], ps[:, c, 0:2 * nk].rearrange("p (i k) -> p i k", k=nk)).then_inc(keys_ready, 1)

            def s5_turn_back(n, i):
                v.wait_ge(bu_ps, n + 1)
                re, im = (ps[:, 4 + r:7 + r:2, :].rearrange("p h (j t) -> p h j t", t=P) for r in range(2))
                hv = lambda t: t.rearrange("p (h j) t -> p h j t", h=2)
                step(v.tensor_tensor(hv(s5a), hv(cosT), re, ALU.mult))
                step(v.tensor_tensor(hv(s5c), hv(sinT), im, ALU.mult))
                step(v.tensor_tensor(hv(s5b), hv(cosT), im, ALU.mult))
                v.tensor_tensor(hv(s5d), hv(sinT), re, ALU.mult).then_inc(bu_used, 1)
                v.wait_ge(bu_used, n + 1)
                step(v.tensor_tensor(s5a, s5a, s5c, ALU.add))
                step(v.tensor_tensor(s5b, s5b, s5d, ALU.subtract))

            carry = small[:, 384:400]

            def s5_scan(n, i):
                for j in range(NJ):
                    for c, buf in enumerate((s5a, s5b)):
                        init = 0.0 if n % NB == 0 else carry[:, c * NJ + j:c * NJ + j + 1]
                        step.free(v.tensor_tensor_scan(buf[:, j, :], rep(mags[:, n // NB, j:j + 1], P), buf[:, j, :], init,
                                                       ALU.mult, ALU.add))
                step.join()

            def s5_turn_on(n, i):
                if i == 0:
                    step(v.tensor_tensor(s5c, cosT, s5a, ALU.mult))
                    step(v.tensor_tensor(s5d, sinT, s5b, ALU.mult))
                    step(v.tensor_tensor(s5c, s5c, s5d, ALU.subtract))
                    return
                step(v.tensor_tensor(s5b, cosT, s5b, ALU.mult))
                step(v.tensor_tensor(s5a, sinT, s5a, ALU.mult))
                v.tensor_tensor(s5b, s5a, s5b, ALU.add).then_inc(s5_state, 1)
                if n % NB == 0:
                    v.wait_ge(s5_state, n + 1)
                    step(v.tensor_copy(carry[:, 0:NJ], s5c[:, :, P - 1]))
                    step(v.tensor_copy(carry[:, NJ:2 * NJ], s5b[:, :, P - 1]))

            def logits(n, g):
                nk = P * (n % NB + 1)
                v.wait_ge(logit_ps, 4 * n + g + 1)
                lg = by(ps[:, 2:4, :].rearrange("p c n -> p (c n)")[:, 0:4 * nk], nk)
                step(v.reduce_max(small[:, 76:80], lg, AX))
                v.tensor_scalar(small[:, 72:76], small[:, 76:80], -1.0, None, ALU.mult).then_inc(logit_max, 1)

            def head_weights(n, g):
                nk = P * (n % NB + 1)
                inv = small[:, 84 + 4 * (g % 2):88 + 4 * (g % 2)]
                v.wait_ge(p_exp, 16 * n + 4 * g + 4)
                if g < 2:
                    v.reciprocal(inv, small[:, 80:84]).then_inc(p_ready, 1)
                    v.wait_ge(p_ready, 4 * n + g + 1)
                    return
                step(v.reciprocal(inv, small[:, 80:84]))
                step(v.tensor_scalar(small[:, 92:96], inv, nlam, None, ALU.mult))
                for i in range(2):
                    step(v.tensor_scalar(pbuf[:, 2 * i + 1, 0:nk], pbuf[:, 2 * i + 1, 0:nk],
                                         small[:, 93 + 2 * i:94 + 2 * i], None, ALU.mult))
                for i in range(2):
                    ins = v.scalar_tensor_tensor(out=pbuf[:, 2 * i, 0:nk], in0=pbuf[:, 2 * i, 0:nk], scalar=inv[:, 2 * i:2 * i + 1],
                                                 in1=pbuf[:, 2 * i + 1, 0:nk], op0=ALU.mult, op1=ALU.add)
                    if i:
                        ins.then_inc(p_ready, 1)
                    else:
                        step(ins)

            def heads(n, g):
                b = n % NB
                v.wait_ge(o_ps, 4 * n + g + 1)
                if g < 2:
                    v.tensor_tensor(by(mixed[:, b, g * GW:(g + 1) * GW], HD), by(ps[:, 7, 256:512], HD),
                                    bc(small[:, 84 + 4 * g:88 + 4 * g], 2, HD), ALU.mult).then_inc(o_used, 1)
                else:
                    v.tensor_copy(mixed[:, b, 2 * GW + (g - 2) * P:2 * GW + (g - 1) * P], ps[:, 7, 256:384]).then_inc(o_used, 1)
                v.wait_ge(o_used, 4 * n + g + 1)
                if g == 3:
                    co = mixed[:, b, 2 * GW:3 * GW]
                    step(v.tensor_tensor(T[:, 2048:2304], co, co, ALU.mult))
                    step(v.reduce_sum(small[:, 192:196], by(T[:, 2048:2304], HD), AX))
                    step(v.tensor_scalar(small[:, 192:196], small[:, 192:196], 1.0 / HD, EPS, ALU.mult, ALU.add))
                    v.reciprocal(small[:, 192:196], small[:, 192:196]).then_inc(co_inv, 1)
                    v.wait_ge(co_rstd, n + 1)
                    co = by(co, HD)
                    step(v.tensor_tensor(co, co, bc(small[:, 196:200], 2, HD), ALU.mult))
                    step(v.tensor_tensor(co, co, bc(row[:, R_CO:R_CO + HD], 1, NH), ALU.mult))

            def s5_output(n, i):
                step(v.tensor_tensor(T[:, 2048:2304], zq[:, SU:SU + GW], row[:, R_SD:R_SD + GW], ALU.mult))
                v.wait_ge(y_ps, n + 1)
                v.tensor_tensor(ybuf, T[:, 2048:2304], ps[:, 6, 0:256], ALU.add).then_inc(y_ready, 1)
                v.wait_ge(y_ready, n + 1)

            def s5_gate(n, i):
                v.wait_ge(gT_ps, n + 1)
                v.tensor_copy(gT, ps[:, 6, 0:256]).then_inc(gT_ready, 1)

            def mix_end(n, i):
                v.wait_ge(glu_ps, n + 1)
                v.tensor_tensor(sbuf, ps[:, 6, 0:256], row[:, R_GB:R_GB + GW], ALU.add).then_inc(glu_sum, 1)
                v.wait_ge(glu_sig, n + 1)
                v.tensor_tensor(mixed[:, n % NB, 3 * GW:4 * GW], ybuf, sbuf, ALU.mult).then_inc(mixed_ready, 1)

            def out_rows(n, i):
                if i == 0:
                    v.wait_ge(mT_ps, n + 1)
                    v.tensor_copy(hT[:, 0:4, :], by(ps[:, 4, :], P)).then_inc(mT_dve, 1)
                else:
                    b = n % NB
                    v.wait_ge(wo_ps, 2 * n + 2)
                    v.tensor_tensor(x[:, b, :], x[:, b, :], ps[:, 2:4, :].rearrange("p c n -> p (c n)"), ALU.add).then_inc(x_ready, 1)

            def score(n, q):
                v.wait_ge(sc_ps, 4 * n + q + 1)
                four = [(4 * q + i, ps[:, 2 + q, i * NK:(i + 1) * NK], sc2[:, i, :]) for i in range(4)]
                for k, sc, _ in four:
                    step.free(v.max(v16[:, k, 0:8], sc))
                step.join()
                for k, sc, rest in four:
                    step.free(v.max_index(i16[:, k, 0:8], v16[:, k, 0:8], sc))
                    step.free(v.match_replace(rest, v16[:, k, 0:8], sc, NEG))
                step.join()
                for k, _, rest in four:
                    step.free(v.max(v16[:, k, 8:16], rest))
                step.join()
                for k, _, rest in four[:3]:
                    step.free(v.max_index(i16[:, k, 8:16], v16[:, k, 8:16], rest))
                step.join()
                k, _, rest = four[3]
                v.max_index(i16[:, k, 8:16], v16[:, k, 8:16], rest).then_inc(sc_used, 1)
                v.wait_ge(sc_used, 4 * n + q + 1)

            def pairs(n, q):
                four = [(4 * q + i, cand[:, i, :]) for i in range(4)]
                for k, c in four:
                    step.free(v.tensor_tensor(by(c, TOPK), bc(v16[:, 2 * k, :], 2, TOPK), bc(v16[:, 2 * k + 1, :], 1, TOPK), ALU.add))
                step.join()
                for k, c in four:
                    step.free(v.max(best[:, k, 0:8], c))
                step.join()
                for k, c in four:
                    step.free(v.max_index(pos[:, k, 0:8], best[:, k, 0:8], c))
                step.join()
                for k, c in four:
                    step.free(v.match_replace(c, best[:, k, 0:8], c, NEG))
                step.join()
                for k, c in four:
                    step.free(v.max(best[:, k, 8:16], c))
                step.join()
                for k, c in four:
                    step.free(v.max_index(pos[:, k, 8:16], best[:, k, 8:16], c))
                step.join()

            def find_ids(n, q):
                b, heads, half = n % NB, slice(4 * q, 4 * q + 4), slice(q * SLOTS // 2, (q + 1) * SLOTS // 2)
                g3 = by(gates[:, b, half], TOPK)
                v.tensor_tensor(g3, best[:, heads, :], bc(best[:, heads, 0], 2, TOPK), ALU.subtract).then_inc(best_sub, 1)
                step(v.tensor_copy(i16f[:, 8 * q:8 * q + 8, :], i16[:, 8 * q:8 * q + 8, :]))
                pos_f = pos.rearrange("p n k -> p (n k)")[:, half]
                i4 = i16f[:, 8 * q:8 * q + 8, :].rearrange("p (n s) k -> p n s k", s=2)
                for s in range(2):
                    if s == 0:
                        step(v.tensor_single_scalar(posd[:, half], pos_f, 4, op=ALU.logical_shift_right))
                    else:
                        step(v.tensor_single_scalar(posd[:, half], pos_f, TOPK - 1, op=ALU.bitwise_and))
                    step(v.tensor_copy(posf[:, half], posd[:, half]))
                    step(v.tensor_tensor(hit.rearrange("p n k a -> p (n k) a"), bc(posf[:, half], 2, TOPK),
                                         bc(cst[:, C_IOTA:C_IOTA + TOPK], 1, SLOTS // 2), ALU.is_equal))
                    step(v.tensor_tensor(hit, hit, bc(i4[:, :, s, :], 2, TOPK), ALU.mult))
                    step(v.reduce_sum(idf[s][:, half], hit.rearrange("p n k a -> p (n k) a"), AX))
                step(v.scalar_tensor_tensor(out=idf[0][:, half], in0=idf[0][:, half], scalar=float(NK), in1=idf[1][:, half],
                                            op0=ALU.mult, op1=ALU.add))
                step(v.tensor_scalar(idf[0][:, half], idf[0][:, half], row[:, R_LC + 2:R_LC + 3], None, ALU.add))
                v.tensor_copy(ids[:, b, half], idf[0][:, half]).then_inc(ids_ready, 1)
                v.wait_ge(gate_exp, 2 * n + q + 1)
                step(v.reduce_sum(small[:, 400:404], g3, AX))
                step(v.reciprocal(small[:, 400:404], small[:, 400:404]))
                v.tensor_tensor(g3, g3, bc(small[:, 400:404], 2, TOPK), ALU.mult).then_inc(gates_ready, 1)
                v.wait_ge(gates_ready, 2 * n + q + 1)

            def take_dots(n, i):
                m, g, b = HALVES * n + i, i % 2, n % NB
                for j in range(RING_G):
                    s = g * RING_G + j
                    v.wait_ge(u_in[s], 16 * (m // 2 + 1))
                    v.wait_ge(dots_done, RING + RING_G * m + j)
                    if m >= 2 and j == 0:
                        v.wait_ge(gelu_done, m - 1)
                    v.tensor_tensor_reduce(junk[:, :], ring_u[:, s, :], h[:, b, :], 1.0, 0.0, ALU.mult, ALU.add,
                                           dots[:, s:s + 1]).then_inc(dots_done, 1)

            def weigh(n, i):
                m, g, b = HALVES * n + i, i % 2, n % NB
                ss = slice(g * RING_G, (g + 1) * RING_G)
                v.wait_ge(gelu_done, m + 1)
                if m >= 2:
                    v.wait_ge(diag_ready, RING_G * (m - 1))
                v.tensor_tensor(weights[:, ss], acts[:, ss], gates[:, b, i * RING_G:(i + 1) * RING_G], ALU.mult)\
                    .then_inc(weights_done, 1)

            def gathered(n, i):
                v.wait_ge(acc_ps, n + 1)
                v.tensor_copy(x[:, n % NB, :], ps[:, 0:2, :].rearrange("p c n -> p (c n)")).then_inc(x_done, 1)

            walk({"phases": phases, "tables": tables, "turned": turned, "norm": norm, "rows": rows, "project": project, "qk sums": qk_sums, "qk scale": qk_scale, "s5 in": s5_inputs, "keys": keys,
                  "s5 turn back": s5_turn_back, "s5 scan": s5_scan, "s5 turn on": s5_turn_on, "logits": logits,
                  "weights": head_weights, "heads": heads, "s5 out": s5_output, "s5 gate": s5_gate, "mixed": mix_end,
                  "out": out_rows, "score": score, "pairs": pairs, "ids": find_ids, "dots": take_dots,
                  "weigh": weigh, "gathered": gathered})

        @block.tensor
        def _(pe):
            def turn_rows(src, bank, done):
                for k in range(KC):
                    mm = pe.transpose(ps[:, bank + k // 4, (k % 4) * P:(k % 4 + 1) * P], src[:, k * P:(k + 1) * P], ident)
                mm.then_inc(done, 1)

            pe.wait_ge(once_in, 64)
            pe.sem_inc(v_used, RING)

            def rows(n, i):
                m, b = 2 * n + i, n % NB
                pe.wait_ge(h_ready, m + 1)
                if i == 0 and n:
                    pe.wait_ge(sc_used, 4 * n)
                if i == 1:
                    pe.wait_ge(mT_act, n + 1)
                turn_rows(h[:, b, :], 2 + 2 * i, rows_ps)

            def turned(_, n):
                pe.wait_ge(s5_bx, n + 1)
                if n:
                    pe.wait_ge(toep_copied, 2 * NH)
                for k in range(4):
                    mm = pe.transpose(ps[:, 1 - n, k * P:(k + 1) * P], bsc[n][:, 512 + k * P:512 + (k + 1) * P], ident)
                mm.then_inc(s5_bt_ps, 1)

            def lines_out(n, i):
                pe.wait_ge(toep_ready, 1)
                pe.wait_ge(s5_tabled, 1)
                for j in range(2 * NH):
                    if j >= 2:
                        pe.wait_ge(toep_copied, j - 1)
                    pe.matmul(ps[:, j % 2, :], tabx[:, j, :], line, start=True, stop=True).then_inc(toep_ps, 1)

            def project(n, k):
                if k == 0:
                    pe.wait_ge(rows_dve, 2 * n + 1)
                    pe.wait_ge(rows_act, 2 * n + 1)
                    if n:
                        pe.wait_ge(qT_ready, 4 * n)
                slot = k % WIN_SLOTS
                pe.wait_ge(win_in[slot], 16 * (n * (1 + (slot < KC - WIN_SLOTS)) + k // WIN_SLOTS + 1))
                for i in range(6):
                    c0, c1 = BANK_CUTS[i:i + 2]
                    mm = pe.matmul(ps[:, 2 + i, 0:c1 - c0], hT[:, k, :], win[:, slot, c0:c1], start=(k == 0), stop=(k == KC - 1))
                    if k == KC - 1:
                        mm.then_inc(z_ps, 1)
                if k < KC - 1:
                    mm.then_inc(chunk_used, 1)
                else:
                    pe.sem_inc(chunk_used, 1)

            def s5_inputs(n, i):
                pe.wait_ge(z_act, 3 * n + 3)
                pe.wait_ge(z_dve, 4 * n + 4)
                for j in range(2):
                    mm = pe.transpose(ps[:, 2, j * P:(j + 1) * P], zq[:, SU + j * P:SU + (j + 1) * P], ident)
                mm.then_inc(uT_ps, 1)

            def bu(n, i):
                pe.wait_ge(um_ready, n + 1)
                if n < NB:
                    pe.wait_ge(s5_tabled, 1)
                else:
                    pe.wait_ge(s5_load, 16 * (n // NB))
                for hf in range(2):
                    for r in range(2):
                        for j in range(4):
                            mm = pe.matmul(ps[:, 4 + 2 * hf + r, j * P:(j + 1) * P], bT[:, 2 * r + hf, :], um[:, 4 * hf + j, :],
                                           start=True, stop=True)
                mm.then_inc(bu_ps, 1)

            def keys(n, g):
                b = n % NB
                pe.wait_ge(qk_ready, 3 * n + g + 1)
                c = keys_bank(g)
                if g:
                    pe.wait_ge(keys_ready, 3 * n + g)
                    if g == 1:
                        pe.wait_ge(bu_used, n + 1)
                    else:
                        pe.wait_ge(o_used, 4 * n + 1)
                for i in range(2):
                    for s in range(b + 1):
                        c0 = KEYS + GW * g + i * P
                        t = i * (b + 1) + s
                        pe.transpose(ps[:, c, t * P:(t + 1) * P], zkv[:, s, c0:c0 + P], ident)
                for i in range(2):
                    mm = pe.transpose(ps[:, c + 1, i * P:(i + 1) * P], zq[:, GW * g + i * P:GW * g + (i + 1) * P], ident)
                mm.then_inc(keys_ps, 1)

            def logits(n, g):
                b = n % NB
                nk = P * (b + 1)
                pe.wait_ge(keys_ready, 3 * n + min(g, 2) + 1)
                if g == 0:
                    pe.wait_ge(f_ready, n + 1)
                else:
                    pe.wait_ge(bias_in, 16 * 2 * NH)
                    pe.wait_ge(p_exp, 16 * n + 4 * g)
                lg = ps[:, 2:4, :].rearrange("p c n -> p (c n)")
                for i in range(4):
                    dst = lg[:, i * nk:(i + 1) * nk]
                    own = lg[:, i * nk + b * P:(i + 1) * nk]
                    if g < 2:
                        q, k = qm[:, i * P:(i + 1) * P], kT[:, i // 2, 0:nk]
                    else:
                        q, k = qm[:, (g - 2) * 512 + i * P:(g - 2) * 512 + (i + 1) * P], kT[:, g - 2, 0:nk]
                    pe.matmul(dst, q, k, start=True, stop=False)
                    if g == 0:
                        for s in range(b + 1):
                            ls = small[:, 352 + s * NH + i:353 + s * NH + i]
                            nls = small[:, 360 + s * NH + i:361 + s * NH + i]
                            pe.matmul(dst, tri if s == b else ones, rep(ls, nk), start=False, stop=False)
                            pe.matmul(own if s == b else dst, rep(nls, P), tri if s == b else triones, start=False, stop=False)
                        mm = pe.matmul(own, ident, causal, start=False, stop=True)
                    else:
                        j = i if g == 1 else NH + 2 * (g - 2) + i // 2
                        mm = pe.matmul(dst, ident, bias[:, j, SEQ - nk:SEQ], start=False, stop=True)
                mm.then_inc(logit_ps, 1)

            def head_weights(n, g):
                b = n % NB
                pe.wait_ge(p_ready, 4 * n + g + 1)
                if g == 0:
                    pe.wait_ge(bu_used, n + 1)
                else:
                    pe.wait_ge(pT_ready, 4 * n + g)
                t = 0
                for i in range(4 if g < 2 else 2):
                    for s in range(b + 1):
                        src = pbuf[:, i if g < 2 else 2 * i, s * P:(s + 1) * P]
                        mm = pe.transpose(ps[:, 4 + t // 4, (t % 4) * P:(t % 4 + 1) * P], src, ident)
                        t += 1
                mm.then_inc(pT_ps, 1)

            def heads(n, g):
                b = n % NB
                pe.wait_ge(pT_ready, 4 * n + g + 1)
                pe.wait_ge(keys_ready, 3 * n + min(g + 2, 3))
                if g:
                    pe.wait_ge(o_used, 4 * n + g)
                v0 = VALS + (0, GW, 2 * GW, 2 * GW + P)[g]
                for i in range(4 if g < 2 else 2):
                    for s in range(b + 1):
                        mm = pe.matmul(ps[:, 7, 256 + i * HD:256 + (i + 1) * HD], pT[:, i * (b + 1) + s, :],
                                       zkv[:, s, v0 + i * HD:v0 + (i + 1) * HD], start=(s == 0), stop=(s == b))
                mm.then_inc(o_ps, 1)

            def s5_output(n, i):
                pe.wait_ge(s5_state, n + 1)
                for j in range(NJ):
                    y = ps[:, 6, j * 32:(j + 1) * 32]
                    pe.matmul(y, s5c[:, j, :], cR[:, 32 * j:32 * (j + 1)], start=True, stop=False)
                    mm = pe.matmul(y, s5b[:, j, :], cI[:, 32 * j:32 * (j + 1)], start=False, stop=True)
                mm.then_inc(y_ps, 1)

            def s5_gate(n, i):
                pe.wait_ge(g_ready, n + 1)
                for j in range(2):
                    mm = pe.transpose(ps[:, 6, j * P:(j + 1) * P], ybuf[:, j * P:(j + 1) * P], ident)
                mm.then_inc(gT_ps, 1)

            def mix_end(n, i):
                pe.wait_ge(gT_ready, n + 1)
                pe.wait_ge(glu_load, 16 * (n // NB + 1))
                for j in range(2):
                    mm = pe.matmul(ps[:, 6, 0:256], gT[:, j * P:(j + 1) * P], glu[:, j, :], start=(j == 0), stop=(j == 1))
                mm.then_inc(glu_ps, 1)

            def out_rows(n, c):
                if c == 0:
                    pe.wait_ge(mixed_ready, n + 1)
                    turn_rows(mixed[:, n % NB, :], 4, mT_ps)
                    pe.wait_ge(mT_dve, n + 1)
                    pe.wait_ge(mT_act, n + 1)
                    pe.wait_ge(wout_load, 16 * (n + 1))
                for k in range(KC):
                    mm = pe.matmul(ps[:, 2 + c, :], hT[:, k, :], wout_v[:, k, c * 512:(c + 1) * 512], start=(k == 0), stop=(k == KC - 1))
                mm.then_inc(wo_ps, 1)

            def query(n, q):
                if q == 0:
                    pe.wait_ge(rows_dve, 2 * n + 2)
                    pe.wait_ge(rows_act, 2 * n + 2)
                elif q >= 2:
                    pe.wait_ge(qT_ready, 4 * n + q - 1)
                pe.wait_ge(wq_in[q % 2], 16 * (2 * n + q // 2 + 1))
                for i in range(4):
                    for k in range(KC):
                        mm = pe.matmul(ps[:, 6 + q % 2, i * P:(i + 1) * P], wq_v[q % 2][:, k, i * P:(i + 1) * P], hT[:, k, :],
                                       start=(k == 0), stop=(k == KC - 1))
                mm.then_inc(qT_ps, 1)

            def score(n, q):
                if q == 0:
                    pe.wait_ge(keys_load, 16 * (n + 1))
                    pe.wait_ge(x_ready, n + 1)
                pe.wait_ge(qT_ready, 4 * n + q + 1)
                for i in range(4):
                    mm = pe.matmul(ps[:, 2 + q, i * NK:(i + 1) * NK], qts[:, 4 * q + i, :], kts[:, 4 * q + i, :], start=True, stop=True)
                mm.then_inc(sc_ps, 1)

            def add_rows(n, i):
                m, g, b = HALVES * n + i, i % 2, n % NB
                if i == 0:
                    if n:
                        pe.wait_ge(x_done, n)
                    else:
                        pe.wait_ge(s5_tabled, DEPTH)
                        pe.wait_ge(zero_set, 1)
                    for c in range(2):
                        pe.matmul(ps[:, c, :], zero[:, :], x[:, b, c * 512:(c + 1) * 512], start=True, stop=False,
                                  skip_group_check=True)
                for j in range(RING_G):
                    s = g * RING_G + j
                    pe.wait_ge(v_in[s], 16 * (m // 2 + 1))
                    pe.wait_ge(diag_ready, RING_G * m + j + 1)
                    for c in range(2):
                        mm = pe.matmul(ps[:, c, :], diag[:, s, :], ring_v[:, s, c * 512:(c + 1) * 512], start=False, stop=False,
                                       skip_group_check=True)
                    mm.then_inc(v_used, 1)
                if i == HALVES - 1:
                    for c in range(2):
                        mm = pe.matmul(ps[:, c, :], ident, x[:, b, c * 512:(c + 1) * 512], start=False, stop=True,
                                       skip_group_check=True)
                    mm.then_inc(acc_ps, 1)

            walk({"lines": lines_out, "turned": turned, "rows": rows, "project": project, "s5 in": s5_inputs, "bu": bu, "keys": keys, "logits": logits,
                  "weights": head_weights, "heads": heads, "s5 out": s5_output, "s5 gate": s5_gate, "mixed": mix_end,
                  "out": out_rows, "query": query, "score": score, "rows of v": add_rows})

        @block.gpsimd
        def _(gp):
            gp.wait_ge(toep_out, 16)
            gp.wait_ge(s5_out, 16 * (DEPTH - 1))
            for n in range(PASSES):
                b = n % NB
                for q in range(2):
                    gp.wait_ge(ids_ready, 2 * n + q + 1)
                    with gp.Fori((2 * n + q) * ITERS // 2, (2 * n + q + 1) * ITERS // 2) as turn:
                        for g in range(2):
                            ss = range(g * RING_G, (g + 1) * RING_G)
                            now = bass.ds(turn * RING + (g * RING_G - n * SLOTS), RING_G)
                            gp.wait_ge(dots_done, turn * RING + (g + 1) * RING_G)
                            gp.wait_ge(ids_ready, 2 * n + q + 1)
                            gp.tensor_copy(ring_ids[:, 0, g * RING_G:(g + 1) * RING_G], ids[:, b, now]).then_inc(u_staged, RING_G)
                            gp.wait_ge(ids_ready, 2 * n + q + 1)
                            gp.wait_ge(u_staged, turn * RING + (g + 1) * RING_G)
                            for s in ss:
                                gp.indirect_dma_start(ring_u[:, s, :], None, table_u,
                                                      bass.IndirectOffsetOnAxis(ap=ring_ids[:, 0, s:s + 1], axis=0)).then_inc(u_in[s], 16)
                            gp.wait_ge(v_used, turn * RING + (g + 1) * RING_G)
                            gp.wait_ge(ids_ready, 2 * n + q + 1)
                            gp.tensor_copy(ring_ids[:, 1, g * RING_G:(g + 1) * RING_G], ids[:, b, now]).then_inc(v_staged, RING_G)
                            gp.wait_ge(ids_ready, 2 * n + q + 1)
                            gp.wait_ge(v_staged, turn * RING + (g + 1) * RING_G)
                            for s in ss:
                                gp.indirect_dma_start(ring_v[:, s, :], None, table_v,
                                                      bass.IndirectOffsetOnAxis(ap=ring_ids[:, 1, s:s + 1], axis=0)).then_inc(v_in[s], 16)


def shape_constants():
    c = np.zeros((P, C_W), np.float32)
    p = np.arange(P)
    c[:, C_ID:C_ID + P] = np.eye(P)
    c[:, C_TRI:C_TRI + P] = p[:, None] <= p[None, :]
    c[:, C_ONE:C_ONE + P] = 1.0
    c[:, C_MASK:C_MASK + P] = np.where(p[None, :] <= p[:, None], 0.0, NEG)
    c[:, C_TAU:C_TAU + P] = p + 1
    for i in range(2):
        c[:, C_HM2 + i] = p // 64 == i
    for i in range(4):
        c[:, C_HM4 + i] = p // 32 == i
    c[:, C_IOTA:C_IOTA + TOPK] = np.arange(TOPK)
    return c


def bucket_constants():
    dist = 255 - np.arange(512)
    n = np.maximum(dist, 0)
    nf = np.maximum(n, MAX_EXACT).astype(np.float32)
    large = MAX_EXACT + (np.log(nf / np.float32(MAX_EXACT)) / math.log(MAX_DIST / MAX_EXACT)
                         * (BUCKETS - MAX_EXACT)).astype(np.int32)
    bucket = np.where(n < MAX_EXACT, n, np.minimum(large, BUCKETS - 1))
    c = np.zeros((BUCKETS + 2, 512), np.float32)
    c[bucket, np.arange(512)] = 1.0
    count = (dist <= 128).astype(int) + (dist % 4 == 0) + (dist % 16 == 0)
    seen = (dist >= 0) & (count > 0)
    c[BUCKETS] = np.where(seen, np.log(np.maximum(count, 1)), NEG)
    c[BUCKETS + 1] = np.where(dist >= 0, 0.0, NEG)
    return c


def mask_rows():
    c = np.zeros((2, 2 * NH), np.float32)
    c[0, :NH] = c[1, NH:] = 1.0
    return c


def layer_constants():
    c = np.zeros((DEPTH, 4), np.float32)
    for n in range(DEPTH):
        lam = 0.8 - 0.6 * math.exp(-0.3 * n)
        c[n] = lam, 1.0 - lam, n * NE, 0.0
    return c


def kernel(x, w_in, b_forget, w_out, norm_mix, norm_ffn, fox_q_norm, fox_k_norm, dil_q_norm, dil_k_norm,
           diff_q_norm, diff_k_norm, diff_lambda, diff_out_norm, rel_bias, s5_a_re, s5_a_im, s5_log_dt,
           s5_b_re, s5_b_im, s5_c_re, s5_c_im, s5_d, s5_glu_w, s5_glu_b, peer_wq, peer_keys, peer_u, peer_v):
    import concourse.bacc as bacc
    from concourse.bass_utils import run_bass_kernel_spmd

    L = DEPTH
    rows = np.concatenate([np.asarray(t).reshape(L, -1) for t in (
        fox_q_norm, fox_k_norm, dil_q_norm, dil_k_norm, diff_q_norm, diff_k_norm, diff_out_norm, b_forget,
        diff_lambda, layer_constants(), s5_d, s5_glu_b)], axis=1)

    def by_state(t):
        t = np.asarray(t)
        t = t.reshape((L, NJ, 2, S5_N) + t.shape[3:])
        t = np.moveaxis(t, 1, 3)
        return t.reshape((L, P, -1))

    def c_blocks(t):
        t = np.asarray(t)
        o = np.zeros((L, 2, S5_N, NJ, 2, S5_C), t.dtype)
        for g in range(2):
            o[:, g, :, :, g, :] = t.reshape(L, NJ, 2, S5_C, S5_N)[:, :, g].transpose(0, 3, 1, 2)
        return o.reshape(L, P, GW)

    parts = np.split(np.asarray(w_in), np.cumsum(IN_SPLIT)[:-1], axis=2)
    w_in = np.concatenate([parts[i] for i in IN_ORDER], axis=2)
    dt = np.repeat(np.asarray(s5_log_dt)[:, :, None], S5_N, axis=2)
    s5 = np.concatenate([by_state(s5_a_re), by_state(s5_a_im), by_state(dt), by_state(s5_b_re), by_state(s5_b_im),
                         c_blocks(s5_c_re), c_blocks(s5_c_im)], axis=2)
    keys = np.asarray(peer_keys).reshape(L, HP, NK, P).transpose(0, 3, 1, 2)
    arrays = {
        "x_in": np.asarray(x).reshape(SEQ, D), "w_in": w_in, "w_out": w_out, "row_in": rows,
        "gain_mix": norm_mix, "gain_ffn": norm_ffn, "s5_in": s5, "glu_w": s5_glu_w, "peer_wq": peer_wq,
        "keys_t": keys, "table_u": np.asarray(peer_u).reshape(L * NE, D), "table_v": np.asarray(peer_v).reshape(L * NE, D),
        "rel_bias": np.concatenate([np.asarray(rel_bias), mask_rows()]), "const_in": shape_constants(), "bucket_in": bucket_constants(),
    }
    arrays = {k: np.ascontiguousarray(v) for k, v in arrays.items()}
    nc = bacc.Bacc("TRN2", target_bir_lowering=False, num_devices=1)
    args = {k: nc.dram_tensor(k, v.shape, mybir.dt.from_np(v.dtype), kind="ExternalInput").ap() for k, v in arrays.items()}
    out = nc.dram_tensor("out", (SEQ, D), F32, kind="ExternalOutput").ap()
    trunk(nc, **args, out=out)
    r = run_bass_kernel_spmd(nc, [arrays], core_ids=[0])
    return r.results[0]["out"].reshape(1, SEQ, D)
```
